# Optimizing a Trainium2 kernel written in Bass

```python
import math
import jax, jax.numpy as jnp
from jax import lax
import numpy as np

D_MODEL = 1024
BATCH = 1
SEQ = 256
DEPTH = 1

D_MIX = D_MODEL
ATTN_WIDTH = D_MIX // 2
CONV_WIDTH = D_MIX - ATTN_WIDTH
N_HEADS = 8
HEAD_DIM = ATTN_WIDTH // N_HEADS
CONV_KERNEL = 31
MOBA_BLOCK = 256
MOBA_TOPK = 3
Q_CHUNK = 64
ROPE_THETA = 10000.0
D_FF = -(-8 * D_MODEL // (3 * 256)) * 256
EPS = 1e-6
D_IN = 3 * ATTN_WIDTH + 2 * CONV_WIDTH


def rms_norm(x, g):
    xf = x.astype(jnp.float32)
    y = xf * lax.rsqrt(jnp.mean(xf * xf, axis=-1, keepdims=True) + EPS)
    return (y * g.astype(jnp.float32)).astype(x.dtype)

def layer_norm(x, g, b):
    xf = x.astype(jnp.float32)
    mu = jnp.mean(xf, axis=-1, keepdims=True)
    var = jnp.mean(jnp.square(xf - mu), axis=-1, keepdims=True)
    y = (xf - mu) * lax.rsqrt(var + EPS)
    return (y * g.astype(jnp.float32) + b.astype(jnp.float32)).astype(x.dtype)

def rope_tables(seq_len):
    pos = jnp.arange(seq_len, dtype=jnp.float32)
    inv_freq = ROPE_THETA ** (-jnp.arange(0, HEAD_DIM, 2, dtype=jnp.float32) / HEAD_DIM)
    ang = pos[:, None] * inv_freq[None, :]
    ang = jnp.concatenate([ang, ang], axis=-1)
    return jnp.cos(ang)[:, None, :], jnp.sin(ang)[:, None, :]

def apply_rope(x, cos, sin):
    xf = x.astype(jnp.float32)
    x1, x2 = jnp.split(xf, 2, axis=-1)
    rot = jnp.concatenate([-x2, x1], axis=-1)
    return (xf * cos + rot * sin).astype(x.dtype)

def moba_attention(q, k, v):
    B, H, S, Dh = q.shape
    n_blocks = -(-S // MOBA_BLOCK)
    pad = n_blocks * MOBA_BLOCK - S
    kp = jnp.pad(k, ((0, 0), (0, 0), (0, pad), (0, 0)))
    vp = jnp.pad(v, ((0, 0), (0, 0), (0, pad), (0, 0)))
    kb = kp.reshape(B, H, n_blocks, MOBA_BLOCK, Dh)
    vb = vp.reshape(B, H, n_blocks, MOBA_BLOCK, Dh)
    k_mean = jnp.mean(kb.astype(jnp.float32), axis=3)
    topk = min(MOBA_TOPK, n_blocks)
    scale = HEAD_DIM ** -0.5
    b_idx = jnp.arange(B)[:, None, None, None]
    h_idx = jnp.arange(H)[None, :, None, None]
    key_off = jnp.arange(MOBA_BLOCK)
    block_ids = jnp.arange(n_blocks)
    n_chunks = S // Q_CHUNK

    def chunk_fn(c):
        start = c * Q_CHUNK
        qc = lax.dynamic_slice_in_dim(q, start, Q_CHUNK, axis=2)
        q_pos = start + jnp.arange(Q_CHUNK)
        own = start // MOBA_BLOCK
        gate = jnp.einsum('bhqd,bhnd->bhqn', qc.astype(jnp.float32), k_mean)
        gate = jnp.where((block_ids < own)[None, None, None, :], gate, -jnp.inf)
        _, top_idx = lax.top_k(gate, topk)
        sel_valid = top_idx < own
        k_sel = kb[b_idx, h_idx, top_idx]
        v_sel = vb[b_idx, h_idx, top_idx]
        s_sel = jnp.einsum('bhqd,bhqnkd->bhqnk', qc, k_sel).astype(jnp.float32) * scale
        s_sel = jnp.where(sel_valid[..., None], s_sel, -jnp.inf)
        s_sel = s_sel.reshape(B, H, Q_CHUNK, topk * MOBA_BLOCK)
        k_own = lax.dynamic_slice_in_dim(kp, own * MOBA_BLOCK, MOBA_BLOCK, axis=2)
        v_own = lax.dynamic_slice_in_dim(vp, own * MOBA_BLOCK, MOBA_BLOCK, axis=2)
        s_own = jnp.einsum('bhqd,bhkd->bhqk', qc, k_own).astype(jnp.float32) * scale
        own_pos = own * MOBA_BLOCK + key_off
        s_own = jnp.where((own_pos[None, :] <= q_pos[:, None])[None, None], s_own, -jnp.inf)
        p = jax.nn.softmax(jnp.concatenate([s_own, s_sel], axis=-1), axis=-1)
        p_own = p[..., :MOBA_BLOCK].astype(v.dtype)
        p_sel = p[..., MOBA_BLOCK:].reshape(B, H, Q_CHUNK, topk, MOBA_BLOCK).astype(v.dtype)
        out = (jnp.einsum('bhqk,bhkd->bhqd', p_own, v_own)
               + jnp.einsum('bhqnk,bhqnkd->bhqd', p_sel, v_sel))
        return out

    outs = lax.map(chunk_fn, jnp.arange(n_chunks))
    return outs.transpose(1, 2, 0, 3, 4).reshape(B, H, S, Dh)

def conformer_conv(u, glu_b, dw_w, dw_b, ln_g, ln_b):
    u = u + glu_b.astype(u.dtype)
    a, g = jnp.split(u, 2, axis=-1)
    h = a * jax.nn.sigmoid(g)
    h = jnp.pad(h, ((0, 0), (CONV_KERNEL - 1, 0), (0, 0)))
    h = lax.conv_general_dilated(
        h, dw_w[:, None, :].astype(h.dtype), window_strides=(1,), padding='VALID',
        dimension_numbers=('NWC', 'WIO', 'NWC'), feature_group_count=CONV_WIDTH)
    h = h + dw_b.astype(h.dtype)
    h = layer_norm(h, ln_g, ln_b)
    return jax.nn.silu(h)

def first_inputs(seed: int = 0) -> dict:
    key = jax.random.key(seed)
    ks = jax.random.split(key, 16)
    f32 = jnp.float32
    L = DEPTH

    def nrm(k, shape, scale):
        return jax.random.normal(k, shape, f32) * scale

    return {
        "x": jax.random.normal(ks[0], (BATCH, SEQ, D_MODEL), f32),
        "norm1_g": 1.0 + nrm(ks[1], (L, D_MODEL), 0.02),
        "w_in": nrm(ks[2], (L, D_MODEL, D_IN), D_MODEL ** -0.5),
        "glu_b": nrm(ks[3], (L, 2 * CONV_WIDTH), 0.02),
        "q_norm_g": 1.0 + nrm(ks[4], (L, HEAD_DIM), 0.02),
        "k_norm_g": 1.0 + nrm(ks[5], (L, HEAD_DIM), 0.02),
        "dw_w": nrm(ks[6], (L, CONV_KERNEL, CONV_WIDTH), CONV_KERNEL ** -0.5),
        "dw_b": nrm(ks[7], (L, CONV_WIDTH), 0.02),
        "conv_ln_g": 1.0 + nrm(ks[8], (L, CONV_WIDTH), 0.02),
        "conv_ln_b": nrm(ks[9], (L, CONV_WIDTH), 0.02),
        "w_out": nrm(ks[10], (L, D_MIX, D_MODEL), D_MIX ** -0.5),
        "norm2_g": 1.0 + nrm(ks[11], (L, D_MODEL), 0.02),
        "w_gate": nrm(ks[12], (L, D_MODEL, D_FF), D_MODEL ** -0.5),
        "w_up": nrm(ks[13], (L, D_MODEL, D_FF), D_MODEL ** -0.5),
        "w_down": nrm(ks[14], (L, D_FF, D_MODEL), D_FF ** -0.5),
    }

def first_block(x, norm1_g, w_in, glu_b, q_norm_g, k_norm_g, dw_w, dw_b, conv_ln_g,
              conv_ln_b, w_out, norm2_g, w_gate, w_up, w_down):
    B, S, _ = x.shape
    cos, sin = rope_tables(S)
    for l in range(DEPTH):
        h = rms_norm(x, norm1_g[l])
        proj = h @ w_in[l]
        q, k, v, u = jnp.split(proj, [ATTN_WIDTH, 2 * ATTN_WIDTH, 3 * ATTN_WIDTH], axis=-1)
        q = q.reshape(B, S, N_HEADS, HEAD_DIM)
        k = k.reshape(B, S, N_HEADS, HEAD_DIM)
        v = v.reshape(B, S, N_HEADS, HEAD_DIM)
        q = apply_rope(rms_norm(q, q_norm_g[l]), cos, sin)
        k = apply_rope(rms_norm(k, k_norm_g[l]), cos, sin)
        attn = moba_attention(q.transpose(0, 2, 1, 3), k.transpose(0, 2, 1, 3),
                              v.transpose(0, 2, 1, 3))
        attn = attn.transpose(0, 2, 1, 3).reshape(B, S, ATTN_WIDTH)
        conv = conformer_conv(u, glu_b[l], dw_w[l], dw_b[l], conv_ln_g[l], conv_ln_b[l])
        x = x + jnp.concatenate([attn, conv], axis=-1) @ w_out[l]
        h = rms_norm(x, norm2_g[l])
        x = x + (jax.nn.silu(h @ w_gate[l]) * (h @ w_up[l])) @ w_down[l]
    return x


DEPTH_2 = 2

CHUNK = 64
HEAD_DIM_2 = 64
D_FF_2 = 2816
Q_BLOCK = 128
DSA_Q_BLOCK = 32
A_HEADS = D_MODEL // (4 * HEAD_DIM_2)
A_VDIM = 2 * HEAD_DIM_2
B_HEADS = D_MODEL // (2 * HEAD_DIM_2)
IDX_HEADS = 8
IDX_DIM = 32
TOPK_MAX = 256
C_HEADS = D_MODEL // HEAD_DIM_2
C_LEFT_CHUNKS = 8
MAX_REL = 256
REL_TABLE = MAX_REL + CHUNK

MIX_WIDTH = A_HEADS * A_VDIM + B_HEADS * HEAD_DIM_2
EVEN_SIZES = (2 * A_HEADS * HEAD_DIM_2, 2 * A_HEADS * HEAD_DIM_2, A_HEADS * A_VDIM,
              B_HEADS * HEAD_DIM_2, B_HEADS * HEAD_DIM_2, B_HEADS * HEAD_DIM_2,
              IDX_HEADS * IDX_DIM, IDX_DIM, IDX_HEADS)
EVEN_PROJ = sum(EVEN_SIZES)
EVEN_SPLITS = [sum(EVEN_SIZES[:i + 1]) for i in range(len(EVEN_SIZES) - 1)]


def rmsnorm(x, g):
    xf = x.astype(jnp.float32)
    y = xf * lax.rsqrt(jnp.mean(xf * xf, axis=-1, keepdims=True) + EPS)
    return (y * g.astype(jnp.float32)).astype(x.dtype)

def rope_tables_2(seq, dim):
    inv = ROPE_THETA ** (-jnp.arange(0, dim, 2, dtype=jnp.float32) / dim)
    ang = jnp.arange(seq, dtype=jnp.float32)[:, None] * inv[None, :]
    return jnp.cos(ang), jnp.sin(ang)

def apply_rope_2(x, cos, sin):
    xf = x.astype(jnp.float32)
    x1, x2 = jnp.split(xf, 2, axis=-1)
    c = cos[:, None, :]
    s = sin[:, None, :]
    return jnp.concatenate([x1 * c - x2 * s, x2 * c + x1 * s], axis=-1).astype(x.dtype)

def masked_softmax(s, mask):
    return jax.nn.softmax(jnp.where(mask, s, -jnp.inf), axis=-1)

def swiglu(h, wg, wu, wd):
    return (jax.nn.silu(h @ wg) * (h @ wu)) @ wd

def diff_attention(q, k, v, lam, subln, lambda_init):
    B_, S_ = q.shape[0], q.shape[1]
    nb = S_ // Q_BLOCK
    qb = q.reshape(B_, nb, Q_BLOCK, A_HEADS, 2, HEAD_DIM_2).swapaxes(0, 1)
    kf = k.astype(jnp.float32)
    vf = v.astype(jnp.float32)
    kchunk = jnp.arange(S_) // CHUNK
    scale = HEAD_DIM_2 ** -0.5

    def one_block(args):
        bi, qblk = args
        qpos = bi * Q_BLOCK + jnp.arange(Q_BLOCK)
        mask = kchunk[None, :] <= (qpos // CHUNK)[:, None]
        s = jnp.einsum('bqhcd,bkhcd->bhcqk', qblk.astype(jnp.float32), kf) * scale
        p = masked_softmax(s, mask)
        w = p[:, :, 0] - lam * p[:, :, 1]
        return jnp.einsum('bhqk,bkhe->bqhe', w, vf)

    o = lax.map(one_block, (jnp.arange(nb), qb))
    o = o.swapaxes(0, 1).reshape(B_, S_, A_HEADS, A_VDIM)
    o = rmsnorm(o, subln) * (1.0 - lambda_init)
    return o.reshape(B_, S_, A_HEADS * A_VDIM).astype(v.dtype)

def dsa_attention(q, k, v, qi, ki, wi, topk):
    B_, S_ = q.shape[0], q.shape[1]
    nb = S_ // DSA_Q_BLOCK
    qb = q.reshape(B_, nb, DSA_Q_BLOCK, B_HEADS, HEAD_DIM_2).swapaxes(0, 1)
    qib = qi.reshape(B_, nb, DSA_Q_BLOCK, IDX_HEADS, IDX_DIM).swapaxes(0, 1)
    wib = wi.reshape(B_, nb, DSA_Q_BLOCK, IDX_HEADS).swapaxes(0, 1)
    kf = k.astype(jnp.float32)
    vf = v.astype(jnp.float32)
    kif = ki.astype(jnp.float32)
    kchunk = jnp.arange(S_) // CHUNK
    scale = HEAD_DIM_2 ** -0.5
    gather = jax.vmap(lambda kk, ii: kk[ii])

    def one_block(args):
        bi, qblk, qiblk, wiblk = args
        qpos = bi * DSA_Q_BLOCK + jnp.arange(DSA_Q_BLOCK)
        qchunk = qpos // CHUNK
        rel = jax.nn.relu(jnp.einsum('bqhd,bkd->bqhk', qiblk.astype(jnp.float32), kif))
        score = jnp.einsum('bqhk,bqh->bqk', rel, wiblk.astype(jnp.float32))
        mask = kchunk[None, :] <= qchunk[:, None]
        score = jnp.where(mask[None], score, -jnp.inf)
        _, idx = lax.top_k(score, topk)
        valid = (idx // CHUNK) <= qchunk[None, :, None]
        kg = gather(kf, idx)
        vg = gather(vf, idx)
        s = jnp.einsum('bqhd,bqkhd->bhqk', qblk.astype(jnp.float32), kg) * scale
        p = masked_softmax(s, valid[:, None])
        return jnp.einsum('bhqk,bqkhd->bqhd', p, vg)

    o = lax.map(one_block, (jnp.arange(nb), qb, qib, wib))
    return o.swapaxes(0, 1).reshape(B_, S_, B_HEADS * HEAD_DIM_2).astype(v.dtype)

def chunk_band_attention(q, k, v, rel_bias):
    B_, S_ = q.shape[0], q.shape[1]
    nc = S_ // CHUNK
    left = C_LEFT_CHUNKS * CHUNK
    band = left + CHUNK
    kp = jnp.pad(k.astype(jnp.float32), ((0, 0), (left, 0), (0, 0), (0, 0)))
    vp = jnp.pad(v.astype(jnp.float32), ((0, 0), (left, 0), (0, 0), (0, 0)))
    dist = left + jnp.arange(CHUNK)[:, None] - jnp.arange(band)[None, :]
    bias_idx = jnp.clip(dist, -(CHUNK - 1), MAX_REL) + (CHUNK - 1)
    bias = rel_bias.astype(jnp.float32)[:, bias_idx]
    qc = q.reshape(B_, nc, CHUNK, C_HEADS, HEAD_DIM_2).swapaxes(0, 1)
    scale = HEAD_DIM_2 ** -0.5

    def one_chunk(args):
        ci, qblk = args
        kb = lax.dynamic_slice_in_dim(kp, ci * CHUNK, band, axis=1)
        vb = lax.dynamic_slice_in_dim(vp, ci * CHUNK, band, axis=1)
        valid = (ci * CHUNK - left + jnp.arange(band)) >= 0
        s = jnp.einsum('bqhd,bkhd->bhqk', qblk.astype(jnp.float32), kb) * scale + bias[None]
        p = masked_softmax(s, valid[None, None, None, :])
        return jnp.einsum('bhqk,bkhd->bqhd', p, vb)

    o = lax.map(one_chunk, (jnp.arange(nc), qc))
    return o.swapaxes(0, 1).reshape(B_, S_, C_HEADS * HEAD_DIM_2).astype(v.dtype)

def even_mixer(h, w_in, w_out, lam_p, subln, rope64, rope32, lambda_init, topk):
    B_, S_ = h.shape[0], h.shape[1]
    cos64, sin64 = rope64
    cos32, sin32 = rope32
    a_q, a_k, a_v, b_q, b_k, b_v, i_q, i_k, i_w = jnp.split(h @ w_in, EVEN_SPLITS, axis=-1)
    a_q = apply_rope_2(a_q.reshape(B_, S_, 2 * A_HEADS, HEAD_DIM_2), cos64, sin64).reshape(B_, S_, A_HEADS, 2, HEAD_DIM_2)
    a_k = apply_rope_2(a_k.reshape(B_, S_, 2 * A_HEADS, HEAD_DIM_2), cos64, sin64).reshape(B_, S_, A_HEADS, 2, HEAD_DIM_2)
    a_v = a_v.reshape(B_, S_, A_HEADS, A_VDIM)
    lp = lam_p.astype(jnp.float32)
    lam = jnp.exp(jnp.sum(lp[0] * lp[1])) - jnp.exp(jnp.sum(lp[2] * lp[3])) + lambda_init
    o_a = diff_attention(a_q, a_k, a_v, lam, subln, lambda_init)
    b_q = apply_rope_2(b_q.reshape(B_, S_, B_HEADS, HEAD_DIM_2), cos64, sin64)
    b_k = apply_rope_2(b_k.reshape(B_, S_, B_HEADS, HEAD_DIM_2), cos64, sin64)
    b_v = b_v.reshape(B_, S_, B_HEADS, HEAD_DIM_2)
    i_q = apply_rope_2(i_q.reshape(B_, S_, IDX_HEADS, IDX_DIM), cos32, sin32)
    i_k = apply_rope_2(i_k.reshape(B_, S_, 1, IDX_DIM), cos32, sin32)[:, :, 0]
    i_w = i_w * (IDX_HEADS ** -0.5 * IDX_DIM ** -0.5)
    o_b = dsa_attention(b_q, b_k, b_v, i_q, i_k, i_w, topk)
    return jnp.concatenate([o_a, o_b], axis=-1) @ w_out

def odd_mixer(h, w_in, w_out, rel_bias):
    B_, S_ = h.shape[0], h.shape[1]
    q, k, v = jnp.split(h @ w_in, 3, axis=-1)
    q = q.reshape(B_, S_, C_HEADS, HEAD_DIM_2)
    k = k.reshape(B_, S_, C_HEADS, HEAD_DIM_2)
    v = v.reshape(B_, S_, C_HEADS, HEAD_DIM_2)
    return chunk_band_attention(q, k, v, rel_bias) @ w_out

def second_inputs(seed: int = 0) -> dict:
    key = jax.random.key(seed)
    ks = jax.random.split(key, 12)
    n_even = (DEPTH_2 + 1) // 2
    n_odd = DEPTH_2 // 2
    nrm = jax.random.normal
    f32 = jnp.float32
    return {
        "x": nrm(ks[0], (BATCH, SEQ, D_MODEL), f32),
        "norm_g": 1.0 + 0.01 * nrm(ks[1], (DEPTH_2, 6, D_MODEL), f32),
        "ffn_wg": nrm(ks[2], (DEPTH_2, 2, D_MODEL, D_FF_2), f32) * D_MODEL ** -0.5,
        "ffn_wu": nrm(ks[3], (DEPTH_2, 2, D_MODEL, D_FF_2), f32) * D_MODEL ** -0.5,
        "ffn_wd": nrm(ks[4], (DEPTH_2, 2, D_FF_2, D_MODEL), f32) * D_FF_2 ** -0.5,
        "even_w_in": nrm(ks[5], (n_even, D_MODEL, EVEN_PROJ), f32) * D_MODEL ** -0.5,
        "even_w_out": nrm(ks[6], (n_even, MIX_WIDTH, D_MODEL), f32) * MIX_WIDTH ** -0.5,
        "even_lambda": 0.1 * nrm(ks[7], (n_even, 4, HEAD_DIM_2), f32),
        "even_subln": 1.0 + 0.01 * nrm(ks[8], (n_even, A_VDIM), f32),
        "odd_w_in": nrm(ks[9], (n_odd, D_MODEL, 3 * D_MODEL), f32) * D_MODEL ** -0.5,
        "odd_w_out": nrm(ks[10], (n_odd, D_MODEL, D_MODEL), f32) * D_MODEL ** -0.5,
        "odd_rel_bias": 0.1 * nrm(ks[11], (n_odd, C_HEADS, REL_TABLE), f32),
    }

def second_block(x, norm_g, ffn_wg, ffn_wu, ffn_wd, even_w_in, even_w_out, even_lambda, even_subln,
              odd_w_in, odd_w_out, odd_rel_bias):
    S_ = x.shape[1]
    topk = min(TOPK_MAX, S_ // 4)
    rope64 = rope_tables_2(S_, HEAD_DIM_2)
    rope32 = rope_tables_2(S_, IDX_DIM)
    for l in range(DEPTH_2):
        g = norm_g[l]
        h = rmsnorm(x, g[0])
        x = x + 0.5 * rmsnorm(swiglu(h, ffn_wg[l, 0], ffn_wu[l, 0], ffn_wd[l, 0]), g[1])
        h = rmsnorm(x, g[2])
        if l % 2 == 0:
            e = l // 2
            lambda_init = 0.8 - 0.6 * math.exp(-0.3 * l)
            m = even_mixer(h, even_w_in[e], even_w_out[e], even_lambda[e], even_subln[e],
                           rope64, rope32, lambda_init, topk)
        else:
            o = l // 2
            m = odd_mixer(h, odd_w_in[o], odd_w_out[o], odd_rel_bias[o])
        x = x + rmsnorm(m.astype(x.dtype), g[3])
        h = rmsnorm(x, g[4])
        x = x + 0.5 * rmsnorm(swiglu(h, ffn_wg[l, 1], ffn_wu[l, 1], ffn_wd[l, 1]), g[5])
    return x


def setup_inputs(seed=0):
    out = dict(first_inputs(seed))
    for name, value in second_inputs(seed + 1).items():
        if name != "x":
            out[name + "_2"] = value
    return out


def reference(
    x, norm1_g, w_in, glu_b, q_norm_g, k_norm_g, dw_w, dw_b, conv_ln_g, conv_ln_b, w_out,
    norm2_g, w_gate, w_up, w_down, norm_g_2, ffn_wg_2, ffn_wu_2, ffn_wd_2, even_w_in_2,
    even_w_out_2, even_lambda_2, even_subln_2, odd_w_in_2, odd_w_out_2, odd_rel_bias_2,
):
    x = first_block(
        x, norm1_g, w_in, glu_b, q_norm_g, k_norm_g, dw_w, dw_b, conv_ln_g, conv_ln_b, w_out,
        norm2_g, w_gate, w_up, w_down,
    )
    return second_block(
        x, norm_g_2, ffn_wg_2, ffn_wu_2, ffn_wd_2, even_w_in_2, even_w_out_2, even_lambda_2,
        even_subln_2, odd_w_in_2, odd_w_out_2, odd_rel_bias_2,
    )


_drawn_inputs = setup_inputs


def setup_inputs(seed=0):
    import zlib

    import numpy as np

    out = dict(_drawn_inputs(seed))
    spreads = {}
    factors = {'q_norm_g': 7.378,
     'k_norm_g': 6.8,
     'even_subln_2': 64.0,
     'odd_rel_bias_2': 4.661,
     'glu_b': 2.872,
     'conv_ln_g': 3.061,
     'norm2_g': 3.788,
     'norm_g_2': 3.266}
    for name, (base, spread) in spreads.items():
        noise = np.random.default_rng([zlib.crc32(name.encode()), seed]).standard_normal(out[name].shape)
        drawn = base * np.exp(spread * noise) if base else spread * noise
        out[name] = __import__('jax').numpy.asarray(drawn.astype(out[name].dtype))
    for name, factor in factors.items():
        out[name] = (out[name] * factor).astype(out[name].dtype)
    return out
```

```python
import math
from contextlib import ExitStack

import numpy as np
import concourse.bass as bass
from concourse import mybir

F32 = mybir.dt.float32
F32R = mybir.dt.float32r
ALU = mybir.AluOpType
ACT = mybir.ActivationFunctionType
AX = mybir.AxisListType

P = 128
S = 256
T = S // P
D = 1024
KT = D // P
FF = 2816
UC = 256
UNIT = KT * UC
CHUNKS = FF // UC
HW = 512
RAWS = 3
SLOTS = 6
LEAD = SLOTS - 1
TAPS = 31
EPS = 1e-6
NEG = -1e30
TAKEN = -3e38
TOPK = 64
LAMBDA_INIT = 0.8 - 0.6 * math.exp(-0.3 * 0)
WS = 9984


def host_tables():
    def rope(dim):
        inv = (np.float32(10000.0) ** (-np.arange(0, dim, 2, dtype=np.float32) / np.float32(dim))).astype(np.float32)
        ang = np.arange(S, dtype=np.float32)[:, None] * inv[None, :]
        c, s = np.cos(ang).astype(np.float32), np.sin(ang).astype(np.float32)
        return np.concatenate([c, c, -s, s], axis=1)
    r64, r32 = rope(64), rope(32)
    q, k = np.arange(P)[:, None], np.arange(P)[None, :]
    zero = np.zeros((P, P), np.float32)
    causal = np.where(k <= q, 0.0, NEG).astype(np.float32)
    chunky = np.where(k // 64 <= q // 64, 0.0, NEG).astype(np.float32)
    return {
        "rope_tab": np.concatenate([r64, r32], axis=1).astype(np.float32),
        "mask_tab": np.concatenate([causal, zero, causal, chunky, zero, chunky], axis=1).astype(np.float32),
        "ident_tab": np.eye(P, dtype=np.float32),
    }


def build(nc, a, out, phases):
    stack = ExitStack()
    with stack:
        def sb(name, shape, dt=F32):
            return stack.enter_context(nc.sbuf_tensor(name, shape, dt))

        def sem(name):
            return stack.enter_context(nc.semaphore(name))

        raw = sb("raw", [P, RAWS, UNIT])
        w_hi = sb("w_hi", [P, SLOTS, UNIT], F32R)
        w_lo = sb("w_lo", [P, SLOTS, UNIT], F32R)
        x_sb = sb("x_sb", [P, T, D])
        t_hi = sb("t_hi", [P, KT, S], F32R)
        t_lo = sb("t_lo", [P, KT, S], F32R)
        f_hi = sb("f_hi", [P, 2, 512], F32R)
        f_lo = sb("f_lo", [P, 2, 512], F32R)
        g_row = sb("g_row", [P, D])
        ws = sb("ws", [P, WS])
        st = sb("st", [P, 160])
        ident = sb("ident", [P, P])
        masks = sb("masks", [P, 768])
        rope = sb("rope", [P, T, 192])
        zero_r = sb("zero_r", [P, 256], F32R)
        minus_half = sb("minus_half", [P, 8])
        mean_w = sb("mean_w", [P, P])
        p_col = sb("p_col", [P, P])
        tap_col = sb("tap_col", [P, P])
        qk_rope = sb("qk_rope", [P, 2, T, 128])
        subln = sb("subln", [P, P])

        bank = [stack.enter_context(nc.psum_tensor(f"bank{i}", [P, 512], F32)) for i in range(8)]

        def wv(at, *shape):
            n = int(np.prod(shape))
            v = ws[:, at:at + n]
            if len(shape) == 1:
                return v
            names = "abcd"[:len(shape)]
            return v.rearrange(f"p ({' '.join(names)}) -> p {' '.join(names)}",
                               **{c: s for c, s in zip(names, shape)})

        xn = wv(0, T, D)
        junk = wv(2048, D)
        f_s = wv(3072, 2, 512)
        f_p = wv(4096, 2, 512)
        p_rows, w_rows = wv(5120, P), wv(5248, P)
        lam_in, qk_g = wv(5376, 256), wv(5632, 2, 64)
        t1, t2, qr, qsq = wv(0, 512), wv(512, 512), wv(1024, 2, T, UC), wv(2048, 512)
        s_buf, p_buf, pt_buf = wv(0, 2, 384), wv(768, 2, 384), wv(1536, 2, 384)

        def heads64(buf, h):
            return buf[64 * (h % 2):64 * (h % 2) + 64, h // 2, :]

        def attention_plan(heads, q, k, v, o, mask, h0, bias=False):
            return dict(heads=heads, q=q, k=k, v=v, o=o, mask=mask, h0=h0, bias=bias, scale=1.0 if bias else 0.125,
                        mx=st[:, 48:48 + 2 * heads], nmax=st[:, 80:80 + 2 * heads], sum=st[:, 112:112 + 2 * heads])

        def table_mask(base):
            return lambda h, t: base[:, 0:128] if t == 0 else base[:, 128:384]

        h0 = 0
        for ph in phases:
            if ph["kind"] != "mix":
                continue
            if ph["which"] == "first":
                q, k, v = wv(5752, 4, S), wv(6776, 4, S), wv(7800, T, HW)
                V = dict(sig=wv(2560, 4, S), o=wv(2560, T, HW), hpad=wv(3584, 4, S + TAPS - 1), sq=wv(3584, 4, S),
                         acc=wv(4728, 4, S), cen=wv(0, 4, S), var=wv(1024, S), sw=wv(5752, 4, S), z=wv(6776, 4, S), v=v)
                V["L"] = attention_plan(8, lambda h, q=q: heads64(q, h), lambda h, k=k: heads64(k, h),
                                        lambda h, kt, v=v: v[:, kt, 64 * h:64 * h + 64],
                                        lambda h, t: bank[t][:, 64 * h:64 * h + 64], table_mask(masks[:, 0:384]), h0)
                h0 += 8
                w = a["w_in"][0]
                ph["units"] = ([(w, 3 * HW + HW + UC * i, UC, ("glu_g", i)) for i in range(2)]
                               + [(w, 3 * HW + UC * i, UC, ("glu_a", i)) for i in range(2)]
                               + [(w, HW + UC * i, UC, ("rope", 64, k[:, 2 * i:2 * i + 2, :], 1)) for i in range(2)]
                               + [(w, UC * i, UC, ("rope", 64, q[:, 2 * i:2 * i + 2, :], 0)) for i in range(2)]
                               + [(w, 2 * HW + UC * i, UC, ("v", v[:, :, UC * i:UC * (i + 1)])) for i in range(2)])
                ph["w_out"] = a["w_out"][0]
            elif ph["which"] == "even":
                bq, bk, aq, ak = (wv(2560 + 1024 * i, 4, S) for i in range(4))
                av, bv = wv(6656, T, HW), wv(7680, T, HW)
                iq, ik = wv(8704, 2, S), wv(9216, S)
                sel = wv(9472, 384)
                V = dict(iq=iq, ik=ik, rel=wv(768, 2, 384), sc=wv(0, 384), sel=sel, iw=wv(9856, T, 8),
                         oa=wv(4608, T, HW), oa1=wv(5632, T, HW), ob=wv(5632, T, HW), osq=wv(6656, T, HW))
                V["LA"] = attention_plan(8, lambda h: heads64(aq, h), lambda h: heads64(ak, h),
                                         lambda h, kt: av[:, kt, 128 * (h // 2):128 * (h // 2) + 128],
                                         lambda h, t: bank[2 * t + h % 2][:, 128 * (h // 2):128 * (h // 2) + 128],
                                         table_mask(masks[:, 384:768]), h0)
                V["LB"] = attention_plan(8, lambda h: heads64(bq, h), lambda h: heads64(bk, h),
                                         lambda h, kt: bv[:, kt, 64 * h:64 * h + 64],
                                         lambda h, t: bank[t][:, 64 * h:64 * h + 64], table_mask(sel), h0 + 8)
                h0 += 16
                w = a["even_w_in_2"][0]
                at = 3 * HW
                two = lambda c0, dst: [(w, c0 + UC * i, UC, ("rope", 64, dst[:, 2 * i:2 * i + 2, :], None)) for i in range(2)]
                val = lambda c0, dst: [(w, c0 + UC * i, UC, ("v", dst[:, :, UC * i:UC * (i + 1)])) for i in range(2)]
                ph["units"] = ([(w, 6 * HW, UC, ("rope", 32, iq, None)), (w, 6 * HW + UC, 40, ("tail", 32, ik, None))]
                               + two(at, bq) + two(at + HW, bk) + two(0, aq) + two(HW, ak) + val(2 * HW, av) + val(at + 2 * HW, bv))
                ph["w_out"] = a["even_w_out_2"][0]
            else:
                q, k, v = wv(2304, 8, S), wv(4352, 8, S), wv(6400, T, D)
                bias = wv(8448, 3, 384)
                V = dict(bias=bias, o=wv(2304, T, D))

                def reversed_bias(h, t):
                    b = bias[:, h % 3, 0:128] if t == 0 else bias[:, h % 3, 128:384]
                    n = b.shape[1]
                    return bass.AP(b.tensor, b.offset + n - 1, [list(b.ap[0]), [-1, n]])

                V["L"] = attention_plan(16, lambda h: heads64(q, h), lambda h: heads64(k, h),
                                        lambda h, kt: v[:, kt, 64 * h:64 * h + 64],
                                        lambda h, t: bank[2 * t + h // 8][:, 64 * (h % 8):64 * (h % 8) + 64], reversed_bias, h0, bias=True)
                h0 += 16
                w = a["odd_w_in_2"][0]
                ph["units"] = ([(w, UC * i, UC, ("c", q[:, 2 * i:2 * i + 2, :], 0.125)) for i in range(4)]
                               + [(w, D + UC * i, UC, ("c", k[:, 2 * i:2 * i + 2, :])) for i in range(4)]
                               + [(w, 2 * D + UC * i, UC, ("v", v[:, :, UC * i:UC * (i + 1)])) for i in range(4)])
                ph["w_out"] = a["odd_w_out_2"][0]
            ph["views"] = V

        raw_in = [sem(f"raw_in{i}") for i in range(RAWS)]
        setup_in = [sem(f"setup_in{i}") for i in range(3)]
        x_in = sem("x_in")
        hi_done = sem("hi_done")
        lo_done = sem("lo_done")
        unit_used = sem("unit_used")
        consts_set = sem("consts_set")
        params_T = sem("params_T")
        params_ok = sem("params_ok")
        x_ready = sem("x_ready")
        sq_done = sem("sq_done")
        ms_ready = sem("ms_ready")
        rstd_ready = sem("rstd_ready")
        xn_ready = sem("xn_ready")
        x_T = sem("x_T")
        t_hi_ok = sem("t_hi_ok")
        t_lo_ok = sem("t_lo_ok")
        silu_done = sem("silu_done")
        prod_done = sem("prod_done")
        prodhi_done = sem("prodhi_done")
        prodlo_done = sem("prodlo_done")
        grow_in = sem("grow_in")
        dve_step = sem("dve_step")
        act_step = sem("act_step")
        bank_free = [sem(f"bank_free{i}") for i in range(4)]
        roped = sem("roped")
        rope_T = sem("rope_T")
        rope_kept = sem("rope_kept")
        v_kept = sem("v_kept")
        sig_ok = sem("sig_ok")
        conv_ok = sem("conv_ok")
        mean_ok = sem("mean_ok")
        cen_ok = sem("cen_ok")
        sq4_ok = sem("sq4_ok")
        var_ok = sem("var_ok")
        z_ok = sem("z_ok")
        swish_ok = sem("swish_ok")
        qsq_ok = sem("qsq_ok")
        s_done = sem("s_done")
        nmax_ok = sem("nmax_ok")
        p_done = sem("p_done")
        pt_done = sem("pt_done")
        pt_kept = sem("pt_kept")
        o_done = sem("o_done")
        o_ready = sem("o_ready")
        o_T = sem("o_T")
        idx_done = sem("idx_done")
        idx_relu = sem("idx_relu")
        idx_added = sem("idx_added")
        bias_in = [sem(f"bias_in{i}") for i in range(3)]
        bias_set = sem("bias_set")
        lam_sum = sem("lam_sum")
        lam_exp = sem("lam_exp")
        out_done = sem("out_done")

        n_units = n_ffn = 0
        widths = {}
        uses = [0] * 4
        for ph in phases:
            ph["n0"] = n_units
            if ph["kind"] == "ffn":
                ph["f"] = n_ffn
                n_ffn += 1
                n_units += 3 * CHUNKS
            elif ph["kind"] == "mix":
                ph["left"] = []
                for j, u in enumerate(ph["units"]):
                    widths[n_units + j] = u[2]
                    uses[j % 4] += 1
                    ph["left"].append(uses[j % 4])
                n_units += len(ph["units"]) + 4
            ph["after"] = n_units
        N_UNITS = n_units
        GLU_B, DW_B, LN_G, LN_B = 64, 72, 76, 80

        def col_src(w, c0, nc_=UC):
            return w.rearrange("(k p) n -> p k n", p=P)[:, :, bass.ds(c0, nc_)]

        def row_src(w, r0):
            return w[bass.ds(r0, UC), :].rearrange("(r p) n -> p r n", p=P)

        def raw_view(n, w, by_rows=False):
            v = raw[:, n % RAWS, 0:KT * w]
            return v.rearrange("p (r n) -> p r n", r=2) if by_rows else v.rearrange("p (k n) -> p k n", k=KT)

        block = stack.enter_context(nc.Block())

        @block.sync
        def _(sp):
            def load(n, src, width=UC, by_rows=False, turn=0):
                if n >= RAWS:
                    sp.wait_ge(lo_done, n - RAWS + 1 + SLOTS * turn)
                sp.dma_start(raw_view(n, width, by_rows), src).then_inc(raw_in[n % RAWS], 16)

            for ph in phases:
                n = ph["n0"]
                if ph["kind"] == "mix":
                    for w, c0, width, _ in ph["units"]:
                        load(n, col_src(w, c0, width), width)
                        n += 1
                    for r in range(4):
                        load(n, row_src(ph["w_out"], r * UC), by_rows=True)
                        n += 1
                elif ph["kind"] == "ffn":
                    load(n, col_src(ph["wg"], 0))
                    load(n + 1, col_src(ph["wu"], 0))
                    with sp.Fori(0, CHUNKS // 2) as i:
                        for j in range(2):
                            m = n + 2 + 3 * j
                            c0 = i * (2 * UC) + (1 + j) * UC
                            load(m, col_src(ph["wg"], c0), turn=i)
                            load(m + 1, col_src(ph["wu"], c0), turn=i)
                            load(m + 2, row_src(ph["wd"], i * (2 * UC) + j * UC), by_rows=True, turn=i)
                    load(n + 3 * CHUNKS - 1, row_src(ph["wd"], FF - UC), by_rows=True)
            sp.wait_ge(out_done, 16)

        @block.scalar
        def _(act):
            seen = {}

            def nx(s, k=1):
                seen[id(s)] = seen.get(id(s), 0) + k
                return seen[id(s)]

            cur = [0]

            def split_hi(n, width=UC, turn=0):
                act.wait_ge(raw_in[n % RAWS], 16 * (n // RAWS + 1) + turn * (16 * SLOTS // RAWS))
                if n >= SLOTS:
                    act.wait_ge(unit_used, n - SLOTS + 1 + turn * SLOTS)
                w = KT * width
                nc.scalar.activation(w_hi[:, n % SLOTS, 0:w], raw[:, n % RAWS, 0:w], ACT.Copy).then_inc(hi_done, 1)

            def split_to(n):
                while cur[0] < min(n, N_UNITS):
                    split_hi(cur[0], widths.get(cur[0], UC))
                    cur[0] += 1

            def norm(ph):
                act.wait_ge(x_ready, nx(x_ready))
                for t in range(T):
                    if t:
                        act.wait_ge(sq_done, seen[id(sq_done)])
                    nc.scalar.activation(junk, x_sb[:, t, :], ACT.Square, accum_out=st[:, t:t + 1]).then_inc(sq_done, 1)
                    nx(sq_done)
                for k in range(KT):
                    if k % 2 == 0:
                        act.wait_ge(x_T, nx(x_T))
                    g = ph["g"] * KT + k
                    nc.scalar.activation(t_hi[:, k, :], bank[4 + k // 2][:, (k % 2) * S:(k % 2 + 1) * S], ACT.Copy,
                                         scale=p_col[:, g:g + 1]).then_inc(t_hi_ok, 1)

            def post_squares(ph):
                act.wait_ge(unit_used, ph["after"])
                for i in range(2 * T):
                    if i:
                        act.wait_ge(sq_done, seen[id(sq_done)])
                    nc.scalar.activation(junk[:, 0:512], bank[i][:, :], ACT.Square, accum_out=st[:, 4 + i:5 + i]).then_inc(sq_done, 1)
                    nx(sq_done)

            def ffn(ph):
                n0 = ph["n0"]

                def chunk(s, c, turn=0):
                    act.wait_ge(unit_used, s + 1 + turn * SLOTS)
                    nc.scalar.activation(f_s[:, c % 2, :], bank[4 + 2 * (c % 2)][:, :], ACT.Silu).then_inc(silu_done, 1)
                    act.wait_ge(prod_done, 1 + CHUNKS * ph["f"] + c + 1 + turn * 2)
                    nc.scalar.activation(f_hi[:, c % 2, :], f_p[:, c % 2, :], ACT.Copy).then_inc(prodhi_done, 1)

                split_to(n0 + 5)
                chunk(n0, 0)
                whole = CHUNKS // 2 if ph["n0"] + 3 * CHUNKS < N_UNITS else CHUNKS // 2 - 1
                with act.Fori(0, whole) as i:
                    for j in range(2):
                        for u in range(3):
                            split_hi(n0 + 5 + 3 * j + u, turn=i)
                        chunk(n0 + 2 + 3 * j, 1 + j, turn=i)
                cur[0] = n0 + 5 + 6 * whole
                for c in range(1 + 2 * whole, CHUNKS):
                    split_to(n0 + 3 * c + 5)
                    chunk(n0 + 3 * c - 1, c)

            def keep_rope(role):
                r = nx(rope_T) - 1
                act.wait_ge(rope_T, r + 1)
                n = S if role[0] == "tail" else 2 * S
                src = bank[4 + r % 4][:, 0:n]
                if role[0] != "tail":
                    src = src.rearrange("p (a s) -> p a s", a=2)
                nc.scalar.activation(role[2], src, ACT.Copy).then_inc(rope_kept, 1)

            def keep_unit(ph, j):
                act.wait_ge(unit_used, ph["n0"] + j + 1)
                nc.scalar.activation(ph["units"][j][3][1], bank[j % 4][:, :].rearrange("p (a s) -> p a s", a=2), ACT.Copy,
                                     scale=(ph["units"][j][3] + (1.0,))[2])\
                    .then_inc(bank_free[j % 4], 1)

            def keep_pt(L, h):
                act.wait_ge(pt_done, L["h0"] + h + 1)
                if h >= 2:
                    act.wait_ge(o_done, L["h0"] + h - 1)
                nc.scalar.activation(pt_buf[:, h % 2, :], bank[6 + h % 2][:, 0:384], ACT.Copy).then_inc(pt_kept, 1)

            def attention(L):
                for h in range(L["heads"]):
                    act.wait_ge(nmax_ok, L["h0"] + h + 1)
                    if h >= 2:
                        act.wait_ge(pt_done, L["h0"] + h - 1)
                    for t, (lo, hi) in enumerate(((0, 128), (128, 384))):
                        c = 2 * h + t
                        nc.scalar.activation(p_buf[:, h % 2, lo:hi], s_buf[:, h % 2, lo:hi], ACT.Exp, scale=L["scale"],
                                             bias=L["nmax"][:, c:c + 1], accum_out=L["sum"][:, c:c + 1]).then_inc(p_done, 1)
                    if h >= 1:
                        keep_pt(L, h - 1)
                keep_pt(L, L["heads"] - 1)

            def out_hi(banks):
                for j, b in enumerate(banks):
                    act.wait_ge(o_T, nx(o_T))
                    nc.scalar.activation(t_hi[:, 2 * j:2 * j + 2, :], bank[b][:, :].rearrange("p (a s) -> p a s", a=2),
                                         ACT.Copy).then_inc(t_hi_ok, 1)

            def project(ph):
                roped_before = None
                for j, (_, _, _, role) in enumerate(ph["units"]):
                    m = ph["n0"] + j
                    split_to(m + LEAD)
                    if role[0] in "vc":
                        keep_unit(ph, j)
                    elif role[0] == "glu_g":
                        act.wait_ge(unit_used, m + 1)
                        for c in range(2):
                            ct = 2 * role[1] + c
                            ins = nc.scalar.activation(ph["views"]["sig"][:, ct, :], bank[j % 4][:, c * S:(c + 1) * S], ACT.Sigmoid,
                                                       bias=p_col[:, GLU_B + 4 + ct:GLU_B + 5 + ct])
                        ins.then_inc(bank_free[j % 4], 1)
                    elif role[0] == "rope" and ph["which"] == "first":
                        act.wait_ge(unit_used, m + 1)
                        r = seen.get(id(rope_T), 0) + (roped_before is not None)
                        if r:
                            act.wait_ge(roped, r)
                        nc.scalar.activation(qsq, bank[j % 4][:, :], ACT.Square).then_inc(qsq_ok, 1)
                    if roped_before:
                        keep_rope(roped_before)
                    roped_before = role if role[0] in ("rope", "tail") else None

            def mix_first(ph):
                V = ph["views"]
                project(ph)
                attention(V["L"])
                nx(o_ready)
                act.wait_ge(cen_ok, 1)
                nc.scalar.activation(V["sq"], V["cen"], ACT.Square).then_inc(sq4_ok, 1)
                act.wait_ge(z_ok, 1)
                for ct in range(4):
                    nc.scalar.activation(V["sw"][:, ct, :], V["z"][:, ct, :], ACT.Silu, scale=p_col[:, LN_G + ct:LN_G + ct + 1],
                                         bias=p_col[:, LN_B + ct:LN_B + ct + 1]).then_inc(swish_ok, 1)
                act.wait_ge(swish_ok, 4)
                nc.scalar.activation(t_hi[:, 4:8, :], V["sw"], ACT.Copy).then_inc(t_hi_ok, 1)
                out_hi((6, 7))

            def mix_even(ph):
                V = ph["views"]
                project(ph)
                for h in range(8):
                    act.wait_ge(idx_done, h + 1)
                    if h >= 2:
                        act.wait_ge(idx_added, 2 * (h - 1))
                    nc.scalar.activation(V["rel"][:, h % 2, :], bank[4 + h % 4][:, 0:384], ACT.Relu).then_inc(idx_relu, 1)
                attention(V["LA"])
                attention(V["LB"])
                act.wait_ge(o_ready, nx(o_ready))
                nc.scalar.activation(V["osq"], V["oa"], ACT.Square).then_inc(qsq_ok, 1)
                nx(o_ready)
                out_hi((4, 5, 6, 7))

            def mix_odd(ph):
                project(ph)
                attention(ph["views"]["L"])
                nx(o_ready)
                out_hi((4, 5, 6, 7))

            for t in range(T):
                act.dma_start(x_sb[:, t, :], a["x"][0, t * P:(t + 1) * P, :]).then_inc(x_in, 16)
            act.wait_ge(lam_sum, 1)
            nc.scalar.activation(st[:, 22:24], st[:, 20:22], ACT.Exp).then_inc(lam_exp, 1)
            act.wait_ge(params_T, 2)
            nc.scalar.activation(p_col[:, :], bank[0][:, 0:P], ACT.Copy).then_inc(params_ok, 1)
            nc.scalar.activation(tap_col[:, :], bank[1][:, 0:P], ACT.Copy).then_inc(params_ok, 1)
            act.wait_ge(params_ok, 2)
            for ph in phases:
                if ph["kind"] == "norm":
                    norm(ph)
                elif ph["kind"] == "ffn":
                    ffn(ph)
                elif ph["kind"] == "post":
                    post_squares(ph)
                elif ph["kind"] == "mix":
                    {"first": mix_first, "even": mix_even, "odd": mix_odd}[ph["which"]](ph)
            act.wait_ge(x_ready, nx(x_ready))
            act.dma_start(out[0].rearrange("(t p) d -> p t d", p=P), x_sb[:, :, :]).then_inc(out_done, 16)

        @block.gpsimd
        def _(pool):
            seen = {}

            def nx(s, k=1):
                seen[id(s)] = seen.get(id(s), 0) + k
                return seen[id(s)]

            nc.gpsimd.memset(minus_half[:, :], -0.5).then_inc(consts_set, 1)
            nc.gpsimd.memset(mean_w[:, :], 1.0 / HW).then_inc(consts_set, 1)
            nc.gpsimd.memset(ws[:, 5120:5376], 0.0).then_inc(consts_set, 1)
            pool.wait_ge(consts_set, 3)
            pool.dma_start(ident[:, :], a["ident_tab"]).then_inc(setup_in[0], 16)
            for src, r0, nr in a["param_rows"]:
                pool.dma_start(p_rows[r0:r0 + nr, :], src).then_inc(setup_in[0], 16)
            pool.dma_start(w_rows[0:4 * TAPS, :], a["dw_w"][0].rearrange("t (c p) -> (t c) p", p=P)).then_inc(setup_in[0], 16)
            pool.dma_start(rope[:, :, :], a["rope_tab"].rearrange("(t p) c -> p t c", p=P)).then_inc(setup_in[1], 16)
            for i, name in enumerate(("q_norm_g", "k_norm_g")):
                pool.dma_start(qk_g[:, i, :], a[name][0, :].partition_broadcast(P)).then_inc(setup_in[1], 16)
            pool.dma_start(lam_in, a["even_lambda_2"][0].rearrange("a b -> (a b)").partition_broadcast(P)).then_inc(setup_in[1], 16)
            pool.dma_start(masks[:, :], a["mask_tab"]).then_inc(setup_in[1], 16)
            pool.dma_start(subln[:, :], a["even_subln_2"][0, :].partition_broadcast(P)).then_inc(setup_in[1], 16)

            def inv_root(v):
                pool.wait_ge(ms_ready, nx(ms_ready))
                nc.gpsimd.tensor_tensor(v, v, minus_half[:, 0:1].broadcast_to([P, v.shape[1]]), ALU.pow).then_inc(rstd_ready, 1)

            posts = [ph for ph in phases if ph["kind"] == "post"]
            if posts:
                pool.dma_start(g_row[:, :], posts[0]["row"].partition_broadcast(P)).then_inc(grow_in, 16)
            n_post = 0
            x_turn = 1
            for ph in phases:
                if ph["kind"] == "norm":
                    inv_root(st[:, 2:4])
                elif ph["kind"] == "add":
                    x_turn += 1
                elif ph["kind"] == "post":
                    inv_root(st[:, 8:10])
                    x_turn += 1
                    n_post += 1
                    if n_post < len(posts):
                        pool.wait_ge(x_ready, x_turn)
                        pool.dma_start(g_row[:, :], posts[n_post]["row"].partition_broadcast(P)).then_inc(grow_in, 16)
                elif ph["which" if ph["kind"] == "mix" else "kind"] == "first":
                    for r in range(4):
                        inv_root(st[:, 32 + 8 * (r % 2):40 + 8 * (r % 2)])
                    inv_root(ph["views"]["var"])
                elif ph["kind"] == "mix" and ph["which"] == "even":
                    inv_root(st[:, 32:40])
                elif ph["kind"] == "mix":
                    bias, L = ph["views"]["bias"], ph["views"]["L"]
                    for lo in (0, 128):
                        nc.gpsimd.memset(bias[0:64, :, lo:lo + 64], NEG).then_inc(bias_set, 1)
                    for h in range(16):
                        if h >= 3:
                            pool.wait_ge(nmax_ok, L["h0"] + h - 2)
                        for c in range(4):
                            row = a["odd_rel_bias_2"][0, h, 0:1]
                            src = bass.AP(row.tensor, row.offset, [[1, 64], [1, 64 * (c + 1)]])
                            end = (128, 384)[c // 2]
                            pool.dma_start(bias[64 * (c % 2):64 * (c % 2) + 64, h % 3, end - 64 * (c + 1):end], src)\
                                .then_inc(bias_in[h % 3], 16)

        @block.tensor
        def _(pe):
            seen = {}

            def nx(s, k=1):
                seen[id(s)] = seen.get(id(s), 0) + k
                return seen[id(s)]

            def three(o, lh, ll, rh, rl, start, stop):
                nc.tensor.matmul(o, lh, rh, start=start, stop=False)
                nc.tensor.matmul(o, lh, rl, start=False, stop=False)
                return nc.tensor.matmul(o, ll, rh, start=False, stop=stop)

            def w_cols(n, width=UC):
                v = [w[:, n % SLOTS, 0:KT * width].rearrange("p (k n) -> p k n", k=KT) for w in (w_hi, w_lo)]
                return v

            def by_channels(n, b, turn=0):
                pe.wait_ge(lo_done, n + 1 + turn * SLOTS)
                wh, wl = w_cols(n)
                for c in range(2):
                    for k in range(KT):
                        mm = three(bank[b][:, c * S:(c + 1) * S], wh[:, k, c * P:(c + 1) * P], wl[:, k, c * P:(c + 1) * P],
                                   t_hi[:, k, :], t_lo[:, k, :], k == 0, k == KT - 1)
                mm.then_inc(unit_used, 1)

            def by_tokens(n, b, width=UC):
                pe.wait_ge(lo_done, n + 1)
                wh, wl = w_cols(n, width)
                for t in range(T):
                    for k in range(KT):
                        mm = three(bank[b][:, t * UC:t * UC + width], t_hi[:, k, t * P:(t + 1) * P], t_lo[:, k, t * P:(t + 1) * P],
                                   wh[:, k, :], wl[:, k, :], k == 0, k == KT - 1)
                mm.then_inc(unit_used, 1)

            def by_rows(n, lh, ll, first=False, last=False, turn=0):
                pe.wait_ge(lo_done, n + 1 + turn * SLOTS)
                wh, wl = [w[:, n % SLOTS, :].rearrange("p (r n) -> p r n", r=2) for w in (w_hi, w_lo)]
                for r in range(2):
                    for t in range(T):
                        for h in range(2):
                            mm = three(bank[2 * t + h][:, :], lh(r, t), ll(r, t), wh[:, r, h * 512:(h + 1) * 512],
                                       wl[:, r, h * 512:(h + 1) * 512], first and r == 0, last and r == 1)
                mm.then_inc(unit_used, 1)

            def norm(ph):
                for t in range(T):
                    pe.wait_ge(xn_ready, nx(xn_ready))
                    for k in range(KT):
                        mm = nc.tensor.transpose(bank[4 + k // 2][:, (k % 2) * S + t * P:(k % 2) * S + (t + 1) * P],
                                                 xn[:, t, k * P:(k + 1) * P], ident[:, :])
                        if t == 1 and k % 2 == 1:
                            mm.then_inc(x_T, 1)
                pe.wait_ge(t_lo_ok, nx(t_lo_ok, KT))

            def ffn(ph):
                n0, c0 = ph["n0"], CHUNKS * ph["f"]
                for b in range(4):
                    for h in range(2):
                        nc.tensor.matmul(bank[b][:, h * 256:(h + 1) * 256], zero_r[:, 0:P], zero_r[:, :], start=h == 0, stop=False)

                def down(n, c, turn=0, last=False):
                    pe.wait_ge(prodlo_done, c0 + c + 1 + turn * 2)
                    by_rows(n, lambda r, t: f_hi[:, c % 2, r * S + t * P:r * S + (t + 1) * P],
                            lambda r, t: f_lo[:, c % 2, r * S + t * P:r * S + (t + 1) * P], turn=turn, last=last)

                by_channels(n0, 4)
                by_channels(n0 + 1, 5)
                with pe.Fori(0, CHUNKS // 2) as i:
                    for j in range(2):
                        b = 4 + 2 * ((1 + j) % 2)
                        pe.wait_ge(prod_done, 1 + c0 + j + i * 2)
                        by_channels(n0 + 2 + 3 * j, b, i)
                        by_channels(n0 + 3 + 3 * j, b + 1, i)
                        down(n0 + 4 + 3 * j, j, i)
                down(n0 + 3 * CHUNKS - 1, CHUNKS - 1, last=True)

            def turn_rope(role):
                r = nx(roped) - 1
                pe.wait_ge(roped, r + 1)
                if r >= 4:
                    pe.wait_ge(rope_kept, r - 3)
                for p in range(1 if role[0] == "tail" else 2):
                    for t in range(T):
                        mm = nc.tensor.transpose(bank[4 + r % 4][:, p * S + t * P:p * S + (t + 1) * P],
                                                 qr[:, r % 2, t, p * P:(p + 1) * P], ident[:, :])
                mm.then_inc(rope_T, 1)

            def project(ph):
                before = None
                for j, (_, _, width, role) in enumerate(ph["units"]):
                    if ph["left"][j] > 1:
                        pe.wait_ge(bank_free[j % 4], ph["left"][j] - 1)
                    if role[0] in ("glu_g", "glu_a", "c"):
                        by_channels(ph["n0"] + j, j % 4)
                    else:
                        by_tokens(ph["n0"] + j, j % 4, width)
                    if before:
                        turn_rope(before)
                    before = role if role[0] in ("rope", "tail") else None
                for j in range(len(ph["units"]) - 4, len(ph["units"])):
                    pe.wait_ge(bank_free[j % 4], ph["left"][j])
                if id(roped) in seen:
                    pe.wait_ge(rope_kept, seen[id(roped)])

            def attention(L):
                H = L["heads"]

                def scores(h):
                    if h >= 2:
                        pe.wait_ge(nmax_ok, L["h0"] + h - 1)
                    b = bank[4 + h % 2]
                    q, k = L["q"](h), L["k"](h)
                    nc.tensor.matmul(b[:, 0:128], q[:, 0:128], k[:, 0:128], start=True, stop=True)
                    nc.tensor.matmul(b[:, 128:384], q[:, 128:256], k[:, 0:256], start=True, stop=True).then_inc(s_done, 1)

                def turn(h):
                    pe.wait_ge(p_done, 2 * (L["h0"] + h + 1))
                    if h >= 2:
                        pe.wait_ge(pt_kept, L["h0"] + h - 1)
                    for i in range(3):
                        mm = nc.tensor.transpose(bank[6 + h % 2][:, i * P:(i + 1) * P], p_buf[:, h % 2, i * P:(i + 1) * P], ident[:, :])
                    mm.then_inc(pt_done, 1)

                def values(h):
                    pe.wait_ge(pt_kept, L["h0"] + h + 1)
                    pt = pt_buf
                    o0, o1 = L["o"](h, 0), L["o"](h, 1)
                    nc.tensor.matmul(o0, pt[:, h % 2, 0:128], L["v"](h, 0), start=True, stop=True)
                    nc.tensor.matmul(o1, pt[:, h % 2, 128:256], L["v"](h, 0), start=True, stop=False)
                    nc.tensor.matmul(o1, pt[:, h % 2, 256:384], L["v"](h, 1), start=False, stop=True).then_inc(o_done, 1)

                for h in range(H + 2):
                    if h < H:
                        scores(h)
                    if 1 <= h <= H:
                        turn(h - 1)
                    if h >= 2:
                        values(h - 2)

            def out_turn(src, banks):
                for j, b in enumerate(banks):
                    for c in range(2):
                        for t in range(T):
                            mm = nc.tensor.transpose(bank[b][:, c * S + t * P:c * S + (t + 1) * P], src(2 * j + c, t), ident[:, :])
                    mm.then_inc(o_T, 1)

            def out_proj(ph, n_lo):
                pe.wait_ge(t_lo_ok, nx(t_lo_ok, n_lo))
                n = ph["n0"] + len(ph["units"])
                for u in range(4):
                    by_rows(n + u, lambda r, t: t_hi[:, 2 * u + r, t * P:(t + 1) * P],
                            lambda r, t: t_lo[:, 2 * u + r, t * P:(t + 1) * P], first=u == 0, last=u == 3)

            def mix_first(ph):
                V = ph["views"]
                project(ph)
                attention(V["L"])
                pe.wait_ge(conv_ok, 4)
                for ct in range(4):
                    mm = nc.tensor.matmul(bank[4][:, 0:S], mean_w[:, :], V["acc"][:, ct, :], start=ct == 0, stop=ct == 3)
                mm.then_inc(mean_ok, 1)
                pe.wait_ge(sq4_ok, 1)
                for ct in range(4):
                    mm = nc.tensor.matmul(bank[5][:, 0:S], mean_w[:, :], V["sq"][:, ct, :], start=ct == 0, stop=ct == 3)
                mm.then_inc(var_ok, 1)
                pe.wait_ge(o_ready, nx(o_ready))
                out_turn(lambda k, t: V["o"][:, t, k * P:(k + 1) * P], (6, 7))
                out_proj(ph, 3)

            def mix_even(ph):
                V = ph["views"]
                project(ph)
                for h in range(8):
                    if h >= 4:
                        pe.wait_ge(idx_relu, h - 3)
                    q = V["iq"][32 * (h % 4):32 * (h % 4) + 32, h // 4, :]
                    k = V["ik"][32 * (h % 4):32 * (h % 4) + 32, :]
                    nc.tensor.matmul(bank[4 + h % 4][:, 0:128], q[:, 0:128], k[:, 0:128], start=True, stop=True)
                    nc.tensor.matmul(bank[4 + h % 4][:, 128:384], q[:, 128:256], k, start=True, stop=True).then_inc(idx_done, 1)
                pe.wait_ge(idx_relu, 8)
                attention(V["LA"])
                pe.wait_ge(o_ready, nx(o_ready))
                attention(V["LB"])
                pe.wait_ge(o_ready, nx(o_ready))
                out_turn(lambda k, t: (V["oa"] if k < 4 else V["ob"])[:, t, (k % 4) * P:(k % 4 + 1) * P], (4, 5, 6, 7))
                out_proj(ph, 4)

            def mix_odd(ph):
                V = ph["views"]
                project(ph)
                attention(V["L"])
                pe.wait_ge(o_ready, nx(o_ready))
                out_turn(lambda k, t: V["o"][:, t, k * P:(k + 1) * P], (4, 5, 6, 7))
                out_proj(ph, 4)

            pe.wait_ge(setup_in[0], 16 * (len(a["param_rows"]) + 2))
            nc.tensor.transpose(bank[0][:, 0:P], p_rows[:, :], ident[:, :]).then_inc(params_T, 1)
            nc.tensor.transpose(bank[1][:, 0:P], w_rows[:, :], ident[:, :]).then_inc(params_T, 1)
            pe.wait_ge(params_ok, 2)
            pe.wait_ge(dve_step, 1)
            for ph in phases:
                if ph["kind"] == "norm":
                    norm(ph)
                elif ph["kind"] == "ffn":
                    ffn(ph)
                elif ph["kind"] == "mix":
                    {"first": mix_first, "even": mix_even, "odd": mix_odd}[ph["which"]](ph)

        @block.vector
        def _(dve):
            seen = {}

            def nx(s, k=1):
                seen[id(s)] = seen.get(id(s), 0) + k
                return seen[id(s)]

            steps = [0]

            def step(ins):
                steps[0] += 1
                ins.then_inc(dve_step, 1)
                return steps[0]

            def link(ins):
                dve.wait_ge(dve_step, step(ins))

            cur = [0]

            def split_lo(n, width=UC, turn=0):
                dve.wait_ge(hi_done, n + 1 + turn * SLOTS)
                w = KT * width
                nc.vector.tensor_tensor(w_lo[:, n % SLOTS, 0:w], raw[:, n % RAWS, 0:w], w_hi[:, n % SLOTS, 0:w].bitcast(F32),
                                        ALU.subtract).then_inc(lo_done, 1)

            def split_to(n):
                while cur[0] < min(n, N_UNITS):
                    split_lo(cur[0], widths.get(cur[0], UC))
                    cur[0] += 1

            def norm(ph):
                dve.wait_ge(sq_done, nx(sq_done, T))
                nc.vector.tensor_scalar(st[:, 2:4], st[:, 0:2], 1.0 / D, EPS, ALU.mult, ALU.add).then_inc(ms_ready, 1)
                dve.wait_ge(rstd_ready, nx(rstd_ready))
                for t in range(T):
                    nc.vector.tensor_scalar(xn[:, t, :], x_sb[:, t, :], st[:, 2 + t:3 + t], None, ALU.mult).then_inc(xn_ready, 1)
                for k in range(KT):
                    if k % 2 == 0:
                        dve.wait_ge(t_hi_ok, nx(t_hi_ok, 2))
                    g = ph["g"] * KT + k
                    nc.vector.scalar_tensor_tensor(out=t_lo[:, k, :], in0=bank[4 + k // 2][:, (k % 2) * S:(k % 2 + 1) * S],
                                                   scalar=p_col[:, g:g + 1], in1=t_hi[:, k, :].bitcast(F32),
                                                   op0=ALU.mult, op1=ALU.subtract).then_inc(t_lo_ok, 1)

            def add(ph):
                dve.wait_ge(unit_used, ph["after"])
                for t in range(T):
                    for h in range(2):
                        xv = x_sb[:, t, h * 512:(h + 1) * 512]
                        ins = nc.vector.tensor_tensor(xv, bank[2 * t + h][:, :], xv, ALU.add)
                ins.then_inc(x_ready, 1)

            def post(ph):
                dve.wait_ge(sq_done, nx(sq_done, 2 * T))
                sy = st[:, 4:8].rearrange("p (t h) -> p t h", h=2)
                link(nc.vector.tensor_tensor(st[:, 8:10], sy[:, :, 0], sy[:, :, 1], ALU.add))
                nc.vector.tensor_scalar(st[:, 8:10], st[:, 8:10], 1.0 / D, EPS, ALU.mult, ALU.add).then_inc(ms_ready, 1)
                dve.wait_ge(rstd_ready, nx(rstd_ready))
                dve.wait_ge(grow_in, nx(grow_in, 16))
                for t in range(T):
                    for h in range(2):
                        ins = nc.vector.scalar_tensor_tensor(out=xn[:, t, h * 512:(h + 1) * 512], in0=bank[2 * t + h][:, :],
                                                             scalar=st[:, 8 + t:9 + t], in1=g_row[:, h * 512:(h + 1) * 512],
                                                             op0=ALU.mult, op1=ALU.mult)
                link(ins)
                nc.vector.scalar_tensor_tensor(out=x_sb[:, :, :], in0=xn[:, :, :], scalar=ph["scale"], in1=x_sb[:, :, :],
                                               op0=ALU.mult, op1=ALU.add).then_inc(x_ready, 1)

            def ffn(ph):
                n0, c0 = ph["n0"], CHUNKS * ph["f"]

                def chunk(s, c, turn=0):
                    b = c % 2
                    dve.wait_ge(silu_done, c0 + c + 1 + turn * 2)
                    dve.wait_ge(unit_used, s + 1 + turn * SLOTS)
                    nc.vector.tensor_tensor(f_p[:, b, :], bank[5 + 2 * b][:, :], f_s[:, b, :], ALU.mult).then_inc(prod_done, 1)
                    dve.wait_ge(prodhi_done, c0 + c + 1 + turn * 2)
                    nc.vector.tensor_tensor(f_lo[:, b, :], f_p[:, b, :], f_hi[:, b, :].bitcast(F32), ALU.subtract)\
                        .then_inc(prodlo_done, 1)

                split_to(n0 + 5)
                chunk(n0 + 1, 0)
                whole = CHUNKS // 2 if n0 + 3 * CHUNKS < N_UNITS else CHUNKS // 2 - 1
                with dve.Fori(0, whole) as i:
                    for j in range(2):
                        for u in range(3):
                            split_lo(n0 + 5 + 3 * j + u, turn=i)
                        chunk(n0 + 3 + 3 * j, 1 + j, turn=i)
                cur[0] = n0 + 5 + 6 * whole
                for c in range(1 + 2 * whole, CHUNKS):
                    split_to(n0 + 3 * c + 5)
                    chunk(n0 + 3 * c, c)

            def rope_unit(ph, j, tab, per=None):
                _, _, width, role = ph["units"][j]
                dim = role[1]
                r = nx(roped) - 1
                if r >= 2:
                    dve.wait_ge(rope_T, r - 1)
                if r:
                    dve.wait_ge(roped, r)
                w = dim if role[0] == "tail" else width
                H, hd = w // dim, dim // 2
                x = bank[j % 4][:, :].rearrange("p (t w) -> p t w", t=T)[:, :, 0:w].rearrange("p t (h d) -> p t h d", d=dim)
                cos = tab[:, :, 0:dim].unsqueeze(2).broadcast_to([P, T, H, dim])
                sin = tab[:, :, dim:2 * dim].unsqueeze(2).broadcast_to([P, T, H, dim])
                c_ = t1[:, 0:T * w].rearrange("p (t h d) -> p t h d", t=T, h=H)
                s_ = t2[:, 0:T * w].rearrange("p (t h d) -> p t h d", t=T, h=H)
                if role[0] == "tail":
                    iw = bank[j % 4][:, :].rearrange("p (t w) -> p t w", t=T)[:, :, dim:dim + 8]
                    nc.vector.tensor_scalar(ph["views"]["iw"], iw, 1.0 / 16, None, ALU.mult)
                nc.vector.tensor_tensor(c_, x, cos, ALU.mult)
                nc.vector.tensor_tensor(s_[:, :, :, 0:hd], x[:, :, :, hd:dim], sin[:, :, :, 0:hd], ALU.mult)
                nc.vector.tensor_tensor(s_[:, :, :, hd:dim], x[:, :, :, 0:hd], sin[:, :, :, hd:dim], ALU.mult)\
                    .then_inc(bank_free[j % 4], 1)
                dve.wait_ge(bank_free[j % 4], ph["left"][j])
                dst = qr[:, r % 2, :, :].rearrange("p t (h d) -> p t h d", d=dim)
                if per is not None:
                    link(nc.vector.tensor_tensor(c_, c_, s_, ALU.add))
                    nc.vector.tensor_tensor(dst, c_, per, ALU.mult).then_inc(roped, 1)
                elif role[0] == "tail":
                    four = [P, T, 4, dim]
                    nc.vector.tensor_tensor(dst[:, :, 0:4, :], c_.broadcast_to(four), s_.broadcast_to(four), ALU.add).then_inc(roped, 1)
                else:
                    nc.vector.tensor_tensor(dst, c_, s_, ALU.add).then_inc(roped, 1)

            def attention(L, between=None):
                for h in range(L["heads"]):
                    dve.wait_ge(s_done, L["h0"] + h + 1)
                    if h >= 2:
                        dve.wait_ge(p_done, 2 * (L["h0"] + h - 1))
                    if L["bias"]:
                        dve.wait_ge(bias_in[h % 3], 64 * (h // 3 + 1))
                    for t, (lo, hi) in enumerate(((0, 128), (128, 384))):
                        c = 2 * h + t
                        ins = nc.vector.tensor_tensor_reduce(
                            out=s_buf[:, h % 2, lo:hi], in0=bank[4 + h % 2][:, lo:hi], in1=L["mask"](h, t), scale=1.0,
                            scalar=-3e38, op0=ALU.add, op1=ALU.max, accum_out=L["mx"][:, c:c + 1])
                    link(ins)
                    nc.vector.tensor_scalar(L["nmax"][:, 2 * h:2 * h + 2], L["mx"][:, 2 * h:2 * h + 2], -L["scale"], None, ALU.mult)\
                        .then_inc(nmax_ok, 1)
                    if between:
                        between()

            def inverse_sums(L):
                dve.wait_ge(o_done, L["h0"] + L["heads"])
                link(nc.vector.reciprocal(L["sum"], L["sum"]))
                return L["sum"]

            def out_lo(banks):
                for j, b in enumerate(banks):
                    dve.wait_ge(t_hi_ok, nx(t_hi_ok))
                    nc.vector.tensor_tensor(t_lo[:, 2 * j:2 * j + 2, :], bank[b][:, :].rearrange("p (a s) -> p a s", a=2),
                                            t_hi[:, 2 * j:2 * j + 2, :].bitcast(F32), ALU.subtract).then_inc(t_lo_ok, 1)

            def heads_out(L, o, per_bank):
                rs = inverse_sums(L).rearrange("p (h t) -> p h t", t=T)
                G = L["heads"] // per_bank
                for t in range(T):
                    for g in range(G):
                        ins = nc.vector.tensor_tensor(
                            o[:, t, g * HW:(g + 1) * HW].rearrange("p (h d) -> p h d", d=64),
                            bank[G * t + g][:, :].rearrange("p (h d) -> p h d", d=64),
                            rs[:, g * 8:(g + 1) * 8, t].unsqueeze(2).broadcast_to([P, 8, 64]), ALU.mult)
                return ins

            def mix_first(ph):
                V = ph["views"]
                link(nc.vector.memset(V["hpad"][:, :, 0:TAPS - 1], 0.0))
                taps_done = [0]
                tap_step = {}

                def taps(n):
                    for tap in range(taps_done[0], min(TAPS, taps_done[0] + n)):
                        for ct in range(4):
                            src = V["hpad"][:, ct, tap:tap + S]
                            w = tap_col[:, 4 * tap + ct:4 * tap + ct + 1]
                            acc = V["acc"][:, ct, :]
                            if tap == 0:
                                ins = nc.vector.tensor_scalar(acc, src, w, p_col[:, DW_B + ct:DW_B + ct + 1], ALU.mult, ALU.add)
                            else:
                                dve.wait_ge(dve_step, tap_step[ct])
                                ins = nc.vector.scalar_tensor_tensor(out=acc, in0=src, scalar=w, in1=acc, op0=ALU.mult, op1=ALU.add)
                            if tap == TAPS - 1:
                                ins.then_inc(conv_ok, 1)
                            else:
                                tap_step[ct] = step(ins)
                    taps_done[0] = min(TAPS, taps_done[0] + n)

                for j, (_, _, _, role) in enumerate(ph["units"]):
                    m = ph["n0"] + j
                    split_to(m + LEAD)
                    if role[0] == "glu_a":
                        dve.wait_ge(unit_used, m + 1)
                        dve.wait_ge(bank_free[j % 4 - 2], ph["left"][j - 2])
                        for c in range(2):
                            ct = 2 * role[1] + c
                            ins = nc.vector.scalar_tensor_tensor(
                                out=V["hpad"][:, ct, TAPS - 1:TAPS - 1 + S], in0=bank[j % 4][:, c * S:(c + 1) * S],
                                scalar=p_col[:, GLU_B + ct:GLU_B + ct + 1], in1=V["sig"][:, ct, :], op0=ALU.add, op1=ALU.mult)
                        ins.then_inc(bank_free[j % 4], 1)
                        dve.wait_ge(bank_free[j % 4], ph["left"][j])
                    elif role[0] == "rope":
                        r = role_index[j]
                        dve.wait_ge(qsq_ok, nx(qsq_ok))
                        s8 = st[:, 32 + 8 * (r % 2):40 + 8 * (r % 2)]
                        link(nc.vector.tensor_reduce(s8, qsq.rearrange("p (a d) -> p a d", d=64), AX.X, ALU.add))
                        nc.vector.tensor_scalar(s8, s8, 1.0 / 64, EPS, ALU.mult, ALU.add).then_inc(ms_ready, 1)
                        taps(1)
                        dve.wait_ge(rstd_ready, nx(rstd_ready))
                        rope_unit(ph, j, qk_rope[:, role[3], :, :],
                                  per=s8.rearrange("p (t h) -> p t h", t=T).unsqueeze(3).broadcast_to([P, T, 4, 64]))
                        taps(3)
                    elif role[0] == "v":
                        taps(3)
                attention(V["L"], between=lambda: taps(1))
                taps(TAPS)
                heads_out(V["L"], V["o"], 8).then_inc(o_ready, 1)
                dve.wait_ge(mean_ok, 1)
                nc.vector.tensor_tensor(V["cen"], V["acc"], bank[4][:, 0:S].unsqueeze(1).broadcast_to([P, 4, S]), ALU.subtract)\
                    .then_inc(cen_ok, 1)
                dve.wait_ge(var_ok, 1)
                nc.vector.tensor_scalar(V["var"], bank[5][:, 0:S], EPS, None, ALU.add).then_inc(ms_ready, 1)
                dve.wait_ge(rstd_ready, nx(rstd_ready))
                nc.vector.tensor_tensor(V["z"], V["cen"], V["var"].unsqueeze(1).broadcast_to([P, 4, S]), ALU.mult).then_inc(z_ok, 1)
                dve.wait_ge(t_hi_ok, nx(t_hi_ok))
                nc.vector.tensor_tensor(t_lo[:, 4:8, :], V["sw"], t_hi[:, 4:8, :].bitcast(F32), ALU.subtract).then_inc(t_lo_ok, 1)
                out_lo((6, 7))

            role_index = {4: 0, 5: 1, 6: 2, 7: 3}

            def select_keys(V):
                sc, sel = V["sc"], V["sel"]
                tiles = ((0, 128), (128, 384))
                for h in range(8):
                    dve.wait_ge(idx_relu, h + 1)
                    if h:
                        dve.wait_ge(idx_added, 2 * h)
                    for t, (lo, hi) in enumerate(tiles):
                        prior = masks[:, 384 + lo:384 + hi] if h == 0 else sc[:, lo:hi]
                        nc.vector.scalar_tensor_tensor(out=sc[:, lo:hi], in0=V["rel"][:, h % 2, lo:hi], scalar=V["iw"][:, t, h:h + 1],
                                                       in1=prior, op0=ALU.mult, op1=ALU.add).then_inc(idx_added, 1)
                dve.wait_ge(idx_added, 16)
                for i in range(TOPK // 8):
                    for t, (lo, hi) in enumerate(tiles):
                        ins = nc.vector.max(out=st[:, 144 + 8 * t:152 + 8 * t], in_=sc[:, lo:hi])
                    link(ins)
                    for t, (lo, hi) in enumerate(tiles):
                        ins = nc.vector.match_replace(out=sc[:, lo:hi], in_to_replace=st[:, 144 + 8 * t:152 + 8 * t],
                                                      in_values=sc[:, lo:hi], imm_value=TAKEN)
                    link(ins)
                link(nc.vector.tensor_scalar(sel, sc, TAKEN / 2, -NEG, ALU.is_le, ALU.mult))
                link(nc.vector.tensor_scalar(sel, sel, NEG, None, ALU.add))

            def mix_even(ph):
                V = ph["views"]
                for j, (_, _, _, role) in enumerate(ph["units"]):
                    split_to(ph["n0"] + j + LEAD)
                    if role[0] in ("rope", "tail"):
                        dve.wait_ge(unit_used, ph["n0"] + j + 1)
                        rope_unit(ph, j, rope[:, :, 0:128] if role[1] == 64 else rope[:, :, 128:192])
                select_keys(V)
                LA, LB = V["LA"], V["LB"]
                attention(LA)
                rs = inverse_sums(LA).rearrange("p (h c t) -> p h c t", c=2, t=T)
                for t in range(T):
                    ins = nc.vector.tensor_scalar(rs[:, :, 1, t], rs[:, :, 1, t], st[:, 24:25], None, ALU.mult)
                link(ins)
                for t in range(T):
                    for c in range(2):
                        ins = nc.vector.tensor_tensor(
                            (V["oa"], V["oa1"])[c][:, t, :].rearrange("p (h d) -> p h d", d=128),
                            bank[2 * t + c][:, :].rearrange("p (h d) -> p h d", d=128),
                            rs[:, :, c, t].unsqueeze(2).broadcast_to([P, 4, 128]), ALU.mult)
                link(ins)
                nc.vector.tensor_tensor(V["oa"], V["oa"], V["oa1"], ALU.subtract).then_inc(o_ready, 1)
                attention(LB)
                link(heads_out(LB, V["ob"], 8))
                dve.wait_ge(qsq_ok, nx(qsq_ok))
                link(nc.vector.tensor_reduce(st[:, 32:40], V["osq"].rearrange("p t (h d) -> p (t h) d", d=128), AX.X, ALU.add))
                nc.vector.tensor_scalar(st[:, 32:40], st[:, 32:40], 1.0 / 128, EPS, ALU.mult, ALU.add).then_inc(ms_ready, 1)
                dve.wait_ge(rstd_ready, nx(rstd_ready))
                oa = V["oa"].rearrange("p t (h d) -> p (t h) d", d=128)
                link(nc.vector.scalar_tensor_tensor(out=oa, in0=oa, scalar=1.0 - LAMBDA_INIT, in1=st[:, 32:40].unsqueeze(2).broadcast_to([P, 8, 128]),
                                                    op0=ALU.mult, op1=ALU.mult))
                nc.vector.tensor_tensor(oa, oa, subln[:, :].unsqueeze(1).broadcast_to([P, 8, 128]), ALU.mult).then_inc(o_ready, 1)
                out_lo((4, 5, 6, 7))

            def mix_odd(ph):
                V = ph["views"]
                for j in range(len(ph["units"])):
                    split_to(ph["n0"] + j + LEAD)
                dve.wait_ge(bias_set, 2)
                attention(V["L"])
                heads_out(V["L"], V["o"], 8).then_inc(o_ready, 1)
                out_lo((4, 5, 6, 7))

            nc.vector.memset(zero_r[:, :].bitcast(F32), 0.0).then_inc(dve_step, 1)
            steps[0] = 1
            dve.wait_ge(x_in, 16 * T)
            dve.wait_ge(consts_set, 3)
            dve.wait_ge(setup_in[1], 16 * 6)
            for i in range(2):
                ins = nc.vector.tensor_tensor_reduce(out=t1[:, 64 * i:64 * i + 64], in0=lam_in[:, 128 * i:128 * i + 64],
                                                     in1=lam_in[:, 128 * i + 64:128 * i + 128], scale=1.0, scalar=0.0,
                                                     op0=ALU.mult, op1=ALU.add, accum_out=st[:, 20 + i:21 + i])
            ins.then_inc(lam_sum, 1)
            dve.wait_ge(lam_exp, 1)
            link(nc.vector.tensor_tensor(st[:, 24:25], st[:, 22:23], st[:, 23:24], ALU.subtract))
            nc.vector.tensor_scalar(st[:, 24:25], st[:, 24:25], LAMBDA_INIT, None, ALU.add)
            for i in range(2):
                g = qk_g[:, i, :].unsqueeze(1).broadcast_to([P, T, 64])
                nc.vector.tensor_tensor(qk_rope[:, i, :, 0:64], rope[:, :, 0:64], g, ALU.mult)
                nc.vector.tensor_tensor(qk_rope[:, i, :, 64:96], rope[:, :, 64:96], g[:, :, 32:64], ALU.mult)
                ins = nc.vector.tensor_tensor(qk_rope[:, i, :, 96:128], rope[:, :, 96:128], g[:, :, 0:32], ALU.mult)
            link(ins)
            nc.vector.memset(st[:, 101:102], 0.0).then_inc(x_ready, 1)
            nc.vector.memset(st[:, 102:103], 0.0).then_inc(prod_done, 1)
            for ph in phases:
                if ph["kind"] == "norm":
                    norm(ph)
                elif ph["kind"] == "ffn":
                    ffn(ph)
                elif ph["kind"] == "add":
                    add(ph)
                elif ph["kind"] == "post":
                    post(ph)
                elif ph["kind"] == "mix":
                    {"first": mix_first, "even": mix_even, "odd": mix_odd}[ph["which"]](ph)


_INS = ["x", "norm1_g", "w_in", "glu_b", "q_norm_g", "k_norm_g", "dw_w", "dw_b", "conv_ln_g", "conv_ln_b", "w_out", "norm2_g",
        "w_gate", "w_up", "w_down", "norm_g_2", "ffn_wg_2", "ffn_wu_2", "ffn_wd_2", "even_w_in_2", "even_w_out_2",
        "even_lambda_2", "even_subln_2", "odd_w_in_2", "odd_w_out_2", "odd_rel_bias_2"]
STOP = None


def plan(a):
    def mlp(l, i):
        return dict(kind="ffn", wg=a["ffn_wg_2"][l, i], wu=a["ffn_wu_2"][l, i], wd=a["ffn_wd_2"][l, i])

    def post(l, i, scale):
        return dict(kind="post", row=a["norm_g_2"][l, i, :], scale=scale)

    ph = [dict(kind="norm", g=0), dict(kind="mix", which="first"), dict(kind="add"),
          dict(kind="norm", g=1), dict(kind="ffn", wg=a["w_gate"][0], wu=a["w_up"][0], wd=a["w_down"][0]), dict(kind="add")]
    for l in range(2):
        ph += [dict(kind="norm", g=2 + 3 * l), mlp(l, 0), post(l, 1, 0.5),
               dict(kind="norm", g=3 + 3 * l), dict(kind="mix", which=("even", "odd")[l]), post(l, 3, 1.0),
               dict(kind="norm", g=4 + 3 * l), mlp(l, 1), post(l, 5, 0.5)]
    return ph[STOP] if STOP else ph


def kernel(**inputs):
    import concourse.bacc as _bacc
    from concourse.bass_utils import run_bass_kernel_spmd as _run

    nc = _bacc.Bacc("TRN2", target_bir_lowering=False, num_devices=1)
    arrays, a = {}, {}
    given = {name: np.ascontiguousarray(inputs[name]) for name in _INS}
    given.update(host_tables())
    for name, v in given.items():
        arrays[f"in_{name}"] = v
        a[name] = nc.dram_tensor(f"in_{name}", v.shape, mybir.dt.from_np(v.dtype), kind="ExternalInput").ap()
    out = nc.dram_tensor("out_x", (1, S, D), F32, kind="ExternalOutput").ap()

    def rows(v):
        return v.rearrange("(r p) -> r p", p=P)

    norms = [a["norm1_g"][0], a["norm2_g"][0]] + [a["norm_g_2"][l, i] for l in range(2) for i in (0, 2, 4)]
    a["param_rows"] = ([(rows(v), 8 * i, 8) for i, v in enumerate(norms)]
                       + [(rows(a["glu_b"][0]), 64, 8), (rows(a["dw_b"][0]), 72, 4), (rows(a["conv_ln_g"][0]), 76, 4),
                          (rows(a["conv_ln_b"][0]), 80, 4)])
    build(nc, a, out, plan(a))
    r = _run(nc, [arrays], core_ids=[0])
    return r.results[0]["out_x"]
```

```python
import math
from contextlib import ExitStack

import numpy as np
import concourse.bass as bass
from concourse import mybir

F32 = mybir.dt.float32
F32R = mybir.dt.float32r
ALU = mybir.AluOpType
ACT = mybir.ActivationFunctionType
AX = mybir.AxisListType

P = 128
S = 256
T = S // P
D = 1024
KT = D // P
FF = 2816
UC = 256
UNIT = KT * UC
CHUNKS = FF // UC
HW = 512
RAWS = 3
SLOTS = 6
LEAD = SLOTS - 1
TAPS = 31
EPS = 1e-6
NEG = -1e30
TAKEN = -3e38
TOPK = 64
LAMBDA_INIT = 0.8 - 0.6 * math.exp(-0.3 * 0)
WS = 9984


def host_tables():
    def rope(dim):
        inv = (np.float32(10000.0) ** (-np.arange(0, dim, 2, dtype=np.float32) / np.float32(dim))).astype(np.float32)
        ang = np.arange(S, dtype=np.float32)[:, None] * inv[None, :]
        c, s = np.cos(ang).astype(np.float32), np.sin(ang).astype(np.float32)
        return np.concatenate([c, c, -s, s], axis=1)
    r64, r32 = rope(64), rope(32)
    q, k = np.arange(P)[:, None], np.arange(P)[None, :]
    zero = np.zeros((P, P), np.float32)
    causal = np.where(k <= q, 0.0, NEG).astype(np.float32)
    chunky = np.where(k // 64 <= q // 64, 0.0, NEG).astype(np.float32)
    return {
        "rope_tab": np.concatenate([r64, r32], axis=1).astype(np.float32),
        "mask_tab": np.concatenate([causal, zero, causal, chunky, zero, chunky], axis=1).astype(np.float32),
        "ident_tab": np.eye(P, dtype=np.float32),
    }


def build(nc, a, out, phases):
    stack = ExitStack()
    with stack:
        def sb(name, shape, dt=F32):
            return stack.enter_context(nc.sbuf_tensor(name, shape, dt))

        def sem(name):
            return stack.enter_context(nc.semaphore(name))

        raw = sb("raw", [P, RAWS, UNIT])
        w_hi = sb("w_hi", [P, SLOTS, UNIT], F32R)
        w_lo = sb("w_lo", [P, SLOTS, UNIT], F32R)
        x_sb = sb("x_sb", [P, T, D])
        t_hi = sb("t_hi", [P, KT, S], F32R)
        t_lo = sb("t_lo", [P, KT, S], F32R)
        f_hi = sb("f_hi", [P, 2, 512], F32R)
        f_lo = sb("f_lo", [P, 2, 512], F32R)
        g_row = sb("g_row", [P, D])
        ws = sb("ws", [P, WS])
        st = sb("st", [P, 160])
        ident = sb("ident", [P, P])
        masks = sb("masks", [P, 768])
        rope = sb("rope", [P, T, 192])
        zero_r = sb("zero_r", [P, 256], F32R)
        minus_half = sb("minus_half", [P, 8])
        mean_w = sb("mean_w", [P, P])
        p_col = sb("p_col", [P, P])
        tap_col = sb("tap_col", [P, P])
        qk_rope = sb("qk_rope", [P, 2, T, 128])
        subln = sb("subln", [P, P])

        psum = stack.enter_context(nc.psum_tensor("psum", [P, 8, 512], F32))
        bank = [psum[:, i, :] for i in range(8)]

        def wv(at, *shape):
            n = int(np.prod(shape))
            v = ws[:, at:at + n]
            if len(shape) == 1:
                return v
            names = "abcd"[:len(shape)]
            return v.rearrange(f"p ({' '.join(names)}) -> p {' '.join(names)}",
                               **{c: s for c, s in zip(names, shape)})

        xn = wv(0, T, D)
        junk = wv(5120, 2, D)
        f_s = wv(3072, 2, 512)
        f_p = wv(4096, 2, 512)
        yg = wv(7168, T, D)
        p_rows, w_rows = wv(9216, P), wv(9344, P)
        lam_in, qk_g = wv(9472, 256), wv(9728, 2, 64)
        t1, t2, qr, qsq = wv(0, 512), wv(512, 512), wv(1024, 2, T, UC), wv(2048, 512)
        s_buf, p_buf, pt_buf = wv(0, 2, 384), wv(768, 2, 384), wv(1536, 2, 384)

        def heads64(buf, h):
            return buf[64 * (h % 2):64 * (h % 2) + 64, h // 2, :]

        def attention_plan(heads, q, k, v, o, mask, h0, bias=False):
            return dict(heads=heads, q=q, k=k, v=v, o=o, mask=mask, h0=h0, bias=bias, scale=1.0 if bias else 0.125,
                        mx=st[:, 48:48 + 2 * heads], nmax=st[:, 80:80 + 2 * heads], sum=st[:, 112:112 + 2 * heads])

        def table_mask(base):
            return lambda h, t: base[:, 0:128] if t == 0 else base[:, 128:384]

        h0 = 0
        for ph in phases:
            if ph["kind"] != "mix":
                continue
            if ph["which"] == "first":
                q, k, v = wv(5752, 4, S), wv(6776, 4, S), wv(7800, T, HW)
                V = dict(sig=wv(2560, 4, S), o=wv(2560, T, HW), hpad=wv(3584, 4, S + TAPS - 1), sq=wv(3584, 4, S),
                         acc=wv(4728, 4, S), sw=wv(5752, 4, S), z=wv(6776, 4, S), v=v,
                         product=wv(8824, 2, S))
                V["cen"] = V["acc"]
                V["L"] = attention_plan(8, lambda h, q=q: heads64(q, h), lambda h, k=k: heads64(k, h),
                                        lambda h, kt, v=v: v[:, kt, 64 * h:64 * h + 64],
                                        lambda h, t: bank[t][:, 64 * h:64 * h + 64], table_mask(masks[:, 0:384]), h0)
                h0 += 8
                w = a["w_in"][0]
                ph["units"] = ([(w, 3 * HW + HW + UC * i, UC, ("glu_g", i)) for i in range(2)]
                               + [(w, 3 * HW + UC * i, UC, ("glu_a", i)) for i in range(2)]
                               + [(w, HW + UC * i, UC, ("rope", 64, k[:, 2 * i:2 * i + 2, :], 1)) for i in range(2)]
                               + [(w, UC * i, UC, ("rope", 64, q[:, 2 * i:2 * i + 2, :], 0)) for i in range(2)]
                               + [(w, 2 * HW + UC * i, UC, ("v", v[:, :, UC * i:UC * (i + 1)])) for i in range(2)])
                ph["w_out"] = a["w_out"][0]
            elif ph["which"] == "even":
                bq, bk, aq, ak = (wv(2560 + 1024 * i, 4, S) for i in range(4))
                av, bv = wv(6656, T, HW), wv(7680, T, HW)
                iq, ik = wv(8704, 2, S), wv(9216, S)
                sel = wv(9472, 384)
                V = dict(iq=iq, ik=ik, rel=wv(6656, 4, 384), sel=sel, iw=wv(9856, T, 8),
                         oa=wv(4608, T, HW), oa1=wv(5632, T, HW), ob=wv(5632, T, HW), osq=wv(6656, T, HW))
                V["L"] = attention_plan(
                    16, lambda h: heads64((aq, bq)[h // 8], h % 8), lambda h: heads64((ak, bk)[h // 8], h % 8),
                    lambda h, kt: av[:, kt, 128 * (h // 2):128 * (h // 2) + 128] if h < 8 else bv[:, kt, 64 * h - 512:64 * h - 448],
                    lambda h, t: (bank[2 * t + h % 2][:, 128 * (h // 2):128 * (h // 2) + 128] if h < 8
                                  else bank[t][:, 64 * h - 512:64 * h - 448]),
                    lambda h, t: table_mask(masks[:, 384:768] if h < 8 else sel)(h, t), h0)
                h0 += 16
                w = a["even_w_in_2"][0]
                at = 3 * HW
                two = lambda c0, dst: [(w, c0 + UC * i, UC, ("rope", 64, dst[:, 2 * i:2 * i + 2, :], None)) for i in range(2)]
                val = lambda c0, dst: [(w, c0 + UC * i, UC, ("v", dst[:, :, UC * i:UC * (i + 1)])) for i in range(2)]
                ph["units"] = ([(w, 6 * HW, UC, ("rope", 32, iq, None)), (w, 6 * HW + UC, 40, ("tail", 32, ik, None))]
                               + two(at, bq) + two(at + HW, bk) + two(0, aq) + two(HW, ak) + val(2 * HW, av) + val(at + 2 * HW, bv))
                ph["w_out"] = a["even_w_out_2"][0]
            else:
                q, k, v = wv(2304, 8, S), wv(4352, 8, S), wv(6400, T, D)
                bias = wv(8448, 3, 384)
                V = dict(bias=bias, o=wv(2304, T, D))

                def reversed_bias(h, t):
                    b = bias[:, h % 3, 0:128] if t == 0 else bias[:, h % 3, 128:384]
                    n = b.shape[1]
                    return bass.AP(b.tensor, b.offset + n - 1, [list(b.ap[0]), [-1, n]])

                V["L"] = attention_plan(16, lambda h: heads64(q, h), lambda h: heads64(k, h),
                                        lambda h, kt: v[:, kt, 64 * h:64 * h + 64],
                                        lambda h, t: bank[2 * t + h // 8][:, 64 * (h % 8):64 * (h % 8) + 64], reversed_bias, h0, bias=True)
                h0 += 16
                w = a["odd_w_in_2"][0]
                ph["units"] = ([(w, UC * i, UC, ("c", q[:, 2 * i:2 * i + 2, :], 0.125)) for i in range(4)]
                               + [(w, D + UC * i, UC, ("c", k[:, 2 * i:2 * i + 2, :])) for i in range(4)]
                               + [(w, 2 * D + UC * i, UC, ("v", v[:, :, UC * i:UC * (i + 1)])) for i in range(4)])
                ph["w_out"] = a["odd_w_out_2"][0]
            ph["views"] = V

        raw_in = [sem(f"raw_in{i}") for i in range(RAWS)]
        setup_in = [sem(f"setup_in{i}") for i in range(3)]
        x_in = [sem(f"x_in{t}") for t in range(T)]
        ident_in = sem("ident_in")
        summed0 = sem("summed0")
        yg_done = sem("yg_done")
        glu_ok = sem("glu_ok")
        pool_step = sem("pool_step")
        conv_pool_ok = sem("conv_pool_ok")
        spread_ok = sem("spread_ok")
        halves_out = sem("halves_out")
        diff_ok = sem("diff_ok")
        hi_done = sem("hi_done")
        lo_done = sem("lo_done")
        unit_used = sem("unit_used")
        consts_set = sem("consts_set")
        params_T = sem("params_T")
        params_ok = sem("params_ok")
        x_ready = sem("x_ready")
        sq_done = sem("sq_done")
        ms_ready = sem("ms_ready")
        rstd_ready = sem("rstd_ready")
        xn_ready = sem("xn_ready")
        x_T = sem("x_T")
        t_hi_ok = sem("t_hi_ok")
        t_lo_ok = sem("t_lo_ok")
        silu_done = sem("silu_done")
        prod_done = sem("prod_done")
        prodhi_done = sem("prodhi_done")
        prodlo_done = sem("prodlo_done")
        grow_in = sem("grow_in")
        dve_step = sem("dve_step")
        act_step = sem("act_step")
        bank_free = [sem(f"bank_free{i}") for i in range(4)]
        roped = sem("roped")
        rope_T = sem("rope_T")
        rope_kept = sem("rope_kept")
        v_kept = sem("v_kept")
        sig_ok = sem("sig_ok")
        conv_ok = sem("conv_ok")
        mean_ok = sem("mean_ok")
        cen_ok = sem("cen_ok")
        sq4_ok = sem("sq4_ok")
        var_ok = sem("var_ok")
        z_ok = sem("z_ok")
        swish_ok = sem("swish_ok")
        qsq_ok = sem("qsq_ok")
        s_done = sem("s_done")
        nmax_ok = sem("nmax_ok")
        p_done = sem("p_done")
        pt_done = sem("pt_done")
        pt_kept = sem("pt_kept")
        o_done = sem("o_done")
        o_ready = sem("o_ready")
        o_T = sem("o_T")
        idx_done = sem("idx_done")
        idx_relu = sem("idx_relu")
        idx_added = sem("idx_added")
        bias_in = [sem(f"bias_in{i}") for i in range(3)]
        bias_set = sem("bias_set")
        lam_sum = sem("lam_sum")
        lam_exp = sem("lam_exp")
        out_done = sem("out_done")

        n_units = n_ffn = n_rope = n_rstd = 0
        widths = {}
        uses = [0] * 4
        for ph in phases:
            ph["n0"] = n_units
            if ph["kind"] == "ffn":
                ph["f"] = n_ffn
                n_ffn += 1
                n_units += 3 * CHUNKS
            elif ph["kind"] == "mix":
                ph["r0"] = n_rope
                n_rope += sum(u[3][0] in ("rope", "tail") for u in ph["units"])
                ph["left"] = []
                for j, u in enumerate(ph["units"]):
                    widths[n_units + j] = u[2]
                    uses[j % 4] += 1
                    ph["left"].append(uses[j % 4])
                n_units += len(ph["units"]) + 4
            ph["after"] = n_units
            n_rstd += {"edge": T * (ph.get("take") == "post") + T * (ph.get("g") is not None), "ffn": 0,
                       "mix": {"first": 5, "even": 1}.get(ph.get("which"), 0)}[ph["kind"]]
            ph["rstd"] = n_rstd
        N_UNITS = n_units
        GLU_B, DW_B, LN_G, LN_B = 64, 72, 76, 80

        def idx_bank(ph, h):
            return 4 + (ph["r0"] + h // 2 + 3 + h % 2) % 4

        def col_src(w, c0, nc_=UC):
            return w.rearrange("(k p) n -> p k n", p=P)[:, :, bass.ds(c0, nc_)]

        def row_src(w, r0):
            return w[bass.ds(r0, UC), :].rearrange("(r p) n -> p r n", p=P)

        def raw_view(n, w, by_rows=False):
            v = raw[:, n % RAWS, 0:KT * w]
            return v.rearrange("p (r n) -> p r n", r=2) if by_rows else v.rearrange("p (k n) -> p k n", k=KT)

        block = stack.enter_context(nc.Block())

        @block.sync
        def _(sp):
            def load(n, src, width=UC, by_rows=False, turn=0):
                if n >= RAWS:
                    sp.wait_ge(lo_done, n - RAWS + 1 + SLOTS * turn)
                sp.dma_start(raw_view(n, width, by_rows), src).then_inc(raw_in[n % RAWS], 16)

            for t in range(T):
                sp.dma_start(x_sb[:, t, :], a["x"][0, t * P:(t + 1) * P, :]).then_inc(x_in[t], 16)
            for ph in phases:
                n = ph["n0"]
                if ph["kind"] == "mix":
                    for w, c0, width, _ in ph["units"]:
                        load(n, col_src(w, c0, width), width)
                        n += 1
                    for r in range(4):
                        load(n, row_src(ph["w_out"], r * UC), by_rows=True)
                        n += 1
                elif ph["kind"] == "ffn":
                    load(n, col_src(ph["wg"], 0))
                    load(n + 1, col_src(ph["wu"], 0))
                    with sp.Fori(0, CHUNKS // 2) as i:
                        for j in range(2):
                            m = n + 2 + 3 * j
                            c0 = i * (2 * UC) + (1 + j) * UC
                            load(m, col_src(ph["wg"], c0), turn=i)
                            load(m + 1, col_src(ph["wu"], c0), turn=i)
                            load(m + 2, row_src(ph["wd"], i * (2 * UC) + j * UC), by_rows=True, turn=i)
                    load(n + 3 * CHUNKS - 1, row_src(ph["wd"], FF - UC), by_rows=True)
            sp.wait_ge(out_done, 16 * T)

        @block.scalar
        def _(act):
            seen = {}

            def nx(s, k=1):
                seen[id(s)] = seen.get(id(s), 0) + k
                return seen[id(s)]

            cur = [0]

            def split_hi(n, width=UC, turn=0):
                act.wait_ge(raw_in[n % RAWS], 16 * (n // RAWS + 1) + turn * (16 * SLOTS // RAWS))
                if n >= SLOTS:
                    act.wait_ge(unit_used, n - SLOTS + 1 + turn * SLOTS)
                w = KT * width
                nc.scalar.activation(w_hi[:, n % SLOTS, 0:w], raw[:, n % RAWS, 0:w], ACT.Copy).then_inc(hi_done, 1)

            def split_to(n):
                while cur[0] < min(n, N_UNITS):
                    split_hi(cur[0], widths.get(cur[0], UC))
                    cur[0] += 1

            def edge(ph):
                if ph["take"] == "post":
                    for i in range(2 * T):
                        if i % 2:
                            act.wait_ge(yg_done, nx(yg_done, 2) - 1)
                        elif i == 0:
                            act.wait_ge(summed0, nx(summed0))
                        else:
                            act.wait_ge(unit_used, ph["after"])
                        nc.scalar.activation(junk[:, i // 2, (i % 2) * 512:(i % 2 + 1) * 512], bank[i], ACT.Square,
                                             accum_out=st[:, 4 + i:5 + i]).then_inc(sq_done, 1)
                        nx(sq_done)
                elif ph["take"] == "add":
                    nx(summed0)
                if ph["g"] is None:
                    for t in range(T):
                        act.wait_ge(x_ready, nx(x_ready))
                        act.dma_start(out[0, t * P:(t + 1) * P, :], x_sb[:, t, :]).then_inc(out_done, 16)
                    return
                for t in range(T):
                    if ph["take"] == "input":
                        act.wait_ge(x_in[t], 16)
                    else:
                        act.wait_ge(x_ready, nx(x_ready))
                    if ph["take"] == "post":
                        act.wait_ge(sq_done, seen[id(sq_done)] - 3)
                    nc.scalar.activation(junk[:, t, :], x_sb[:, t, :], ACT.Square, accum_out=st[:, t:t + 1]).then_inc(sq_done, 1)
                    nx(sq_done)
                if ph["take"] == "input":
                    split_to(1)
                    act.wait_ge(params_T, 2)
                    nc.scalar.activation(p_col[:, :], bank[0][:, 0:P], ACT.Copy).then_inc(params_ok, 1)
                    nc.scalar.activation(tap_col[:, :], bank[1][:, 0:P], ACT.Copy).then_inc(params_ok, 1)
                    act.wait_ge(params_ok, 2)
                for k in range(KT):
                    if k % 2 == 0:
                        act.wait_ge(x_T, nx(x_T))
                    g = ph["g"] * KT + k
                    nc.scalar.activation(t_hi[:, k, :], bank[4 + k // 2][:, (k % 2) * S:(k % 2 + 1) * S], ACT.Copy,
                                         scale=p_col[:, g:g + 1]).then_inc(t_hi_ok, 1)

            def ffn(ph):
                n0 = ph["n0"]

                def chunk(s, c, turn=0):
                    act.wait_ge(unit_used, s + 1 + turn * SLOTS)
                    nc.scalar.activation(f_s[:, c % 2, :], bank[4 + 2 * (c % 2)][:, :], ACT.Silu).then_inc(silu_done, 1)
                    act.wait_ge(prod_done, 1 + CHUNKS * ph["f"] + c + 1 + turn * 2)
                    nc.scalar.activation(f_hi[:, c % 2, :], f_p[:, c % 2, :], ACT.Copy).then_inc(prodhi_done, 1)

                split_to(n0 + 5)
                chunk(n0, 0)
                whole = CHUNKS // 2 if ph["n0"] + 3 * CHUNKS < N_UNITS else CHUNKS // 2 - 1
                with act.Fori(0, whole) as i:
                    for j in range(2):
                        for u in range(3):
                            split_hi(n0 + 5 + 3 * j + u, turn=i)
                        chunk(n0 + 2 + 3 * j, 1 + j, turn=i)
                cur[0] = n0 + 5 + 6 * whole
                for c in range(1 + 2 * whole, CHUNKS):
                    split_to(n0 + 3 * c + 5)
                    chunk(n0 + 3 * c - 1, c)

            def keep_rope(role):
                r = nx(rope_T) - 1
                act.wait_ge(rope_T, r + 1)
                n = S if role[0] == "tail" else 2 * S
                src = bank[4 + r % 4][:, 0:n]
                if role[0] != "tail":
                    src = src.rearrange("p (a s) -> p a s", a=2)
                nc.scalar.activation(role[2], src, ACT.Copy).then_inc(rope_kept, 1)

            def keep_unit(ph, j):
                act.wait_ge(unit_used, ph["n0"] + j + 1)
                nc.scalar.activation(ph["units"][j][3][1], bank[j % 4][:, :].rearrange("p (a s) -> p a s", a=2), ACT.Copy,
                                     scale=(ph["units"][j][3] + (1.0,))[2])\
                    .then_inc(bank_free[j % 4], 1)

            def keep_pt(L, h):
                act.wait_ge(pt_done, L["h0"] + h + 1)
                if h >= 2:
                    act.wait_ge(o_done, L["h0"] + h - 1)
                nc.scalar.activation(pt_buf[:, h % 2, :], bank[6 + h % 2][:, 0:384], ACT.Copy).then_inc(pt_kept, 1)

            def attention(L, hooks={}):
                for h in range(L["heads"]):
                    act.wait_ge(nmax_ok, L["h0"] + h + 1)
                    if h >= 2:
                        act.wait_ge(pt_done, L["h0"] + h - 1)
                    for t, (lo, hi) in enumerate(((0, 128), (128, 384))):
                        c = 2 * h + t
                        nc.scalar.activation(p_buf[:, h % 2, lo:hi], s_buf[:, h % 2, lo:hi], ACT.Exp, scale=L["scale"],
                                             bias=L["nmax"][:, c:c + 1], accum_out=L["sum"][:, c:c + 1]).then_inc(p_done, 1)
                    if h >= 1:
                        keep_pt(L, h - 1)
                    if h in hooks:
                        hooks[h]()
                keep_pt(L, L["heads"] - 1)

            def out_hi(banks):
                for j, b in enumerate(banks):
                    act.wait_ge(o_T, nx(o_T))
                    nc.scalar.activation(t_hi[:, 2 * j:2 * j + 2, :], bank[b][:, :].rearrange("p (a s) -> p a s", a=2),
                                         ACT.Copy).then_inc(t_hi_ok, 1)

            def project(ph):
                roped_before = None
                for j, (_, _, _, role) in enumerate(ph["units"]):
                    m = ph["n0"] + j
                    split_to(m + LEAD)
                    if role[0] in "vc":
                        if ph["which"] == "even":
                            act.wait_ge(idx_added, 16)
                        keep_unit(ph, j)
                    elif role[0] == "glu_g":
                        act.wait_ge(unit_used, m + 1)
                        for c in range(2):
                            ct = 2 * role[1] + c
                            ins = nc.scalar.activation(ph["views"]["sig"][:, ct, :], bank[j % 4][:, c * S:(c + 1) * S], ACT.Sigmoid,
                                                       bias=p_col[:, GLU_B + 4 + ct:GLU_B + 5 + ct])
                        ins.then_inc(bank_free[j % 4], 1)
                    elif role[0] == "rope" and ph["which"] == "first":
                        act.wait_ge(unit_used, m + 1)
                        r = seen.get(id(rope_T), 0) + (roped_before is not None)
                        if r:
                            act.wait_ge(roped, r)
                        nc.scalar.activation(qsq, bank[j % 4][:, :], ACT.Square).then_inc(qsq_ok, 1)
                    if ph["which"] == "even" and 4 <= j < 8:
                        for h in (2 * j - 8, 2 * j - 7):
                            act.wait_ge(idx_done, h + 1)
                            if h >= 4:
                                act.wait_ge(idx_added, 2 * (h - 3))
                            nc.scalar.activation(ph["views"]["rel"][:, h % 4, :], bank[idx_bank(ph, h)][:, 0:384], ACT.Relu)\
                                .then_inc(idx_relu, 1)
                    if roped_before:
                        keep_rope(roped_before)
                    roped_before = role if role[0] in ("rope", "tail") else None

            def mix_first(ph):
                V = ph["views"]
                project(ph)

                def squares():
                    act.wait_ge(cen_ok, 1)
                    nc.scalar.activation(V["sq"], V["cen"], ACT.Square).then_inc(sq4_ok, 1)

                attention(V["L"], {6: squares})
                out_hi((6, 7))
                act.wait_ge(z_ok, 1)
                for ct in range(4):
                    nc.scalar.activation(V["sw"][:, ct, :], V["z"][:, ct, :], ACT.Silu, scale=p_col[:, LN_G + ct:LN_G + ct + 1],
                                         bias=p_col[:, LN_B + ct:LN_B + ct + 1]).then_inc(swish_ok, 1)
                act.wait_ge(swish_ok, 4)
                nc.scalar.activation(t_hi[:, 4:8, :], V["sw"], ACT.Copy).then_inc(t_hi_ok, 1)
                split_to(ph["after"] + 2)

            def mix_even(ph):
                V = ph["views"]
                project(ph)

                def squares():
                    act.wait_ge(diff_ok, 1)
                    nc.scalar.activation(V["osq"], V["oa"], ACT.Square).then_inc(qsq_ok, 1)

                attention(V["L"], {11: squares})
                out_hi((4, 5, 6, 7))
                split_to(ph["after"] + 2)

            def mix_odd(ph):
                project(ph)
                attention(ph["views"]["L"])
                out_hi((4, 5, 6, 7))
                split_to(ph["after"] + 2)

            act.dma_start(ident[:, :], a["ident_tab"]).then_inc(ident_in, 16)
            act.wait_ge(consts_set, 1)
            for src, r0, nr in a["param_rows"]:
                act.dma_start(p_rows[r0:r0 + nr, :], src).then_inc(setup_in[0], 16)
            act.dma_start(w_rows[0:4 * TAPS, :], a["dw_w"][0].rearrange("t (c p) -> (t c) p", p=P)).then_inc(setup_in[0], 16)
            for ph in phases:
                if ph["kind"] == "edge":
                    edge(ph)
                    if ph["take"] == "input":
                        split_to(LEAD)
                        act.wait_ge(lam_sum, 1)
                        nc.scalar.activation(st[:, 22:24], st[:, 20:22], ACT.Exp).then_inc(lam_exp, 1)
                elif ph["kind"] == "ffn":
                    ffn(ph)
                elif ph["kind"] == "mix":
                    {"first": mix_first, "even": mix_even, "odd": mix_odd}[ph["which"]](ph)
        @block.gpsimd
        def _(pool):
            seen = {}

            def nx(s, k=1):
                seen[id(s)] = seen.get(id(s), 0) + k
                return seen[id(s)]

            nc.gpsimd.memset(ws[:, 9216:9472], 0.0).then_inc(consts_set, 1)
            nc.gpsimd.memset(minus_half[:, :], -0.5).then_inc(consts_set, 1)
            nc.gpsimd.memset(mean_w[:, :], 1.0 / HW).then_inc(consts_set, 1)
            pool.wait_ge(consts_set, 3)
            pool.dma_start(rope[:, :, :], a["rope_tab"].rearrange("(t p) c -> p t c", p=P)).then_inc(setup_in[1], 16)
            for i, name in enumerate(("q_norm_g", "k_norm_g")):
                pool.dma_start(qk_g[:, i, :], a[name][0, :].partition_broadcast(P)).then_inc(setup_in[1], 16)
            pool.dma_start(lam_in, a["even_lambda_2"][0].rearrange("a b -> (a b)").partition_broadcast(P)).then_inc(setup_in[1], 16)
            pool.dma_start(masks[:, :], a["mask_tab"]).then_inc(setup_in[1], 16)
            pool.dma_start(subln[:, :], a["even_subln_2"][0, :].partition_broadcast(P)).then_inc(setup_in[1], 16)

            def inv_root(v):
                pool.wait_ge(ms_ready, nx(ms_ready))
                nc.gpsimd.tensor_tensor(v, v, minus_half[:, 0:1].broadcast_to([P, v.shape[1]]), ALU.pow).then_inc(rstd_ready, 1)

            posts = [ph for ph in phases if ph.get("take") == "post"]
            if posts:
                pool.dma_start(g_row[:, :], posts[0]["row"].partition_broadcast(P)).then_inc(grow_in, 16)
            n_post = 0
            for ph in phases:
                if ph["kind"] == "edge":
                    if ph["take"] == "post":
                        for t in range(T):
                            inv_root(st[:, 8 + t:9 + t])
                    if ph["g"] is not None:
                        for t in range(T):
                            inv_root(st[:, 2 + t:3 + t])
                    if ph["take"] == "post":
                        n_post += 1
                        if n_post < len(posts):
                            pool.wait_ge(yg_done, 2 * T * n_post)
                            pool.dma_start(g_row[:, :], posts[n_post]["row"].partition_broadcast(P)).then_inc(grow_in, 16)
                elif ph["kind"] == "mix" and ph["which"] == "first":
                    V = ph["views"]
                    done = [0]

                    def taps(n):
                        for tap in range(done[0], min(TAPS, done[0] + n)):
                            src, acc = V["hpad"][:, 3, tap:tap + S], V["acc"][:, 3, :]
                            w = tap_col[:, 4 * tap + 3:4 * tap + 4]
                            if tap == 0:
                                nc.gpsimd.tensor_scalar(acc, src, w, p_col[:, DW_B + 3:DW_B + 4], ALU.mult, ALU.add).then_inc(pool_step, 1)
                                continue
                            if tap >= 3:
                                pool.wait_ge(pool_step, 2 * tap - 3)
                            nc.gpsimd.tensor_scalar(V["product"][:, tap % 2, :], src, w, None, ALU.mult).then_inc(pool_step, 1)
                            pool.wait_ge(pool_step, 2 * tap)
                            nc.gpsimd.tensor_tensor(acc, acc, V["product"][:, tap % 2, :], ALU.add)\
                                .then_inc(pool_step if tap < TAPS - 1 else conv_pool_ok, 1)
                        done[0] = min(TAPS, done[0] + n)

                    pool.wait_ge(bank_free[3], ph["left"][3])
                    taps(3)
                    for r in range(4):
                        inv_root(st[:, 32 + 8 * (r % 2):40 + 8 * (r % 2)])
                        taps(4)
                    taps(TAPS)
                    inv_root(st[:, 10:12])
                elif ph["kind"] == "mix" and ph["which"] == "even":
                    inv_root(st[:, 32:40])
                elif ph["kind"] == "mix":
                    bias, L = ph["views"]["bias"], ph["views"]["L"]
                    for lo in (0, 128):
                        nc.gpsimd.memset(bias[0:64, :, lo:lo + 64], NEG).then_inc(bias_set, 1)
                    for h in range(16):
                        if h >= 3:
                            pool.wait_ge(nmax_ok, L["h0"] + h - 2)
                        for c in range(4):
                            row = a["odd_rel_bias_2"][0, h, 0:1]
                            src = bass.AP(row.tensor, row.offset, [[1, 64], [1, 64 * (c + 1)]])
                            end = (128, 384)[c // 2]
                            pool.dma_start(bias[64 * (c % 2):64 * (c % 2) + 64, h % 3, end - 64 * (c + 1):end], src)\
                                .then_inc(bias_in[h % 3], 16)

        @block.tensor
        def _(pe):
            seen = {}

            def nx(s, k=1):
                seen[id(s)] = seen.get(id(s), 0) + k
                return seen[id(s)]

            def three(o, lh, ll, rh, rl, start, stop):
                nc.tensor.matmul(o, lh, rh, start=start, stop=False)
                nc.tensor.matmul(o, lh, rl, start=False, stop=False)
                return nc.tensor.matmul(o, ll, rh, start=False, stop=stop)

            def w_cols(n, width=UC):
                v = [w[:, n % SLOTS, 0:KT * width].rearrange("p (k n) -> p k n", k=KT) for w in (w_hi, w_lo)]
                return v

            fresh = [None]

            def rows_ready(k, first, b=0):
                if first and fresh[0] is not None:
                    pe.wait_ge(t_lo_ok, fresh[0] + (2 if b == 4 and k == 0 else k + 1))
                    if k == KT - 1:
                        fresh[0] = None

            def by_channels(n, b, turn=0):
                pe.wait_ge(lo_done, n + 1 + turn * SLOTS)
                wh, wl = w_cols(n)
                for c in range(2):
                    for k in range(KT):
                        rows_ready(k, c == 0, b)
                        mm = three(bank[b][:, c * S:(c + 1) * S], wh[:, k, c * P:(c + 1) * P], wl[:, k, c * P:(c + 1) * P],
                                   t_hi[:, k, :], t_lo[:, k, :], k == 0, k == KT - 1)
                mm.then_inc(unit_used, 1)

            def by_tokens(n, b, width=UC):
                pe.wait_ge(lo_done, n + 1)
                wh, wl = w_cols(n, width)
                for t in range(T):
                    for k in range(KT):
                        rows_ready(k, t == 0)
                        mm = three(bank[b][:, t * UC:t * UC + width], t_hi[:, k, t * P:(t + 1) * P], t_lo[:, k, t * P:(t + 1) * P],
                                   wh[:, k, :], wl[:, k, :], k == 0, k == KT - 1)
                mm.then_inc(unit_used, 1)

            def by_rows(n, lh, ll, first=False, last=False, turn=0):
                pe.wait_ge(lo_done, n + 1 + turn * SLOTS)
                wh, wl = [w[:, n % SLOTS, :].rearrange("p (r n) -> p r n", r=2) for w in (w_hi, w_lo)]
                for r, t in (((0, 0), (1, 0), (0, 1), (1, 1)) if last else ((0, 0), (0, 1), (1, 0), (1, 1))):
                    for h in range(2):
                        mm = three(bank[2 * t + h][:, :], lh(r, t), ll(r, t), wh[:, r, h * 512:(h + 1) * 512],
                                   wl[:, r, h * 512:(h + 1) * 512], first and r == 0, last and r == 1)
                    if last and (r, t) == (1, 0):
                        mm.then_inc(summed0, 1)
                mm.then_inc(unit_used, 1)

            def edge(ph):
                if ph["g"] is None:
                    return
                if ph["take"] == "input":
                    pe.wait_ge(ident_in, 16)
                    pe.wait_ge(setup_in[0], 16 * (len(a["param_rows"]) + 1))
                    nc.tensor.transpose(bank[0][:, 0:P], p_rows, ident[:, :]).then_inc(params_T, 1)
                    nc.tensor.transpose(bank[1][:, 0:P], w_rows, ident[:, :]).then_inc(params_T, 1)
                for t in range(T):
                    pe.wait_ge(xn_ready, nx(xn_ready))
                    for k in range(KT):
                        mm = nc.tensor.transpose(bank[4 + k // 2][:, (k % 2) * S + t * P:(k % 2) * S + (t + 1) * P],
                                                 xn[:, t, k * P:(k + 1) * P], ident[:, :])
                        if t == 1 and k % 2 == 1:
                            mm.then_inc(x_T, 1)
                fresh[0] = seen.get(id(t_lo_ok), 0)
                nx(t_lo_ok, KT)

            def ffn(ph):
                n0, c0 = ph["n0"], CHUNKS * ph["f"]
                for b in range(4):
                    for h in range(2):
                        nc.tensor.matmul(bank[b][:, h * 256:(h + 1) * 256], zero_r[:, 0:P], zero_r[:, :], start=h == 0, stop=False)

                def down(n, c, turn=0, last=False):
                    pe.wait_ge(prodlo_done, c0 + c + 1 + turn * 2)
                    by_rows(n, lambda r, t: f_hi[:, c % 2, r * S + t * P:r * S + (t + 1) * P],
                            lambda r, t: f_lo[:, c % 2, r * S + t * P:r * S + (t + 1) * P], turn=turn, last=last)

                by_channels(n0, 4)
                by_channels(n0 + 1, 5)
                with pe.Fori(0, CHUNKS // 2) as i:
                    for j in range(2):
                        b = 4 + 2 * ((1 + j) % 2)
                        pe.wait_ge(prod_done, 1 + c0 + j + i * 2)
                        by_channels(n0 + 2 + 3 * j, b, i)
                        by_channels(n0 + 3 + 3 * j, b + 1, i)
                        down(n0 + 4 + 3 * j, j, i)
                down(n0 + 3 * CHUNKS - 1, CHUNKS - 1, last=True)

            idx_sent = [0]

            def turn_rope(role):
                r = nx(roped) - 1
                pe.wait_ge(roped, r + 1)
                if r >= 4:
                    pe.wait_ge(rope_kept, r - 3)
                if idx_sent[0]:
                    pe.wait_ge(idx_relu, idx_sent[0])
                for p in range(1 if role[0] == "tail" else 2):
                    for t in range(T):
                        mm = nc.tensor.transpose(bank[4 + r % 4][:, p * S + t * P:p * S + (t + 1) * P],
                                                 qr[:, r % 2, t, p * P:(p + 1) * P], ident[:, :])
                mm.then_inc(rope_T, 1)

            def project(ph):
                before = None
                for j, (_, _, width, role) in enumerate(ph["units"]):
                    if ph["left"][j] > 1:
                        pe.wait_ge(bank_free[j % 4], ph["left"][j] - 1)
                    if role[0] in ("glu_g", "glu_a", "c"):
                        by_channels(ph["n0"] + j, j % 4)
                    else:
                        by_tokens(ph["n0"] + j, j % 4, width)
                    if before:
                        turn_rope(before)
                    before = role if role[0] in ("rope", "tail") else None
                    if ph["which"] == "even" and 3 <= j < 7:
                        V = ph["views"]
                        pe.wait_ge(rope_kept, ph["r0"] + max(j - 2, 2))
                        for h in (2 * j - 6, 2 * j - 5):
                            q = V["iq"][32 * (h % 4):32 * (h % 4) + 32, h // 4, :]
                            k = V["ik"][32 * (h % 4):32 * (h % 4) + 32, :]
                            o = bank[idx_bank(ph, h)]
                            nc.tensor.matmul(o[:, 0:128], q[:, 0:128], k[:, 0:128], start=True, stop=True)
                            nc.tensor.matmul(o[:, 128:384], q[:, 128:256], k, start=True, stop=True).then_inc(idx_done, 1)
                            idx_sent[0] += 1
                for j in range(len(ph["units"]) - 4, len(ph["units"])):
                    pe.wait_ge(bank_free[j % 4], ph["left"][j])
                if id(roped) in seen:
                    pe.wait_ge(rope_kept, seen[id(roped)])

            def attention(L, hooks={}):
                H = L["heads"]

                def scores(h):
                    if h >= 2:
                        pe.wait_ge(nmax_ok, L["h0"] + h - 1)
                    b = bank[4 + h % 2]
                    q, k = L["q"](h), L["k"](h)
                    nc.tensor.matmul(b[:, 0:128], q[:, 0:128], k[:, 0:128], start=True, stop=True)
                    nc.tensor.matmul(b[:, 128:384], q[:, 128:256], k[:, 0:256], start=True, stop=True).then_inc(s_done, 1)

                def turn(h):
                    pe.wait_ge(p_done, 2 * (L["h0"] + h + 1))
                    if h >= 2:
                        pe.wait_ge(pt_kept, L["h0"] + h - 1)
                    for i in range(3):
                        mm = nc.tensor.transpose(bank[6 + h % 2][:, i * P:(i + 1) * P], p_buf[:, h % 2, i * P:(i + 1) * P], ident[:, :])
                    mm.then_inc(pt_done, 1)

                def values(h):
                    pe.wait_ge(pt_kept, L["h0"] + h + 1)
                    if L["heads"] == 16 and not L["bias"] and h == 8:
                        pe.wait_ge(halves_out, 1)
                    pt = pt_buf
                    o0, o1 = L["o"](h, 0), L["o"](h, 1)
                    nc.tensor.matmul(o0, pt[:, h % 2, 0:128], L["v"](h, 0), start=True, stop=True)
                    nc.tensor.matmul(o1, pt[:, h % 2, 128:256], L["v"](h, 0), start=True, stop=False)
                    nc.tensor.matmul(o1, pt[:, h % 2, 256:384], L["v"](h, 1), start=False, stop=True).then_inc(o_done, 1)

                for h in range(H + 2):
                    if h < H:
                        scores(h)
                    if 1 <= h <= H:
                        turn(h - 1)
                    if h >= 2:
                        values(h - 2)
                    if h in hooks:
                        hooks[h]()

            def out_turn(src, banks):
                for j, b in enumerate(banks):
                    for c in range(2):
                        for t in range(T):
                            mm = nc.tensor.transpose(bank[b][:, c * S + t * P:c * S + (t + 1) * P], src(2 * j + c, t), ident[:, :])
                    mm.then_inc(o_T, 1)

            def out_proj(ph, parts=(1, 1, 1, 1)):
                n = ph["n0"] + len(ph["units"])
                for u in range(4):
                    if parts[u]:
                        pe.wait_ge(t_lo_ok, nx(t_lo_ok))
                    by_rows(n + u, lambda r, t: t_hi[:, 2 * u + r, t * P:(t + 1) * P],
                            lambda r, t: t_lo[:, 2 * u + r, t * P:(t + 1) * P], first=u == 0, last=u == 3)

            def mix_first(ph):
                V = ph["views"]
                project(ph)

                def mean():
                    pe.wait_ge(conv_ok, 3)
                    pe.wait_ge(conv_pool_ok, 1)
                    for ct in range(4):
                        mm = nc.tensor.matmul(bank[2][:, 0:S], mean_w[:, :], V["acc"][:, ct, :], start=ct == 0, stop=ct == 3)
                    mm.then_inc(mean_ok, 1)

                def variance():
                    pe.wait_ge(sq4_ok, 1)
                    for t in range(T):
                        for ct in range(4):
                            mm = nc.tensor.matmul(bank[3][:, t:t + 1], V["sq"][:, ct, t * P:(t + 1) * P], mean_w[:, 0:1],
                                                  start=ct == 0, stop=ct == 3)
                    mm.then_inc(var_ok, 1)

                def spread():
                    pe.wait_ge(rstd_ready, ph["rstd"])
                    for t in range(T):
                        mm = nc.tensor.matmul(bank[2][:, t * P:(t + 1) * P], st[:, 10 + t:11 + t].broadcast_to([P, P]), ident[:, :],
                                              start=True, stop=True)
                    mm.then_inc(spread_ok, 1)

                attention(V["L"], {5: mean, 8: variance})
                spread()
                pe.wait_ge(o_ready, nx(o_ready))
                out_turn(lambda k, t: V["o"][:, t, k * P:(k + 1) * P], (6, 7))
                out_proj(ph, (1, 1, 1, 0))

            def mix_even(ph):
                V = ph["views"]
                project(ph)
                attention(V["L"])
                for o, banks in ((V["oa"], (4, 5)), (V["ob"], (6, 7))):
                    pe.wait_ge(o_ready, nx(o_ready))
                    out_turn(lambda k, t: o[:, t, k * P:(k + 1) * P], banks)
                out_proj(ph)

            def mix_odd(ph):
                V = ph["views"]
                project(ph)
                attention(V["L"])
                pe.wait_ge(o_ready, nx(o_ready))
                out_turn(lambda k, t: V["o"][:, t, k * P:(k + 1) * P], (4, 5, 6, 7))
                out_proj(ph)

            pe.wait_ge(dve_step, 1)
            for ph in phases:
                if ph["kind"] == "edge":
                    edge(ph)
                elif ph["kind"] == "ffn":
                    ffn(ph)
                elif ph["kind"] == "mix":
                    {"first": mix_first, "even": mix_even, "odd": mix_odd}[ph["which"]](ph)

        @block.vector
        def _(dve):
            seen = {}

            def nx(s, k=1):
                seen[id(s)] = seen.get(id(s), 0) + k
                return seen[id(s)]

            steps = [0]

            def step(ins):
                steps[0] += 1
                ins.then_inc(dve_step, 1)
                return steps[0]

            def link(ins):
                dve.wait_ge(dve_step, step(ins))

            cur = [0]

            def split_lo(n, width=UC, turn=0):
                dve.wait_ge(hi_done, n + 1 + turn * SLOTS)
                w = KT * width
                nc.vector.tensor_tensor(w_lo[:, n % SLOTS, 0:w], raw[:, n % RAWS, 0:w], w_hi[:, n % SLOTS, 0:w].bitcast(F32),
                                        ALU.subtract).then_inc(lo_done, 1)

            def split_to(n):
                while cur[0] < min(n, N_UNITS):
                    split_lo(cur[0], widths.get(cur[0], UC))
                    cur[0] += 1

            def edge(ph):
                take = ph["take"]

                def xv(t):
                    return x_sb[:, t, :]

                if take == "add":
                    nx(summed0)
                    for t in range(T):
                        if t == 0:
                            dve.wait_ge(summed0, seen[id(summed0)])
                        else:
                            dve.wait_ge(unit_used, ph["after"])
                        nc.vector.tensor_tensor(xv(t), psum[:, 2 * t:2 * t + 2, :].rearrange("p a b -> p (a b)"), xv(t), ALU.add)\
                            .then_inc(x_ready, 1)
                elif take == "post":
                    dve.wait_ge(grow_in, nx(grow_in, 16))
                    for t in range(T):
                        if t == 0:
                            dve.wait_ge(summed0, nx(summed0))
                        else:
                            dve.wait_ge(unit_used, ph["after"])
                        for h in (1, 0):
                            if h == 0:
                                dve.wait_ge(sq_done, nx(sq_done))
                            hv = slice(h * 512, (h + 1) * 512)
                            nc.vector.scalar_tensor_tensor(out=yg[:, t, hv], in0=bank[2 * t + h], scalar=ph["scale"] * D ** 0.5,
                                                           in1=g_row[:, hv], op0=ALU.mult, op1=ALU.mult).then_inc(yg_done, 1)
                        dve.wait_ge(sq_done, nx(sq_done))
                        nc.vector.tensor_scalar(st[:, 8 + t:9 + t], st[:, 4 + 2 * t:5 + 2 * t], st[:, 5 + 2 * t:6 + 2 * t], D * EPS,
                                                ALU.add, ALU.add).then_inc(ms_ready, 1)
                        if t == 0:
                            n_yg = nx(yg_done, 2 * T)
                    for t in range(T):
                        dve.wait_ge(rstd_ready, nx(rstd_ready))
                        dve.wait_ge(yg_done, n_yg - 2 * (T - 1 - t))
                        nc.vector.scalar_tensor_tensor(out=xv(t), in0=yg[:, t, :], scalar=st[:, 8 + t:9 + t], in1=xv(t),
                                                       op0=ALU.mult, op1=ALU.add).then_inc(x_ready, 1)
                if ph["g"] is None:
                    return
                for t in range(T):
                    if take == "input":
                        dve.wait_ge(x_in[t], 16)
                    dve.wait_ge(sq_done, nx(sq_done))
                    nc.vector.tensor_scalar(st[:, 2 + t:3 + t], st[:, t:t + 1], D * EPS, None, ALU.add).then_inc(ms_ready, 1)
                    dve.wait_ge(rstd_ready, nx(rstd_ready))
                    nc.vector.tensor_scalar(xn[:, t, :], xv(t), st[:, 2 + t:3 + t], D ** 0.5, ALU.mult, ALU.mult).then_inc(xn_ready, 1)
                if take == "input":
                    split_to(1)
                    dve.wait_ge(params_ok, 2)
                for k in range(KT):
                    if k % 2 == 0:
                        dve.wait_ge(t_hi_ok, nx(t_hi_ok, 2))
                    g = ph["g"] * KT + k
                    nc.vector.scalar_tensor_tensor(out=t_lo[:, k, :], in0=bank[4 + k // 2][:, (k % 2) * S:(k % 2 + 1) * S],
                                                   scalar=p_col[:, g:g + 1], in1=t_hi[:, k, :].bitcast(F32),
                                                   op0=ALU.mult, op1=ALU.subtract).then_inc(t_lo_ok, 1)

            def ffn(ph):
                n0, c0 = ph["n0"], CHUNKS * ph["f"]

                def chunk(s, c, turn=0):
                    b = c % 2
                    dve.wait_ge(silu_done, c0 + c + 1 + turn * 2)
                    dve.wait_ge(unit_used, s + 1 + turn * SLOTS)
                    nc.vector.tensor_tensor(f_p[:, b, :], bank[5 + 2 * b][:, :], f_s[:, b, :], ALU.mult).then_inc(prod_done, 1)
                    dve.wait_ge(prodhi_done, c0 + c + 1 + turn * 2)
                    nc.vector.tensor_tensor(f_lo[:, b, :], f_p[:, b, :], f_hi[:, b, :].bitcast(F32), ALU.subtract)\
                        .then_inc(prodlo_done, 1)

                split_to(n0 + 5)
                chunk(n0 + 1, 0)
                whole = CHUNKS // 2 if n0 + 3 * CHUNKS < N_UNITS else CHUNKS // 2 - 1
                with dve.Fori(0, whole) as i:
                    for j in range(2):
                        for u in range(3):
                            split_lo(n0 + 5 + 3 * j + u, turn=i)
                        chunk(n0 + 3 + 3 * j, 1 + j, turn=i)
                cur[0] = n0 + 5 + 6 * whole
                for c in range(1 + 2 * whole, CHUNKS):
                    split_to(n0 + 3 * c + 5)
                    chunk(n0 + 3 * c, c)

            def rope_unit(ph, j, tab, per=None):
                _, _, width, role = ph["units"][j]
                dim = role[1]
                r = nx(roped) - 1
                if r >= 2:
                    dve.wait_ge(rope_T, r - 1)
                if r:
                    dve.wait_ge(roped, r)
                w = dim if role[0] == "tail" else width
                H, hd = w // dim, dim // 2
                x = bank[j % 4][:, :].rearrange("p (t w) -> p t w", t=T)[:, :, 0:w].rearrange("p t (h d) -> p t h d", d=dim)
                cos = tab[:, :, 0:dim].unsqueeze(2).broadcast_to([P, T, H, dim])
                sin = tab[:, :, dim:2 * dim].unsqueeze(2).broadcast_to([P, T, H, dim])
                c_ = t1[:, 0:T * w].rearrange("p (t h d) -> p t h d", t=T, h=H)
                s_ = t2[:, 0:T * w].rearrange("p (t h d) -> p t h d", t=T, h=H)
                if role[0] == "tail":
                    iw = bank[j % 4][:, :].rearrange("p (t w) -> p t w", t=T)[:, :, dim:dim + 8]
                    nc.vector.tensor_scalar(ph["views"]["iw"], iw, 1.0 / 16, None, ALU.mult)
                nc.vector.tensor_tensor(c_, x, cos, ALU.mult)
                nc.vector.tensor_tensor(s_[:, :, :, 0:hd], x[:, :, :, hd:dim], sin[:, :, :, 0:hd], ALU.mult)
                nc.vector.tensor_tensor(s_[:, :, :, hd:dim], x[:, :, :, 0:hd], sin[:, :, :, hd:dim], ALU.mult)\
                    .then_inc(bank_free[j % 4], 1)
                dve.wait_ge(bank_free[j % 4], ph["left"][j])
                dst = qr[:, r % 2, :, :].rearrange("p t (h d) -> p t h d", d=dim)
                if per is not None:
                    link(nc.vector.tensor_tensor(c_, c_, s_, ALU.add))
                    nc.vector.tensor_tensor(dst, c_, per, ALU.mult).then_inc(roped, 1)
                elif role[0] == "tail":
                    four = [P, T, 4, dim]
                    nc.vector.tensor_tensor(dst[:, :, 0:4, :], c_.broadcast_to(four), s_.broadcast_to(four), ALU.add).then_inc(roped, 1)
                else:
                    nc.vector.tensor_tensor(dst, c_, s_, ALU.add).then_inc(roped, 1)

            def attention(L, hooks={}):
                for h in range(L["heads"]):
                    dve.wait_ge(s_done, L["h0"] + h + 1)
                    if h >= 2:
                        dve.wait_ge(p_done, 2 * (L["h0"] + h - 1))
                    if L["bias"]:
                        dve.wait_ge(bias_in[h % 3], 64 * (h // 3 + 1))
                    for t, (lo, hi) in enumerate(((0, 128), (128, 384))):
                        c = 2 * h + t
                        ins = nc.vector.tensor_tensor_reduce(
                            out=s_buf[:, h % 2, lo:hi], in0=bank[4 + h % 2][:, lo:hi], in1=L["mask"](h, t), scale=1.0,
                            scalar=-3e38, op0=ALU.add, op1=ALU.max, accum_out=L["mx"][:, c:c + 1])
                    link(ins)
                    nc.vector.tensor_scalar(L["nmax"][:, 2 * h:2 * h + 2], L["mx"][:, 2 * h:2 * h + 2], -L["scale"], None, ALU.mult)\
                        .then_inc(nmax_ok, 1)
                    if h in hooks:
                        hooks[h]()

            def inverse_sums(L, lo, hi):
                dve.wait_ge(o_done, L["h0"] + hi)
                v = L["sum"][:, 2 * lo:2 * hi]
                link(nc.vector.reciprocal(v, v))
                return v

            def out_lo(banks):
                for j, b in enumerate(banks):
                    dve.wait_ge(t_hi_ok, nx(t_hi_ok))
                    nc.vector.tensor_tensor(t_lo[:, 2 * j:2 * j + 2, :], bank[b][:, :].rearrange("p (a s) -> p a s", a=2),
                                            t_hi[:, 2 * j:2 * j + 2, :].bitcast(F32), ALU.subtract).then_inc(t_lo_ok, 1)

            def heads_out(L, o, lo=0):
                rs = inverse_sums(L, lo, L["heads"]).rearrange("p (h t) -> p h t", t=T)
                G = (L["heads"] - lo) // 8
                for t in range(T):
                    for g in range(G):
                        ins = nc.vector.tensor_tensor(
                            o[:, t, g * HW:(g + 1) * HW].rearrange("p (h d) -> p h d", d=64),
                            bank[G * t + g][:, :].rearrange("p (h d) -> p h d", d=64),
                            rs[:, g * 8:(g + 1) * 8, t].unsqueeze(2).broadcast_to([P, 8, 64]), ALU.mult)
                return ins

            def mix_first(ph):
                V = ph["views"]
                link(nc.vector.memset(V["hpad"][:, :, 0:TAPS - 1], 0.0))
                taps_done = [0]
                tap_step = {}

                def taps(n):
                    for tap in range(taps_done[0], min(TAPS, taps_done[0] + n)):
                        for ct in range(3):
                            src = V["hpad"][:, ct, tap:tap + S]
                            w = tap_col[:, 4 * tap + ct:4 * tap + ct + 1]
                            acc = V["acc"][:, ct, :]
                            if tap == 0:
                                ins = nc.vector.tensor_scalar(acc, src, w, p_col[:, DW_B + ct:DW_B + ct + 1], ALU.mult, ALU.add)
                            else:
                                dve.wait_ge(dve_step, tap_step[ct])
                                ins = nc.vector.scalar_tensor_tensor(out=acc, in0=src, scalar=w, in1=acc, op0=ALU.mult, op1=ALU.add)
                            if tap == TAPS - 1:
                                ins.then_inc(conv_ok, 1)
                            else:
                                tap_step[ct] = step(ins)
                    taps_done[0] = min(TAPS, taps_done[0] + n)

                for j, (_, _, _, role) in enumerate(ph["units"]):
                    m = ph["n0"] + j
                    split_to(m + LEAD)
                    if role[0] == "glu_a":
                        dve.wait_ge(unit_used, m + 1)
                        dve.wait_ge(bank_free[j % 4 - 2], ph["left"][j - 2])
                        for c in range(2):
                            ct = 2 * role[1] + c
                            ins = nc.vector.scalar_tensor_tensor(
                                out=V["hpad"][:, ct, TAPS - 1:TAPS - 1 + S], in0=bank[j % 4][:, c * S:(c + 1) * S],
                                scalar=p_col[:, GLU_B + ct:GLU_B + ct + 1], in1=V["sig"][:, ct, :], op0=ALU.add, op1=ALU.mult)
                            ins.then_inc(bank_free[j % 4] if c else glu_ok, 1)
                        dve.wait_ge(bank_free[j % 4], ph["left"][j])
                    elif role[0] == "rope":
                        r = role_index[j]
                        dve.wait_ge(qsq_ok, nx(qsq_ok))
                        s8 = st[:, 32 + 8 * (r % 2):40 + 8 * (r % 2)]
                        link(nc.vector.tensor_reduce(s8, qsq.rearrange("p (a d) -> p a d", d=64), AX.X, ALU.add))
                        nc.vector.tensor_scalar(s8, s8, 1.0 / 64, EPS, ALU.mult, ALU.add).then_inc(ms_ready, 1)
                        taps(3)
                        dve.wait_ge(rstd_ready, nx(rstd_ready))
                        rope_unit(ph, j, qk_rope[:, role[3], :, :],
                                  per=s8.rearrange("p (t h) -> p t h", t=T).unsqueeze(3).broadcast_to([P, T, 4, 64]))
                        taps(2)
                    elif role[0] == "v":
                        taps(4)

                def centre():
                    dve.wait_ge(mean_ok, 1)
                    nc.vector.tensor_tensor(V["cen"], V["acc"], bank[2][:, 0:S].unsqueeze(1).broadcast_to([P, 4, S]), ALU.subtract)\
                        .then_inc(cen_ok, 1)

                def deviation():
                    dve.wait_ge(var_ok, 1)
                    nc.vector.tensor_scalar(st[:, 10:12], bank[3][:, 0:T], EPS, None, ALU.add).then_inc(ms_ready, 1)

                attention(V["L"], {0: lambda: taps(1), 1: lambda: taps(1), 2: lambda: taps(TAPS), 6: centre})
                deviation()
                heads_out(V["L"], V["o"]).then_inc(o_ready, 1)
                nx(rstd_ready)
                dve.wait_ge(spread_ok, 1)
                nc.vector.tensor_tensor(V["z"], V["cen"], bank[2][:, 0:S].unsqueeze(1).broadcast_to([P, 4, S]), ALU.mult).then_inc(z_ok, 1)
                out_lo((6, 7))
                dve.wait_ge(t_hi_ok, nx(t_hi_ok))
                nc.vector.tensor_tensor(t_lo[:, 4:8, :], V["sw"], t_hi[:, 4:8, :].bitcast(F32), ALU.subtract).then_inc(t_lo_ok, 1)
                split_to(ph["after"] + 2)

            role_index = {4: 0, 5: 1, 6: 2, 7: 3}

            tiles = ((0, 128), (128, 384))

            def add_index(V, h):
                dve.wait_ge(idx_relu, h + 1)
                if h:
                    dve.wait_ge(idx_added, 2 * h)
                for t, (lo, hi) in enumerate(tiles):
                    prior = masks[:, 384 + lo:384 + hi] if h == 0 else V["sel"][:, lo:hi]
                    nc.vector.scalar_tensor_tensor(out=V["sel"][:, lo:hi], in0=V["rel"][:, h % 4, lo:hi], scalar=V["iw"][:, t, h:h + 1],
                                                   in1=prior, op0=ALU.mult, op1=ALU.add).then_inc(idx_added, 1)

            def take_eight(V):
                for t, (lo, hi) in enumerate(tiles):
                    ins = nc.vector.max(out=st[:, 144 + 8 * t:152 + 8 * t], in_=V["sel"][:, lo:hi])
                link(ins)
                for t, (lo, hi) in enumerate(tiles):
                    ins = nc.vector.match_replace(out=V["sel"][:, lo:hi], in_to_replace=st[:, 144 + 8 * t:152 + 8 * t],
                                                  in_values=V["sel"][:, lo:hi], imm_value=TAKEN)
                link(ins)

            def mix_even(ph):
                V = ph["views"]
                L = V["L"]
                for j, (_, _, _, role) in enumerate(ph["units"]):
                    split_to(ph["n0"] + j + LEAD)
                    if role[0] in ("rope", "tail"):
                        dve.wait_ge(unit_used, ph["n0"] + j + 1)
                        rope_unit(ph, j, rope[:, :, 0:128] if role[1] == 64 else rope[:, :, 128:192])
                    if 5 <= j < 9:
                        add_index(V, 2 * j - 10)
                        add_index(V, 2 * j - 9)
                    if j == 8:
                        dve.wait_ge(idx_added, 16)
                    if j >= 9:
                        for _ in range(2 if j < 12 else 1):
                            take_eight(V)
                sel = V["sel"]
                link(nc.vector.tensor_scalar(sel, sel, TAKEN / 2, -NEG, ALU.is_le, ALU.mult))
                link(nc.vector.tensor_scalar(sel, sel, NEG, None, ALU.add))

                def halves():
                    rs = inverse_sums(L, 0, 8).rearrange("p (h c t) -> p h c t", c=2, t=T)
                    for t in range(T):
                        ins = nc.vector.tensor_scalar(rs[:, :, 1, t], rs[:, :, 1, t], st[:, 24:25], None, ALU.mult)
                    link(ins)
                    for t in range(T):
                        for c in range(2):
                            ins = nc.vector.tensor_tensor(
                                (V["oa"], V["oa1"])[c][:, t, :].rearrange("p (h d) -> p h d", d=128),
                                bank[2 * t + c][:, :].rearrange("p (h d) -> p h d", d=128),
                                rs[:, :, c, t].unsqueeze(2).broadcast_to([P, 4, 128]), ALU.mult)
                    ins.then_inc(halves_out, 1)

                def difference():
                    dve.wait_ge(halves_out, 1)
                    nc.vector.tensor_tensor(V["oa"], V["oa"], V["oa1"], ALU.subtract).then_inc(diff_ok, 1)

                def head_norm():
                    dve.wait_ge(qsq_ok, nx(qsq_ok))
                    link(nc.vector.tensor_reduce(st[:, 32:40], V["osq"].rearrange("p t (h d) -> p (t h) d", d=128), AX.X, ALU.add))
                    nc.vector.tensor_scalar(st[:, 32:40], st[:, 32:40], 1.0 / 128, EPS, ALU.mult, ALU.add).then_inc(ms_ready, 1)

                oa = V["oa"].rearrange("p t (h d) -> p (t h) d", d=128)

                def head_scale():
                    dve.wait_ge(rstd_ready, nx(rstd_ready))
                    link(nc.vector.scalar_tensor_tensor(out=oa, in0=oa, scalar=1.0 - LAMBDA_INIT,
                                                        in1=st[:, 32:40].unsqueeze(2).broadcast_to([P, 8, 128]),
                                                        op0=ALU.mult, op1=ALU.mult))

                def head_gain():
                    nc.vector.tensor_tensor(oa, oa, subln[:, :].unsqueeze(1).broadcast_to([P, 8, 128]), ALU.mult).then_inc(o_ready, 1)

                attention(L, {9: halves, 10: difference, 12: head_norm, 13: head_scale, 14: head_gain})
                heads_out(L, V["ob"], 8).then_inc(o_ready, 1)
                out_lo((4, 5, 6, 7))
                split_to(ph["after"] + 2)

            def mix_odd(ph):
                V = ph["views"]
                for j in range(len(ph["units"])):
                    split_to(ph["n0"] + j + LEAD)
                dve.wait_ge(bias_set, 2)
                attention(V["L"])
                heads_out(V["L"], V["o"]).then_inc(o_ready, 1)
                out_lo((4, 5, 6, 7))
                split_to(ph["after"] + 2)

            nc.vector.memset(zero_r[:, :].bitcast(F32), 0.0).then_inc(dve_step, 1)
            steps[0] = 1
            nc.vector.memset(st[:, 102:103], 0.0).then_inc(prod_done, 1)

            def setup():
                dve.wait_ge(setup_in[1], 16 * 6)
                for i in range(2):
                    ins = nc.vector.tensor_tensor_reduce(out=f_s[:, i, 0:64], in0=lam_in[:, 128 * i:128 * i + 64],
                                                         in1=lam_in[:, 128 * i + 64:128 * i + 128], scale=1.0, scalar=0.0,
                                                         op0=ALU.mult, op1=ALU.add, accum_out=st[:, 20 + i:21 + i])
                ins.then_inc(lam_sum, 1)
                for i in range(2):
                    g = qk_g[:, i, :].unsqueeze(1).broadcast_to([P, T, 64])
                    nc.vector.tensor_tensor(qk_rope[:, i, :, 0:64], rope[:, :, 0:64], g, ALU.mult)
                    nc.vector.tensor_tensor(qk_rope[:, i, :, 64:96], rope[:, :, 64:96], g[:, :, 32:64], ALU.mult)
                    ins = nc.vector.tensor_tensor(qk_rope[:, i, :, 96:128], rope[:, :, 96:128], g[:, :, 0:32], ALU.mult)
                link(ins)
                dve.wait_ge(lam_exp, 1)
                link(nc.vector.tensor_tensor(st[:, 24:25], st[:, 22:23], st[:, 23:24], ALU.subtract))
                link(nc.vector.tensor_scalar(st[:, 24:25], st[:, 24:25], LAMBDA_INIT, None, ALU.add))

            for ph in phases:
                if ph["kind"] == "edge":
                    edge(ph)
                    if ph["take"] == "input":
                        split_to(LEAD)
                        setup()
                elif ph["kind"] == "ffn":
                    ffn(ph)
                elif ph["kind"] == "mix":
                    {"first": mix_first, "even": mix_even, "odd": mix_odd}[ph["which"]](ph)


_INS = ["x", "norm1_g", "w_in", "glu_b", "q_norm_g", "k_norm_g", "dw_w", "dw_b", "conv_ln_g", "conv_ln_b", "w_out", "norm2_g",
        "w_gate", "w_up", "w_down", "norm_g_2", "ffn_wg_2", "ffn_wu_2", "ffn_wd_2", "even_w_in_2", "even_w_out_2",
        "even_lambda_2", "even_subln_2", "odd_w_in_2", "odd_w_out_2", "odd_rel_bias_2"]


def plan(a):
    def mlp(l, i):
        return dict(kind="ffn", wg=a["ffn_wg_2"][l, i], wu=a["ffn_wu_2"][l, i], wd=a["ffn_wd_2"][l, i])

    def edge(take, g, row=None, scale=None):
        return dict(kind="edge", take=take, g=g, row=row, scale=scale)

    def post(l, i, scale, g):
        return edge("post", g, a["norm_g_2"][l, i, :], scale)

    return [edge("input", 0), dict(kind="mix", which="first"),
            edge("add", 1), dict(kind="ffn", wg=a["w_gate"][0], wu=a["w_up"][0], wd=a["w_down"][0]),
            edge("add", 2), mlp(0, 0), post(0, 1, 0.5, 3), dict(kind="mix", which="even"),
            post(0, 3, 1.0, 4), mlp(0, 1), post(0, 5, 0.5, 5), mlp(1, 0),
            post(1, 1, 0.5, 6), dict(kind="mix", which="odd"), post(1, 3, 1.0, 7), mlp(1, 1), post(1, 5, 0.5, None)]


def kernel(**inputs):
    import concourse.bacc as _bacc
    from concourse.bass_utils import run_bass_kernel_spmd as _run

    nc = _bacc.Bacc("TRN2", target_bir_lowering=False, num_devices=1)
    arrays, a = {}, {}
    given = {name: np.ascontiguousarray(inputs[name]) for name in _INS}
    given.update(host_tables())
    for name, v in given.items():
        arrays[f"in_{name}"] = v
        a[name] = nc.dram_tensor(f"in_{name}", v.shape, mybir.dt.from_np(v.dtype), kind="ExternalInput").ap()
    out = nc.dram_tensor("out_x", (1, S, D), F32, kind="ExternalOutput").ap()

    def rows(v):
        return v.rearrange("(r p) -> r p", p=P)

    norms = [a["norm1_g"][0], a["norm2_g"][0]] + [a["norm_g_2"][l, i] for l in range(2) for i in (0, 2, 4)]
    a["param_rows"] = ([(rows(v), 8 * i, 8) for i, v in enumerate(norms)]
                       + [(rows(a["glu_b"][0]), 64, 8), (rows(a["dw_b"][0]), 72, 4), (rows(a["conv_ln_g"][0]), 76, 4),
                          (rows(a["conv_ln_b"][0]), 80, 4)])
    build(nc, a, out, plan(a))
    r = _run(nc, [arrays], core_ids=[0])
    return r.results[0]["out_x"]
```

```python
import math
from contextlib import ExitStack

import numpy as np
import concourse.bass as bass
from concourse import mybir

F32 = mybir.dt.float32
F32R = mybir.dt.float32r
ALU = mybir.AluOpType
ACT = mybir.ActivationFunctionType
AX = mybir.AxisListType

P = 128
S = 256
T = S // P
D = 1024
KT = D // P
FF = 2816
UC = 256
UNIT = KT * UC
CHUNKS = FF // UC
HW = 512
RAWS = 3
SLOTS = 6
LEAD = SLOTS - 1
TAPS = 31
EPS = 1e-6
K_ORDER = (0, 2, 4, 6, 1, 3, 5, 7)
NEG = -1e30
TAKEN = -3e38
TOPK = 64
LAMBDA_INIT = 0.8 - 0.6 * math.exp(-0.3 * 0)
WS = 9984


def host_tables():
    def rope(dim):
        inv = (np.float32(10000.0) ** (-np.arange(0, dim, 2, dtype=np.float32) / np.float32(dim))).astype(np.float32)
        ang = np.arange(S, dtype=np.float32)[:, None] * inv[None, :]
        c, s = np.cos(ang).astype(np.float32), np.sin(ang).astype(np.float32)
        return np.concatenate([c, c, -s, s], axis=1)
    r64, r32 = rope(64), rope(32)
    q, k = np.arange(P)[:, None], np.arange(P)[None, :]
    zero = np.zeros((P, P), np.float32)
    causal = np.where(k <= q, 0.0, NEG).astype(np.float32)
    chunky = np.where(k // 64 <= q // 64, 0.0, NEG).astype(np.float32)
    return {
        "rope_tab": np.concatenate([r64, r32], axis=1).astype(np.float32),
        "mask_tab": np.concatenate([causal, zero, causal, chunky, zero, chunky], axis=1).astype(np.float32),
        "ident_tab": np.eye(P, dtype=np.float32),
    }


def build(nc, a, out, phases):
    stack = ExitStack()
    with stack:
        def sb(name, shape, dt=F32):
            return stack.enter_context(nc.sbuf_tensor(name, shape, dt))

        def sem(name):
            return stack.enter_context(nc.semaphore(name))

        raw = sb("raw", [P, RAWS, UNIT])
        w_hi = sb("w_hi", [P, SLOTS, UNIT], F32R)
        w_lo = sb("w_lo", [P, SLOTS, UNIT], F32R)
        x_sb = sb("x_sb", [P, T, D])
        t_hi = sb("t_hi", [P, KT, S], F32R)
        t_lo = sb("t_lo", [P, KT, S], F32R)
        f_hi = sb("f_hi", [P, 2, 512], F32R)
        f_lo = sb("f_lo", [P, 2, 512], F32R)
        g_row = sb("g_row", [P, D])
        ws = sb("ws", [P, WS])
        st = sb("st", [P, 160])
        ident = sb("ident", [P, P])
        masks = sb("masks", [P, 768])
        rope = sb("rope", [P, T, 192])
        zero_r = sb("zero_r", [P, 256], F32R)
        minus_half = sb("minus_half", [P, 8])
        mean_w = sb("mean_w", [P, P])
        p_col = sb("p_col", [P, a["param_rows"].shape[0]])[:, :]
        tap_col = sb("tap_col", [P, 4 * TAPS])[:, :]
        qk_rope = sb("qk_rope", [P, 2, T, 128])
        subln = sb("subln", [P, P])

        psum = stack.enter_context(nc.psum_tensor("psum", [P, 8, 512], F32))
        bank = [psum[:, i, :] for i in range(8)]

        def wv(at, *shape):
            n = int(np.prod(shape))
            v = ws[:, at:at + n]
            if len(shape) == 1:
                return v
            names = "abcd"[:len(shape)]
            return v.rearrange(f"p ({' '.join(names)}) -> p {' '.join(names)}",
                               **{c: s for c, s in zip(names, shape)})

        xn = wv(0, T, D)
        junk = wv(5120, 2, D)
        f_s = wv(3072, 2, 512)
        f_p = wv(4096, 2, 512)
        yg = wv(7168, T, D)
        p_rows, w_rows = wv(9216, P)[0:a["param_rows"].shape[0], :], wv(9344, P)[0:4 * TAPS, :]
        lam_in, qk_g = wv(9472, 256), wv(9728, 2, 64)
        t1, t2, qr, qsq = wv(0, 512), wv(512, 512), wv(1024, 2, T, UC), wv(2048, 512)
        s_buf, p_buf, pt_buf = wv(0, 2, 384), wv(768, 2, 384), wv(1536, 2, 384)

        def heads64(buf, h):
            return buf[64 * (h % 2):64 * (h % 2) + 64, h // 2, :]

        def attention_plan(heads, q, k, v, o, mask, h0, bias=False):
            return dict(heads=heads, q=q, k=k, v=v, o=o, mask=mask, h0=h0, bias=bias, scale=1.0 if bias else 0.125,
                        mx=st[:, 48:48 + 2 * heads], nmax=st[:, 80:80 + 2 * heads], sum=st[:, 112:112 + 2 * heads])

        def wide(h):
            return 64 if h % 8 == 7 else 128

        def table_mask(base):
            return lambda h, t: base[:, 0:128] if t == 0 else base[:, 128:384]

        h0 = 0
        for ph in phases:
            if ph["kind"] != "mix":
                continue
            if ph["which"] == "first":
                q, k, v = wv(5752, 4, S), wv(6776, 4, S), wv(7800, T, HW)
                V = dict(sig=wv(2560, 4, S), o=wv(2560, T, HW), hpad=wv(3584, 4, S + TAPS - 1), sq=wv(3584, 4, S),
                         acc=wv(4728, 4, S), sw=wv(5752, 4, S), z=wv(6776, 4, S), v=v)
                V["cen"] = V["acc"]
                V["L"] = attention_plan(8, lambda h, q=q: heads64(q, h), lambda h, k=k: heads64(k, h),
                                        lambda h, kt, v=v: v[:, kt, 64 * h:64 * h + wide(h)],
                                        lambda h, t: bank[t][:, 64 * h:64 * h + wide(h)], table_mask(masks[:, 0:384]), h0)
                h0 += 8
                w = a["w_in"][0]
                ph["units"] = ([(w, 3 * HW + HW + UC * i, UC, ("glu_g", i)) for i in range(2)]
                               + [(w, 3 * HW + UC * i, UC, ("glu_a", i)) for i in range(2)]
                               + [(w, HW + UC * i, UC, ("rope", 64, k[:, 2 * i:2 * i + 2, :], 1)) for i in range(2)]
                               + [(w, UC * i, UC, ("rope", 64, q[:, 2 * i:2 * i + 2, :], 0)) for i in range(2)]
                               + [(w, 2 * HW + UC * i, UC, ("v", v[:, :, UC * i:UC * (i + 1)])) for i in range(2)])
                ph["w_out"] = a["w_out"][0]
            elif ph["which"] == "even":
                bq, bk, aq, ak = (wv(2560 + 1024 * i, 4, S) for i in range(4))
                av, bv = wv(6656, T, HW), wv(7680, T, HW)
                iq, ik = wv(8704, 2, S), wv(9216, S)
                sel = wv(9472, 384)
                V = dict(iq=iq, ik=ik, rel=wv(6656, 4, 384), sel=sel, iw=wv(9856, T, 8),
                         oa=wv(4608, T, HW), oa1=wv(5632, T, HW), ob=wv(5632, T, HW), osq=wv(6656, T, HW))
                V["L"] = attention_plan(
                    16, lambda h: heads64((aq, bq)[h // 8], h % 8), lambda h: heads64((ak, bk)[h // 8], h % 8),
                    lambda h, kt: av[:, kt, 128 * (h // 2):128 * (h // 2) + 128] if h < 8 else bv[:, kt, 64 * h - 512:64 * h - 512 + wide(h)],
                    lambda h, t: (bank[2 * t + h % 2][:, 128 * (h // 2):128 * (h // 2) + 128] if h < 8
                                  else bank[t][:, 64 * h - 512:64 * h - 512 + wide(h)]),
                    lambda h, t: table_mask(masks[:, 384:768] if h < 8 else sel)(h, t), h0)
                h0 += 16
                w = a["even_w_in_2"][0]
                at = 3 * HW
                two = lambda c0, dst: [(w, c0 + UC * i, UC, ("rope", 64, dst[:, 2 * i:2 * i + 2, :], None)) for i in range(2)]
                val = lambda c0, dst: [(w, c0 + UC * i, UC, ("v", dst[:, :, UC * i:UC * (i + 1)])) for i in range(2)]
                ph["units"] = ([(w, 6 * HW, UC, ("rope", 32, iq, None)), (w, 6 * HW + UC, 40, ("tail", 32, ik, None))]
                               + two(at, bq) + two(at + HW, bk) + two(0, aq) + two(HW, ak) + val(2 * HW, av) + val(at + 2 * HW, bv))
                ph["w_out"] = a["even_w_out_2"][0]
            else:
                q, k, v = wv(2304, 8, S), wv(4352, 8, S), wv(6400, T, D)
                bias = wv(8448, 4, 256)
                V = dict(bias=bias, o0=wv(2304, T, HW), o1=wv(3328, T, HW))

                def reversed_bias(h, t):
                    n = P * (t + 1)
                    b = bias[:, h % 4, 0:n]
                    return bass.AP(b.tensor, b.offset + n - 1, [list(b.ap[0]), [-1, n]])

                V["L"] = attention_plan(16, lambda h: heads64(q, h), lambda h: heads64(k, h),
                                        lambda h, kt: v[:, kt, 64 * h:64 * h + wide(h)],
                                        lambda h, t: bank[2 * t + h // 8][:, 64 * (h % 8):64 * (h % 8) + wide(h)], reversed_bias, h0, bias=True)
                h0 += 16
                w = a["odd_w_in_2"][0]
                ph["units"] = ([(w, UC * i, UC, ("c", q[:, 2 * i:2 * i + 2, :], 0.125)) for i in range(4)]
                               + [(w, D + UC * i, UC, ("c", k[:, 2 * i:2 * i + 2, :])) for i in range(4)]
                               + [(w, 2 * D + UC * i, UC, ("v", v[:, :, UC * i:UC * (i + 1)])) for i in range(4)])
                ph["w_out"] = a["odd_w_out_2"][0]
            ph["views"] = V

        raw_in = [sem(f"raw_in{i}") for i in range(RAWS)]
        setup_in = [sem(f"setup_in{i}") for i in range(3)]
        x_in = [sem(f"x_in{t}") for t in range(T)]
        ident_in = sem("ident_in")
        summed0 = sem("summed0")
        yg_done = sem("yg_done")
        glu_ok = sem("glu_ok")
        tap_made = sem("tap_made")
        tap_added = sem("tap_added")
        spread_ok = sem("spread_ok")
        halves_out = sem("halves_out")
        diff_ok = sem("diff_ok")
        hi_done = sem("hi_done")
        lo_done = sem("lo_done")
        unit_used = sem("unit_used")
        consts_set = sem("consts_set")
        params_T = sem("params_T")
        params_ok = sem("params_ok")
        x_ready = sem("x_ready")
        sq_done = sem("sq_done")
        ms_ready = sem("ms_ready")
        rstd_ready = sem("rstd_ready")
        xn_ready = sem("xn_ready")
        x_T = sem("x_T")
        t_hi_ok = sem("t_hi_ok")
        t_lo_ok = sem("t_lo_ok")
        silu_done = sem("silu_done")
        prod_done = sem("prod_done")
        prodhi_done = sem("prodhi_done")
        prodlo_done = sem("prodlo_done")
        grow_in = sem("grow_in")
        dve_step = sem("dve_step")
        bank_free = [sem(f"bank_free{i}") for i in range(4)]
        roped = sem("roped")
        rope_T = sem("rope_T")
        rope_kept = sem("rope_kept")
        conv_ok = sem("conv_ok")
        mean_ok = sem("mean_ok")
        cen_ok = sem("cen_ok")
        sq4_ok = sem("sq4_ok")
        var_ok = sem("var_ok")
        z_ok = sem("z_ok")
        swish_ok = sem("swish_ok")
        qsq_ok = sem("qsq_ok")
        s_done = sem("s_done")
        nmax_ok = sem("nmax_ok")
        p_done = sem("p_done")
        pt_done = sem("pt_done")
        pt_kept = sem("pt_kept")
        o_done = sem("o_done")
        o_ready = sem("o_ready")
        o_T = sem("o_T")
        idx_done = sem("idx_done")
        idx_relu = sem("idx_relu")
        idx_added = sem("idx_added")
        bias_in = [sem(f"bias_in{i}") for i in range(4)]
        bias_set = sem("bias_set")
        lam_sum = sem("lam_sum")
        lam_exp = sem("lam_exp")
        out_done = sem("out_done")

        n_units = n_ffn = n_rope = n_rstd = n_lo = 0
        widths = {}
        uses = [0] * 4
        for ph in phases:
            ph["n0"] = n_units
            if ph["kind"] == "ffn":
                ph["f"] = n_ffn
                n_ffn += 1
                n_units += 3 * CHUNKS
            elif ph["kind"] == "mix":
                ph["r0"] = n_rope
                n_rope += sum(u[3][0] in ("rope", "tail") for u in ph["units"])
                ph["left"] = []
                for j, u in enumerate(ph["units"]):
                    widths[n_units + j] = u[2]
                    uses[j % 4] += 1
                    ph["left"].append(uses[j % 4])
                n_units += len(ph["units"]) + 4
            ph["after"] = n_units
            ph["lo0"] = n_lo
            n_lo += {"edge": KT * (ph.get("g") is not None), "ffn": 0, "mix": 3 if ph.get("which") == "first" else 4}[ph["kind"]]
            n_rstd += {"edge": T * (ph.get("take") == "post") + T * (ph.get("g") is not None), "ffn": 0,
                       "mix": {"first": 5, "even": 1}.get(ph.get("which"), 0)}[ph["kind"]]
            ph["rstd"] = n_rstd
        N_UNITS = n_units
        for ph, following in zip(phases, phases[1:]):
            ph["xb"] = 0 if following["kind"] == "ffn" else 4
        GLU_B, DW_B, LN_G, LN_B = 64, 72, 76, 80

        def idx_bank(ph, h):
            return 4 + (ph["r0"] + h // 2 + 3 + h % 2) % 4

        def col_src(w, c0, nc_=UC):
            return w.rearrange("(k p) n -> p k n", p=P)[:, :, bass.ds(c0, nc_)]

        def row_src(w, r0):
            return w[bass.ds(r0, UC), :].rearrange("(r p) n -> p r n", p=P)

        def raw_view(n, w, by_rows=False):
            v = raw[:, n % RAWS, 0:KT * w]
            return v.rearrange("p (r n) -> p r n", r=2) if by_rows else v.rearrange("p (k n) -> p k n", k=KT)

        def tap_product(tap):
            return wv((2560, 3072, 8824, 9336)[tap % 4], 2, S)

        block = stack.enter_context(nc.Block())

        @block.sync
        def _(sp):
            def load(n, src, width=UC, by_rows=False, turn=0):
                if n >= RAWS:
                    sp.wait_ge(lo_done, n - RAWS + 1 + SLOTS * turn)
                sp.dma_start(raw_view(n, width, by_rows), src).then_inc(raw_in[n % RAWS], 16)

            for t in range(T):
                sp.dma_start(x_sb[:, t, :], a["x"][0, t * P:(t + 1) * P, :]).then_inc(x_in[t], 16)
            for ph in phases:
                n = ph["n0"]
                if ph["kind"] == "mix":
                    for w, c0, width, _ in ph["units"]:
                        load(n, col_src(w, c0, width), width)
                        n += 1
                    for r in range(4):
                        load(n, row_src(ph["w_out"], r * UC), by_rows=True)
                        n += 1
                elif ph["kind"] == "ffn":
                    load(n, col_src(ph["wg"], 0))
                    load(n + 1, col_src(ph["wu"], 0))
                    with sp.Fori(0, CHUNKS // 2) as i:
                        for j in range(2):
                            m = n + 2 + 3 * j
                            c0 = i * (2 * UC) + (1 + j) * UC
                            load(m, col_src(ph["wg"], c0), turn=i)
                            load(m + 1, col_src(ph["wu"], c0), turn=i)
                            load(m + 2, row_src(ph["wd"], i * (2 * UC) + j * UC), by_rows=True, turn=i)
                    load(n + 3 * CHUNKS - 1, row_src(ph["wd"], FF - UC), by_rows=True)
            sp.wait_ge(out_done, 16 * T)

        @block.scalar
        def _(act):
            seen = {}

            def nx(s, k=1):
                seen[id(s)] = seen.get(id(s), 0) + k
                return seen[id(s)]

            cur = [0]

            def split_hi(n, width=UC, turn=0):
                act.wait_ge(raw_in[n % RAWS], 16 * (n // RAWS + 1) + turn * (16 * SLOTS // RAWS))
                if n >= SLOTS:
                    act.wait_ge(unit_used, n - SLOTS + 1 + turn * SLOTS)
                w = KT * width
                nc.scalar.activation(w_hi[:, n % SLOTS, 0:w], raw[:, n % RAWS, 0:w], ACT.Copy).then_inc(hi_done, 1)

            def split_to(n):
                while cur[0] < min(n, N_UNITS):
                    split_hi(cur[0], widths.get(cur[0], UC))
                    cur[0] += 1

            def edge(ph):
                if ph["take"] != "input":
                    nx(summed0)
                for t in range(T):
                    if ph["take"] == "post":
                        for h in range(2):
                            if h:
                                act.wait_ge(yg_done, nx(yg_done, 2) - 1)
                            elif t == 0:
                                act.wait_ge(summed0, seen[id(summed0)])
                            else:
                                act.wait_ge(unit_used, ph["after"])
                            i = 2 * t + h
                            nc.scalar.activation(junk[:, t, h * 512:(h + 1) * 512], bank[i], ACT.Square,
                                                 accum_out=st[:, 4 + i:5 + i]).then_inc(sq_done, 1)
                            nx(sq_done)
                    if ph["take"] == "input":
                        act.wait_ge(x_in[t], 16)
                    else:
                        act.wait_ge(x_ready, nx(x_ready))
                    if ph["g"] is None:
                        act.wait_ge(x_ready, nx(x_ready))
                        act.dma_start(out[0, t * P:(t + 1) * P, :], x_sb[:, t, :]).then_inc(out_done, 16)
                        continue
                    if ph["take"] == "post":
                        act.wait_ge(sq_done, seen[id(sq_done)])
                    for h in range(2):
                        if h and ph["take"] != "input":
                            act.wait_ge(x_ready, nx(x_ready))
                        hv, i = slice(h * 512, (h + 1) * 512), 12 + 2 * t + h
                        nc.scalar.activation(junk[:, t, hv], x_sb[:, t, hv], ACT.Square, accum_out=st[:, i:i + 1]).then_inc(sq_done, 1)
                        nx(sq_done)
                if ph["g"] is None:
                    return
                if ph["take"] == "input":
                    split_to(1)
                    act.wait_ge(params_T, 2)
                    nc.scalar.activation(p_col, bank[0][:, 0:p_col.shape[1]], ACT.Copy).then_inc(params_ok, 1)
                    nc.scalar.activation(tap_col, bank[1][:, 0:4 * TAPS], ACT.Copy).then_inc(params_ok, 1)
                    act.wait_ge(params_ok, 2)
                for i, k in enumerate(K_ORDER):
                    if i < 4:
                        act.wait_ge(x_T, nx(x_T))
                    else:
                        act.wait_ge(t_lo_ok, ph["lo0"] + i - 3)
                    g = ph["g"] * KT + k
                    nc.scalar.activation(t_hi[:, k, :], bank[ph["xb"] + k // 2][:, (k % 2) * S:(k % 2 + 1) * S], ACT.Copy,
                                         scale=p_col[:, g:g + 1]).then_inc(t_hi_ok, 1)

            def ffn(ph):
                n0 = ph["n0"]

                def chunk(s, c, turn=0):
                    act.wait_ge(unit_used, s + 1 + turn * SLOTS)
                    nc.scalar.activation(f_s[:, c % 2, :], bank[4 + 2 * (c % 2)][:, :], ACT.Silu).then_inc(silu_done, 1)
                    act.wait_ge(prod_done, 1 + CHUNKS * ph["f"] + c + 1 + turn * 2)
                    nc.scalar.activation(f_hi[:, c % 2, :], f_p[:, c % 2, :], ACT.Copy).then_inc(prodhi_done, 1)

                split_to(n0 + 5)
                chunk(n0, 0)
                whole = CHUNKS // 2 if ph["n0"] + 3 * CHUNKS < N_UNITS else CHUNKS // 2 - 1
                with act.Fori(0, whole) as i:
                    for j in range(2):
                        for u in range(3):
                            split_hi(n0 + 5 + 3 * j + u, turn=i)
                        chunk(n0 + 2 + 3 * j, 1 + j, turn=i)
                cur[0] = n0 + 5 + 6 * whole
                for c in range(1 + 2 * whole, CHUNKS):
                    split_to(n0 + 3 * c + 5)
                    chunk(n0 + 3 * c - 1, c)

            def keep_rope(role):
                r = nx(rope_T) - 1
                act.wait_ge(rope_T, r + 1)
                n = S if role[0] == "tail" else 2 * S
                src = bank[4 + r % 4][:, 0:n]
                if role[0] != "tail":
                    src = src.rearrange("p (a s) -> p a s", a=2)
                nc.scalar.activation(role[2], src, ACT.Copy).then_inc(rope_kept, 1)

            def keep_unit(ph, j):
                act.wait_ge(unit_used, ph["n0"] + j + 1)
                nc.scalar.activation(ph["units"][j][3][1], bank[j % 4][:, :].rearrange("p (a s) -> p a s", a=2), ACT.Copy,
                                     scale=(ph["units"][j][3] + (1.0,))[2])\
                    .then_inc(bank_free[j % 4], 1)

            def keep_pt(L, h):
                act.wait_ge(pt_done, L["h0"] + h + 1)
                if h >= 2:
                    act.wait_ge(o_done, L["h0"] + h - 1)
                nc.scalar.activation(pt_buf[:, h % 2, :], bank[6 + h % 2][:, 0:384], ACT.Copy).then_inc(pt_kept, 1)

            def attention(L, hooks={}):
                for h in range(L["heads"]):
                    act.wait_ge(nmax_ok, L["h0"] + h + 1)
                    if h >= 2:
                        act.wait_ge(pt_done, L["h0"] + h - 1)
                    for t, (lo, hi) in enumerate(((0, 128), (128, 384))):
                        c = 2 * h + t
                        nc.scalar.activation(p_buf[:, h % 2, lo:hi], s_buf[:, h % 2, lo:hi], ACT.Exp, scale=L["scale"],
                                             bias=L["nmax"][:, c:c + 1], accum_out=L["sum"][:, c:c + 1]).then_inc(p_done, 1)
                    if h >= 1:
                        keep_pt(L, h - 1)
                    if h in hooks:
                        hooks[h]()
                keep_pt(L, L["heads"] - 1)

            def out_hi(banks):
                for j, b in enumerate(banks):
                    act.wait_ge(o_T, nx(o_T))
                    nc.scalar.activation(t_hi[:, 2 * j:2 * j + 2, :], bank[b][:, :].rearrange("p (a s) -> p a s", a=2),
                                         ACT.Copy).then_inc(t_hi_ok, 1)

            taps_done = [0]

            def taps(ph, n):
                V = ph["views"]
                for tap in range(taps_done[0], min(TAPS, taps_done[0] + n)):
                    if tap == 0:
                        act.wait_ge(glu_ok, 2)
                        act.wait_ge(bank_free[3], ph["left"][3])
                    if tap > 4:
                        act.wait_ge(tap_added, tap - 4)
                    for ct in (2, 3):
                        src, w = V["hpad"][:, ct, tap:tap + S], tap_col[:, 4 * tap + ct:4 * tap + ct + 1]
                        if tap == 0:
                            ins = nc.scalar.activation(V["acc"][:, ct, :], src, ACT.Identity, scale=w,
                                                       bias=p_col[:, DW_B + ct:DW_B + ct + 1])
                        else:
                            ins = nc.scalar.activation(tap_product(tap)[:, ct - 2, :], src, ACT.Copy, scale=w)
                    ins.then_inc(tap_made, 1)
                taps_done[0] = min(TAPS, taps_done[0] + n)

            def project(ph):
                roped_before = None
                for j, (_, _, _, role) in enumerate(ph["units"]):
                    m = ph["n0"] + j
                    split_to(m + LEAD)
                    if role[0] in "vc":
                        if ph["which"] == "even":
                            act.wait_ge(idx_added, 16)
                        keep_unit(ph, j)
                        if ph["which"] == "first":
                            taps(ph, 5 if j == 8 else 2)
                    elif role[0] == "glu_g":
                        act.wait_ge(unit_used, m + 1)
                        for c in range(2):
                            ct = 2 * role[1] + c
                            ins = nc.scalar.activation(ph["views"]["sig"][:, ct, :], bank[j % 4][:, c * S:(c + 1) * S], ACT.Sigmoid,
                                                       bias=p_col[:, GLU_B + 4 + ct:GLU_B + 5 + ct])
                        ins.then_inc(bank_free[j % 4], 1)
                    elif role[0] == "rope" and ph["which"] == "first":
                        act.wait_ge(unit_used, m + 1)
                        r = seen.get(id(rope_T), 0) + (roped_before is not None)
                        if r:
                            act.wait_ge(roped, r)
                        nc.scalar.activation(qsq, bank[j % 4][:, :], ACT.Square).then_inc(qsq_ok, 1)
                        taps(ph, 4)
                    if ph["which"] == "even" and 4 <= j < 8:
                        for h in (2 * j - 8, 2 * j - 7):
                            act.wait_ge(idx_done, h + 1)
                            if h >= 4:
                                act.wait_ge(idx_added, 2 * (h - 3))
                            nc.scalar.activation(ph["views"]["rel"][:, h % 4, :], bank[idx_bank(ph, h)][:, 0:384], ACT.Relu)\
                                .then_inc(idx_relu, 1)
                    if roped_before:
                        keep_rope(roped_before)
                    roped_before = role if role[0] in ("rope", "tail") else None

            def mix_first(ph):
                V = ph["views"]
                project(ph)

                def squares():
                    act.wait_ge(cen_ok, 1)
                    nc.scalar.activation(V["sq"], V["cen"], ACT.Square).then_inc(sq4_ok, 1)

                attention(V["L"], {h: lambda: taps(ph, 2) for h in range(5)})
                squares()
                out_hi((6, 7))
                split_to(ph["after"] + 1)
                act.wait_ge(z_ok, 1)
                for ct in range(4):
                    nc.scalar.activation(V["sw"][:, ct, :], V["z"][:, ct, :], ACT.Silu, scale=p_col[:, LN_G + ct:LN_G + ct + 1],
                                         bias=p_col[:, LN_B + ct:LN_B + ct + 1]).then_inc(swish_ok, 1)
                act.wait_ge(swish_ok, 4)
                nc.scalar.activation(t_hi[:, 4:8, :], V["sw"], ACT.Copy).then_inc(t_hi_ok, 1)
                split_to(ph["after"] + 2)

            def mix_even(ph):
                V = ph["views"]
                project(ph)

                def squares():
                    act.wait_ge(diff_ok, 1)
                    nc.scalar.activation(V["osq"], V["oa"], ACT.Square).then_inc(qsq_ok, 1)

                attention(V["L"], {11: squares})
                out_hi((4, 5, 6, 7))
                split_to(ph["after"] + 2)

            def mix_odd(ph):
                project(ph)
                attention(ph["views"]["L"])
                out_hi((4, 5, 6, 7))
                split_to(ph["after"] + 2)

            act.dma_start(ident[:, :], a["ident_tab"]).then_inc(ident_in, 16)
            act.dma_start(p_rows, a["param_rows"]).then_inc(setup_in[0], 16)
            act.dma_start(w_rows, a["dw_w"][0].rearrange("t (c p) -> (t c) p", p=P)).then_inc(setup_in[0], 16)
            for ph in phases:
                if ph["kind"] == "edge":
                    edge(ph)
                    if ph["take"] == "input":
                        split_to(LEAD)
                        act.wait_ge(lam_sum, 1)
                        nc.scalar.activation(st[:, 22:24], st[:, 20:22], ACT.Exp).then_inc(lam_exp, 1)
                elif ph["kind"] == "ffn":
                    ffn(ph)
                elif ph["kind"] == "mix":
                    {"first": mix_first, "even": mix_even, "odd": mix_odd}[ph["which"]](ph)
        @block.gpsimd
        def _(pool):
            seen = {}

            def nx(s, k=1):
                seen[id(s)] = seen.get(id(s), 0) + k
                return seen[id(s)]

            nc.gpsimd.memset(minus_half[:, :], -0.5).then_inc(consts_set, 1)
            nc.gpsimd.memset(mean_w[:, :], 1.0 / HW).then_inc(consts_set, 1)
            pool.wait_ge(consts_set, 2)
            pool.dma_start(rope[:, :, :], a["rope_tab"].rearrange("(t p) c -> p t c", p=P)).then_inc(setup_in[1], 16)
            for i, name in enumerate(("q_norm_g", "k_norm_g")):
                pool.dma_start(qk_g[:, i, :], a[name][0, :].partition_broadcast(P)).then_inc(setup_in[1], 16)
            pool.dma_start(lam_in, a["even_lambda_2"][0].rearrange("a b -> (a b)").partition_broadcast(P)).then_inc(setup_in[1], 16)
            pool.dma_start(masks[:, :], a["mask_tab"]).then_inc(setup_in[1], 16)
            pool.dma_start(subln[:, :], a["even_subln_2"][0, :].partition_broadcast(P)).then_inc(setup_in[1], 16)

            def inv_root(v):
                pool.wait_ge(ms_ready, nx(ms_ready))
                nc.gpsimd.tensor_tensor(v, v, minus_half[:, 0:1].broadcast_to([P, v.shape[1]]), ALU.pow).then_inc(rstd_ready, 1)

            posts = [ph for ph in phases if ph.get("take") == "post"]
            if posts:
                pool.dma_start(g_row[:, :], posts[0]["row"].partition_broadcast(P)).then_inc(grow_in, 16)
            n_post = 0
            for ph in phases:
                if ph["kind"] == "edge":
                    for t in range(T):
                        if ph["take"] == "post":
                            inv_root(st[:, 8 + t:9 + t])
                        if ph["g"] is not None:
                            inv_root(st[:, 2 + t:3 + t])
                    if ph["take"] == "post":
                        n_post += 1
                        if n_post < len(posts):
                            pool.wait_ge(yg_done, 2 * T * n_post)
                            pool.dma_start(g_row[:, :], posts[n_post]["row"].partition_broadcast(P)).then_inc(grow_in, 16)
                elif ph["kind"] == "mix" and ph["which"] == "first":
                    V = ph["views"]
                    done = [0]

                    def taps(n):
                        for tap in range(done[0], min(TAPS, done[0] + n)):
                            if tap:
                                pool.wait_ge(tap_made, tap + 1)
                                if tap > 1:
                                    pool.wait_ge(tap_added, tap - 1)
                                nc.gpsimd.tensor_tensor(V["acc"][:, 2:4, :], V["acc"][:, 2:4, :], tap_product(tap), ALU.add)\
                                    .then_inc(tap_added, 1)
                        done[0] = min(TAPS, done[0] + n)

                    for r in range(4):
                        inv_root(st[:, 32 + 8 * (r % 2):40 + 8 * (r % 2)])
                        taps(4)
                    taps(TAPS)
                    inv_root(st[:, 10:12])
                elif ph["kind"] == "mix" and ph["which"] == "even":
                    inv_root(st[:, 32:40])
                elif ph["kind"] == "mix":
                    bias, L = ph["views"]["bias"], ph["views"]["L"]
                    nc.gpsimd.memset(bias[0:64, :, 0:64], NEG).then_inc(bias_set, 1)
                    for h in range(16):
                        if h >= 4:
                            pool.wait_ge(nmax_ok, L["h0"] + h - 3)
                        row = a["odd_rel_bias_2"][0, h, 0:1]
                        for half in range(2):
                            n = 256 - 64 * (1 - half)
                            pool.dma_start(bias[64 * half:64 * half + 64, h % 4, 256 - n:256],
                                           bass.AP(row.tensor, row.offset, [[1, 64], [1, n]])).then_inc(bias_in[h % 4], 16)

        @block.tensor
        def _(pe):
            seen = {}

            def nx(s, k=1):
                seen[id(s)] = seen.get(id(s), 0) + k
                return seen[id(s)]

            def three(o, lh, ll, rh, rl, start, stop):
                nc.tensor.matmul(o, lh, rh, start=start, stop=False)
                nc.tensor.matmul(o, lh, rl, start=False, stop=False)
                return nc.tensor.matmul(o, ll, rh, start=False, stop=stop)

            def w_cols(n, width=UC):
                v = [w[:, n % SLOTS, 0:KT * width].rearrange("p (k n) -> p k n", k=KT) for w in (w_hi, w_lo)]
                return v

            fresh = [None]

            def rows_ready(i, first):
                if first and fresh[0] is not None:
                    pe.wait_ge(t_lo_ok, fresh[0] + i + 1)
                    if i == KT - 1:
                        fresh[0] = None

            def by_channels(n, b, turn=0):
                pe.wait_ge(lo_done, n + 1 + turn * SLOTS)
                wh, wl = w_cols(n)
                for c in range(2):
                    for i, k in enumerate(K_ORDER):
                        rows_ready(i, c == 0)
                        mm = three(bank[b][:, c * S:(c + 1) * S], wh[:, k, c * P:(c + 1) * P], wl[:, k, c * P:(c + 1) * P],
                                   t_hi[:, k, :], t_lo[:, k, :], i == 0, i == KT - 1)
                mm.then_inc(unit_used, 1)

            def by_tokens(n, b, width=UC):
                pe.wait_ge(lo_done, n + 1)
                wh, wl = w_cols(n, width)
                for t in range(T):
                    for i, k in enumerate(K_ORDER):
                        rows_ready(i, t == 0)
                        mm = three(bank[b][:, t * UC:t * UC + width], t_hi[:, k, t * P:(t + 1) * P], t_lo[:, k, t * P:(t + 1) * P],
                                   wh[:, k, :], wl[:, k, :], i == 0, i == KT - 1)
                mm.then_inc(unit_used, 1)

            def by_rows(n, lh, ll, first=False, last=False, turn=0, tiles=range(T)):
                pe.wait_ge(lo_done, n + 1 + turn * SLOTS)
                wh, wl = [w[:, n % SLOTS, :].rearrange("p (r n) -> p r n", r=2) for w in (w_hi, w_lo)]
                for r in range(2):
                    for t in tiles:
                        for h in range(2):
                            mm = three(bank[2 * t + h][:, :], lh(r, t), ll(r, t), wh[:, r, h * 512:(h + 1) * 512],
                                       wl[:, r, h * 512:(h + 1) * 512], first and r == 0, last and r == 1)
                if T - 1 in tiles:
                    mm.then_inc(unit_used, 1)
                elif last:
                    mm.then_inc(summed0, 1)

            def edge(ph):
                if ph["g"] is None:
                    return
                if ph["take"] == "input":
                    pe.wait_ge(ident_in, 16)
                    pe.wait_ge(setup_in[0], 16 * 2)
                    for b, v in enumerate((p_rows, w_rows)):
                        n = v.shape[0]
                        nc.tensor.transpose(bank[b][:, 0:n], v, ident[0:n, 0:n]).then_inc(params_T, 1)
                if ph["take"] != "input":
                    nx(x_ready, 2 * T)
                if ph["take"] == "add" and ph["xb"] == 0:
                    pe.wait_ge(x_ready, seen[id(x_ready)])
                for t in range(T):
                    for k in range(KT):
                        if k % 4 == 0:
                            pe.wait_ge(xn_ready, nx(xn_ready))
                        mm = nc.tensor.transpose(bank[ph["xb"] + k // 2][:, (k % 2) * S + t * P:(k % 2) * S + (t + 1) * P],
                                                 xn[:, t, k * P:(k + 1) * P], ident[:, :])
                        if t == 1 and k % 2 == 1:
                            mm.then_inc(x_T, 1)
                fresh[0] = seen.get(id(t_lo_ok), 0)
                nx(t_lo_ok, KT)

            def ffn(ph):
                n0, c0 = ph["n0"], CHUNKS * ph["f"]
                def down(n, c, turn=0, **how):
                    pe.wait_ge(prodlo_done, c0 + c + 1 + turn * 2)
                    by_rows(n, lambda r, t: f_hi[:, c % 2, r * S + t * P:r * S + (t + 1) * P],
                            lambda r, t: f_lo[:, c % 2, r * S + t * P:r * S + (t + 1) * P], turn=turn, **how)

                by_channels(n0, 4)
                by_channels(n0 + 1, 5)
                for b in range(4):
                    for h in range(2):
                        nc.tensor.matmul(bank[b][:, h * 256:(h + 1) * 256], zero_r[:, 0:P], zero_r[:, :], start=h == 0, stop=False)

                def gate_up(j, i):
                    b = 4 + 2 * ((1 + j) % 2)
                    pe.wait_ge(prod_done, 1 + c0 + j + i * 2)
                    by_channels(n0 + 2 + 3 * j, b, i)
                    by_channels(n0 + 3 + 3 * j, b + 1, i)

                with pe.Fori(0, CHUNKS // 2 - 1) as i:
                    for j in range(2):
                        gate_up(j, i)
                        down(n0 + 4 + 3 * j, j, i)
                gate_up(0, CHUNKS // 2 - 1)
                down(n0 + 4, 0, CHUNKS // 2 - 1)
                gate_up(1, CHUNKS // 2 - 1)
                for t in range(T):
                    for c in (CHUNKS - 2, CHUNKS - 1):
                        down(n0 + (3 * c + 4 if c < CHUNKS - 1 else 3 * c + 2), c, last=c == CHUNKS - 1, tiles=(t,))

            idx_sent = [0]

            def turn_rope(role):
                r = nx(roped) - 1
                pe.wait_ge(roped, r + 1)
                if r >= 4:
                    pe.wait_ge(rope_kept, r - 3)
                if idx_sent[0]:
                    pe.wait_ge(idx_relu, idx_sent[0])
                for p in range(1 if role[0] == "tail" else 2):
                    for t in range(T):
                        mm = nc.tensor.transpose(bank[4 + r % 4][:, p * S + t * P:p * S + (t + 1) * P],
                                                 qr[:, r % 2, t, p * P:(p + 1) * P], ident[:, :])
                mm.then_inc(rope_T, 1)

            def project(ph):
                before = None
                for j, (_, _, width, role) in enumerate(ph["units"]):
                    if ph["left"][j] > 1:
                        pe.wait_ge(bank_free[j % 4], ph["left"][j] - 1)
                    if role[0] in ("glu_g", "glu_a", "c"):
                        by_channels(ph["n0"] + j, j % 4)
                    else:
                        by_tokens(ph["n0"] + j, j % 4, width)
                    if before:
                        turn_rope(before)
                    before = role if role[0] in ("rope", "tail") else None
                    if ph["which"] == "even" and 3 <= j < 7:
                        V = ph["views"]
                        pe.wait_ge(rope_kept, ph["r0"] + max(j - 2, 2))
                        for h in (2 * j - 6, 2 * j - 5):
                            q = V["iq"][32 * (h % 4):32 * (h % 4) + 32, h // 4, :]
                            k = V["ik"][32 * (h % 4):32 * (h % 4) + 32, :]
                            o = bank[idx_bank(ph, h)]
                            nc.tensor.matmul(o[:, 0:128], q[:, 0:128], k[:, 0:128], start=True, stop=True)
                            nc.tensor.matmul(o[:, 128:384], q[:, 128:256], k, start=True, stop=True).then_inc(idx_done, 1)
                            idx_sent[0] += 1
                for j in range(len(ph["units"]) - 4, len(ph["units"])):
                    pe.wait_ge(bank_free[j % 4], ph["left"][j])
                if id(roped) in seen:
                    pe.wait_ge(rope_kept, seen[id(roped)])

            def attention(L, hooks={}):
                H = L["heads"]

                def scores(h):
                    if h >= 2:
                        pe.wait_ge(nmax_ok, L["h0"] + h - 1)
                    b = bank[4 + h % 2]
                    q, k = L["q"](h), L["k"](h)
                    nc.tensor.matmul(b[:, 0:128], q[:, 0:128], k[:, 0:128], start=True, stop=True)
                    nc.tensor.matmul(b[:, 128:384], q[:, 128:256], k[:, 0:256], start=True, stop=True).then_inc(s_done, 1)

                def turn(h):
                    pe.wait_ge(p_done, 2 * (L["h0"] + h + 1))
                    if h >= 2:
                        pe.wait_ge(pt_kept, L["h0"] + h - 1)
                    for i in range(3):
                        mm = nc.tensor.transpose(bank[6 + h % 2][:, i * P:(i + 1) * P], p_buf[:, h % 2, i * P:(i + 1) * P], ident[:, :])
                    mm.then_inc(pt_done, 1)

                def values(h):
                    pe.wait_ge(pt_kept, L["h0"] + h + 1)
                    if L["heads"] == 16 and not L["bias"] and h == 8:
                        pe.wait_ge(halves_out, 1)
                    pt = pt_buf
                    o0, o1 = L["o"](h, 0), L["o"](h, 1)
                    nc.tensor.matmul(o0, pt[:, h % 2, 0:128], L["v"](h, 0), start=True, stop=True)
                    nc.tensor.matmul(o1, pt[:, h % 2, 128:256], L["v"](h, 0), start=True, stop=False)
                    nc.tensor.matmul(o1, pt[:, h % 2, 256:384], L["v"](h, 1), start=False, stop=True).then_inc(o_done, 1)

                for h in range(H + 2):
                    if h < H:
                        scores(h)
                    if 1 <= h <= H:
                        turn(h - 1)
                    if h >= 2:
                        values(h - 2)
                    if h in hooks:
                        hooks[h]()

            def out_turn(src, banks, parts=T):
                for t in range(T):
                    if t < parts:
                        pe.wait_ge(o_ready, nx(o_ready))
                    for j, b in enumerate(banks):
                        for c in range(2):
                            mm = nc.tensor.transpose(bank[b][:, c * S + t * P:c * S + (t + 1) * P], src(2 * j + c, t), ident[:, :])
                        if t == T - 1:
                            mm.then_inc(o_T, 1)

            def out_proj(ph, parts=(1, 1, 1, 1), hooks={}):
                n = ph["n0"] + len(ph["units"])

                def rows(u, tiles):
                    by_rows(n + u, lambda r, t: t_hi[:, 2 * u + r, t * P:(t + 1) * P],
                            lambda r, t: t_lo[:, 2 * u + r, t * P:(t + 1) * P], first=u == 0, last=u == 3, tiles=tiles)

                for u in range(4):
                    if parts[u]:
                        pe.wait_ge(t_lo_ok, nx(t_lo_ok))
                    rows(u, (0, 1) if u < 2 else (0,))
                    if u in hooks:
                        hooks[u]()
                for u in (2, 3):
                    rows(u, (1,))

            def mix_first(ph):
                V = ph["views"]
                project(ph)

                def mean():
                    pe.wait_ge(conv_ok, 2)
                    pe.wait_ge(tap_added, TAPS - 1)
                    for ct in range(4):
                        mm = nc.tensor.matmul(bank[2][:, 0:S], mean_w[:, :], V["acc"][:, ct, :], start=ct == 0, stop=ct == 3)
                    mm.then_inc(mean_ok, 1)

                def variance():
                    pe.wait_ge(sq4_ok, 1)
                    for t in range(T):
                        for ct in range(4):
                            mm = nc.tensor.matmul(bank[4][:, t:t + 1], V["sq"][:, ct, t * P:(t + 1) * P], mean_w[:, 0:1],
                                                  start=ct == 0, stop=ct == 3)
                    mm.then_inc(var_ok, 1)

                def spread():
                    pe.wait_ge(rstd_ready, ph["rstd"])
                    for t in range(T):
                        mm = nc.tensor.matmul(bank[5][:, t * P:(t + 1) * P], st[:, 10 + t:11 + t].broadcast_to([P, P]), ident[:, :],
                                              start=True, stop=True)
                    mm.then_inc(spread_ok, 1)

                attention(V["L"], {7: mean})
                out_turn(lambda k, t: V["o"][:, t, k * P:(k + 1) * P], (6, 7))
                variance()
                out_proj(ph, (1, 1, 1, 0), {0: spread})

            def mix_even(ph):
                V = ph["views"]
                project(ph)
                attention(V["L"])
                out_turn(lambda k, t: V["oa"][:, t, k * P:(k + 1) * P], (4, 5), 1)
                out_turn(lambda k, t: V["ob"][:, t, k * P:(k + 1) * P], (6, 7))
                out_proj(ph)

            def mix_odd(ph):
                V = ph["views"]
                project(ph)
                attention(V["L"])
                out_turn(lambda k, t: V["o0"][:, t, k * P:(k + 1) * P], (4, 5))
                out_turn(lambda k, t: V["o1"][:, t, k * P:(k + 1) * P], (6, 7))
                out_proj(ph)

            pe.wait_ge(dve_step, 1)
            for ph in phases:
                if ph["kind"] == "edge":
                    edge(ph)
                elif ph["kind"] == "ffn":
                    ffn(ph)
                elif ph["kind"] == "mix":
                    {"first": mix_first, "even": mix_even, "odd": mix_odd}[ph["which"]](ph)

        @block.vector
        def _(dve):
            seen = {}

            def nx(s, k=1):
                seen[id(s)] = seen.get(id(s), 0) + k
                return seen[id(s)]

            steps = [0]

            def step(ins):
                steps[0] += 1
                ins.then_inc(dve_step, 1)
                return steps[0]

            def link(ins):
                dve.wait_ge(dve_step, step(ins))

            cur = [0]

            def split_lo(n, width=UC, turn=0):
                dve.wait_ge(hi_done, n + 1 + turn * SLOTS)
                w = KT * width
                nc.vector.tensor_tensor(w_lo[:, n % SLOTS, 0:w], raw[:, n % RAWS, 0:w], w_hi[:, n % SLOTS, 0:w].bitcast(F32),
                                        ALU.subtract).then_inc(lo_done, 1)

            def split_to(n):
                while cur[0] < min(n, N_UNITS):
                    split_lo(cur[0], widths.get(cur[0], UC))
                    cur[0] += 1

            def edge(ph):
                take = ph["take"]

                if take != "input":
                    nx(summed0)
                if take == "post":
                    dve.wait_ge(grow_in, nx(grow_in, 16))

                def take_sums(t):
                    if take == "input":
                        dve.wait_ge(x_in[t], 16)
                    elif t == 0:
                        dve.wait_ge(summed0, seen[id(summed0)])
                    else:
                        dve.wait_ge(unit_used, ph["after"])
                    if take == "add":
                        for h in range(2):
                            hv = slice(h * 512, (h + 1) * 512)
                            nc.vector.tensor_tensor(x_sb[:, t, hv], bank[2 * t + h], x_sb[:, t, hv], ALU.add).then_inc(x_ready, 1)
                        nx(x_ready, 2)
                    elif take == "post":
                        for h in (1, 0):
                            if h == 0:
                                dve.wait_ge(sq_done, nx(sq_done))
                            hv = slice(h * 512, (h + 1) * 512)
                            nc.vector.scalar_tensor_tensor(out=yg[:, t, hv], in0=bank[2 * t + h], scalar=ph["scale"] * D ** 0.5,
                                                           in1=g_row[:, hv], op0=ALU.mult, op1=ALU.mult).then_inc(yg_done, 1)
                        dve.wait_ge(sq_done, nx(sq_done))
                        nc.vector.tensor_scalar(st[:, 8 + t:9 + t], st[:, 4 + 2 * t:5 + 2 * t], st[:, 5 + 2 * t:6 + 2 * t], D * EPS,
                                                ALU.add, ALU.add).then_inc(ms_ready, 1)

                def add_output(t):
                    if take == "post":
                        dve.wait_ge(rstd_ready, nx(rstd_ready))
                        dve.wait_ge(yg_done, nx(yg_done, 2))
                        for h in range(2):
                            hv = slice(h * 512, (h + 1) * 512)
                            nc.vector.scalar_tensor_tensor(out=x_sb[:, t, hv], in0=yg[:, t, hv], scalar=st[:, 8 + t:9 + t],
                                                           in1=x_sb[:, t, hv], op0=ALU.mult, op1=ALU.add).then_inc(x_ready, 1)
                        nx(x_ready, 2)

                def norm_sum(t):
                    if ph["g"] is not None:
                        dve.wait_ge(sq_done, nx(sq_done, 2))
                        nc.vector.tensor_scalar(st[:, 2 + t:3 + t], st[:, 12 + 2 * t:13 + 2 * t], st[:, 13 + 2 * t:14 + 2 * t], D * EPS,
                                                ALU.add, ALU.add).then_inc(ms_ready, 1)

                def norm_scale(t):
                    if ph["g"] is not None:
                        dve.wait_ge(rstd_ready, nx(rstd_ready))
                        for h in range(2):
                            hv = slice(h * 512, (h + 1) * 512)
                            nc.vector.tensor_scalar(xn[:, t, hv], x_sb[:, t, hv], st[:, 2 + t:3 + t], D ** 0.5, ALU.mult, ALU.mult)\
                                .then_inc(xn_ready, 1)

                take_sums(0)
                add_output(0)
                norm_sum(0)
                if take != "post":
                    norm_scale(0)
                take_sums(1)
                if take == "post":
                    norm_scale(0)
                add_output(1)
                norm_sum(1)
                norm_scale(1)
                if ph["g"] is None:
                    return
                if take == "input":
                    split_to(1)
                    dve.wait_ge(params_ok, 2)
                for k in K_ORDER:
                    dve.wait_ge(t_hi_ok, nx(t_hi_ok))
                    g = ph["g"] * KT + k
                    nc.vector.scalar_tensor_tensor(out=t_lo[:, k, :], in0=bank[ph["xb"] + k // 2][:, (k % 2) * S:(k % 2 + 1) * S],
                                                   scalar=p_col[:, g:g + 1], in1=t_hi[:, k, :].bitcast(F32),
                                                   op0=ALU.mult, op1=ALU.subtract).then_inc(t_lo_ok, 1)

            def ffn(ph):
                n0, c0 = ph["n0"], CHUNKS * ph["f"]

                def chunk(s, c, turn=0):
                    b = c % 2
                    dve.wait_ge(silu_done, c0 + c + 1 + turn * 2)
                    dve.wait_ge(unit_used, s + 1 + turn * SLOTS)
                    nc.vector.tensor_tensor(f_p[:, b, :], bank[5 + 2 * b][:, :], f_s[:, b, :], ALU.mult).then_inc(prod_done, 1)
                    dve.wait_ge(prodhi_done, c0 + c + 1 + turn * 2)
                    nc.vector.tensor_tensor(f_lo[:, b, :], f_p[:, b, :], f_hi[:, b, :].bitcast(F32), ALU.subtract)\
                        .then_inc(prodlo_done, 1)

                split_to(n0 + 5)
                chunk(n0 + 1, 0)
                whole = CHUNKS // 2 if n0 + 3 * CHUNKS < N_UNITS else CHUNKS // 2 - 1
                with dve.Fori(0, whole) as i:
                    for j in range(2):
                        for u in range(3):
                            split_lo(n0 + 5 + 3 * j + u, turn=i)
                        chunk(n0 + 3 + 3 * j, 1 + j, turn=i)
                cur[0] = n0 + 5 + 6 * whole
                for c in range(1 + 2 * whole, CHUNKS):
                    split_to(n0 + 3 * c + 5)
                    chunk(n0 + 3 * c, c)

            def rope_unit(ph, j, tab, per=None):
                _, _, width, role = ph["units"][j]
                dim = role[1]
                r = nx(roped) - 1
                if r >= 2:
                    dve.wait_ge(rope_T, r - 1)
                if r:
                    dve.wait_ge(roped, r)
                w = dim if role[0] == "tail" else width
                H, hd = w // dim, dim // 2
                x = bank[j % 4][:, :].rearrange("p (t w) -> p t w", t=T)[:, :, 0:w].rearrange("p t (h d) -> p t h d", d=dim)
                cos = tab[:, :, 0:dim].unsqueeze(2).broadcast_to([P, T, H, dim])
                sin = tab[:, :, dim:2 * dim].unsqueeze(2).broadcast_to([P, T, H, dim])
                c_ = t1[:, 0:T * w].rearrange("p (t h d) -> p t h d", t=T, h=H)
                s_ = t2[:, 0:T * w].rearrange("p (t h d) -> p t h d", t=T, h=H)
                if role[0] == "tail":
                    iw = bank[j % 4][:, :].rearrange("p (t w) -> p t w", t=T)[:, :, dim:dim + 8]
                    nc.vector.tensor_scalar(ph["views"]["iw"], iw, 1.0 / 16, None, ALU.mult)
                nc.vector.tensor_tensor(c_, x, cos, ALU.mult)
                nc.vector.tensor_tensor(s_[:, :, :, 0:hd], x[:, :, :, hd:dim], sin[:, :, :, 0:hd], ALU.mult)
                nc.vector.tensor_tensor(s_[:, :, :, hd:dim], x[:, :, :, 0:hd], sin[:, :, :, hd:dim], ALU.mult)\
                    .then_inc(bank_free[j % 4], 1)
                dve.wait_ge(bank_free[j % 4], ph["left"][j])
                dst = qr[:, r % 2, :, :].rearrange("p t (h d) -> p t h d", d=dim)
                if per is not None:
                    link(nc.vector.tensor_tensor(c_, c_, s_, ALU.add))
                    nc.vector.tensor_tensor(dst, c_, per, ALU.mult).then_inc(roped, 1)
                elif role[0] == "tail":
                    four = [P, T, 4, dim]
                    nc.vector.tensor_tensor(dst[:, :, 0:4, :], c_.broadcast_to(four), s_.broadcast_to(four), ALU.add).then_inc(roped, 1)
                else:
                    nc.vector.tensor_tensor(dst, c_, s_, ALU.add).then_inc(roped, 1)

            def attention(L, hooks={}):
                for h in range(L["heads"]):
                    dve.wait_ge(s_done, L["h0"] + h + 1)
                    if h >= 2:
                        dve.wait_ge(p_done, 2 * (L["h0"] + h - 1))
                    if L["bias"]:
                        dve.wait_ge(bias_in[h % 4], 32 * (h // 4 + 1))
                    for t, (lo, hi) in enumerate(((0, 128), (128, 384))):
                        c = 2 * h + t
                        ins = nc.vector.tensor_tensor_reduce(
                            out=s_buf[:, h % 2, lo:hi], in0=bank[4 + h % 2][:, lo:hi], in1=L["mask"](h, t), scale=1.0,
                            scalar=-3e38, op0=ALU.add, op1=ALU.max, accum_out=L["mx"][:, c:c + 1])
                    link(ins)
                    nc.vector.tensor_scalar(L["nmax"][:, 2 * h:2 * h + 2], L["mx"][:, 2 * h:2 * h + 2], -L["scale"], None, ALU.mult)\
                        .then_inc(nmax_ok, 1)
                    if h in hooks:
                        hooks[h]()

            def inverse_sums(L, lo, hi):
                dve.wait_ge(o_done, L["h0"] + hi)
                v = L["sum"][:, 2 * lo:2 * hi]
                link(nc.vector.reciprocal(v, v))
                return v

            def out_lo(banks):
                for j, b in enumerate(banks):
                    dve.wait_ge(t_hi_ok, nx(t_hi_ok))
                    nc.vector.tensor_tensor(t_lo[:, 2 * j:2 * j + 2, :], bank[b][:, :].rearrange("p (a s) -> p a s", a=2),
                                            t_hi[:, 2 * j:2 * j + 2, :].bitcast(F32), ALU.subtract).then_inc(t_lo_ok, 1)

            def heads_out(L, o, lo, first_bank, apart=1):
                rs = inverse_sums(L, lo, lo + 8).rearrange("p (h t) -> p h t", t=T)
                for t in range(T):
                    nc.vector.tensor_tensor(o[:, t, :].rearrange("p (h d) -> p h d", d=64),
                                            bank[first_bank + apart * t][:, :].rearrange("p (h d) -> p h d", d=64),
                                            rs[:, :, t].unsqueeze(2).broadcast_to([P, 8, 64]), ALU.mult).then_inc(o_ready, 1)

            def mix_first(ph):
                V = ph["views"]
                link(nc.vector.memset(V["hpad"][:, :, 0:TAPS - 1], 0.0))
                taps_done = [0]
                tap_step = {}

                def taps(n):
                    for tap in range(taps_done[0], min(TAPS, taps_done[0] + n)):
                        for ct in range(2):
                            src = V["hpad"][:, ct, tap:tap + S]
                            w = tap_col[:, 4 * tap + ct:4 * tap + ct + 1]
                            acc = V["acc"][:, ct, :]
                            if tap == 0:
                                ins = nc.vector.tensor_scalar(acc, src, w, p_col[:, DW_B + ct:DW_B + ct + 1], ALU.mult, ALU.add)
                            else:
                                dve.wait_ge(dve_step, tap_step[ct])
                                ins = nc.vector.scalar_tensor_tensor(out=acc, in0=src, scalar=w, in1=acc, op0=ALU.mult, op1=ALU.add)
                            if tap == TAPS - 1:
                                ins.then_inc(conv_ok, 1)
                            else:
                                tap_step[ct] = step(ins)
                    taps_done[0] = min(TAPS, taps_done[0] + n)

                for j, (_, _, _, role) in enumerate(ph["units"]):
                    m = ph["n0"] + j
                    if role[0] != "rope":
                        split_to(m + LEAD)
                    if role[0] == "glu_a":
                        dve.wait_ge(unit_used, m + 1)
                        dve.wait_ge(bank_free[j % 4 - 2], ph["left"][j - 2])
                        for c in range(2):
                            ct = 2 * role[1] + c
                            ins = nc.vector.scalar_tensor_tensor(
                                out=V["hpad"][:, ct, TAPS - 1:TAPS - 1 + S], in0=bank[j % 4][:, c * S:(c + 1) * S],
                                scalar=p_col[:, GLU_B + ct:GLU_B + ct + 1], in1=V["sig"][:, ct, :], op0=ALU.add, op1=ALU.mult)
                            ins.then_inc(bank_free[j % 4] if c else glu_ok, 1)
                        dve.wait_ge(bank_free[j % 4], ph["left"][j])
                    elif role[0] == "rope":
                        r = role_index[j]
                        dve.wait_ge(qsq_ok, nx(qsq_ok))
                        s8 = st[:, 32 + 8 * (r % 2):40 + 8 * (r % 2)]
                        link(nc.vector.tensor_reduce(s8, qsq.rearrange("p (a d) -> p a d", d=64), AX.X, ALU.add))
                        nc.vector.tensor_scalar(s8, s8, 1.0 / 64, EPS, ALU.mult, ALU.add).then_inc(ms_ready, 1)
                        split_to(m + LEAD)
                        dve.wait_ge(rstd_ready, nx(rstd_ready))
                        rope_unit(ph, j, qk_rope[:, role[3], :, :],
                                  per=s8.rearrange("p (t h) -> p t h", t=T).unsqueeze(3).broadcast_to([P, T, 4, 64]))
                        taps(1)
                    elif role[0] == "v":
                        taps(5 if j == 8 else 2)

                def centre():
                    dve.wait_ge(mean_ok, 1)
                    nc.vector.tensor_tensor(V["cen"], V["acc"], bank[2][:, 0:S].unsqueeze(1).broadcast_to([P, 4, S]), ALU.subtract)\
                        .then_inc(cen_ok, 1)

                some = lambda: taps(3)
                attention(V["L"], {**{h: some for h in range(6)}, 6: lambda: taps(TAPS), 7: centre})
                heads_out(V["L"], V["o"], 0, 0)
                out_lo((6, 7))
                dve.wait_ge(var_ok, 1)
                nc.vector.tensor_scalar(st[:, 10:12], bank[4][:, 0:T], EPS, None, ALU.add).then_inc(ms_ready, 1)
                nx(rstd_ready)
                split_to(ph["after"] + 1)
                dve.wait_ge(spread_ok, 1)
                nc.vector.tensor_tensor(V["z"], V["cen"], bank[5][:, 0:S].unsqueeze(1).broadcast_to([P, 4, S]), ALU.mult).then_inc(z_ok, 1)
                dve.wait_ge(t_hi_ok, nx(t_hi_ok))
                nc.vector.tensor_tensor(t_lo[:, 4:8, :], V["sw"], t_hi[:, 4:8, :].bitcast(F32), ALU.subtract).then_inc(t_lo_ok, 1)
                split_to(ph["after"] + 2)

            role_index = {4: 0, 5: 1, 6: 2, 7: 3}

            tiles = ((0, 128), (128, 384))

            def add_index(V, h):
                dve.wait_ge(idx_relu, h + 1)
                if h:
                    dve.wait_ge(idx_added, 2 * h)
                for t, (lo, hi) in enumerate(tiles):
                    prior = masks[:, 384 + lo:384 + hi] if h == 0 else V["sel"][:, lo:hi]
                    nc.vector.scalar_tensor_tensor(out=V["sel"][:, lo:hi], in0=V["rel"][:, h % 4, lo:hi], scalar=V["iw"][:, t, h:h + 1],
                                                   in1=prior, op0=ALU.mult, op1=ALU.add).then_inc(idx_added, 1)

            def take_eight(V):
                for t, (lo, hi) in enumerate(tiles):
                    ins = nc.vector.max(out=st[:, 144 + 8 * t:152 + 8 * t], in_=V["sel"][:, lo:hi])
                link(ins)
                for t, (lo, hi) in enumerate(tiles):
                    ins = nc.vector.match_replace(out=V["sel"][:, lo:hi], in_to_replace=st[:, 144 + 8 * t:152 + 8 * t],
                                                  in_values=V["sel"][:, lo:hi], imm_value=TAKEN)
                link(ins)

            def mix_even(ph):
                V = ph["views"]
                L = V["L"]
                for j, (_, _, _, role) in enumerate(ph["units"]):
                    split_to(ph["n0"] + j + LEAD)
                    if role[0] in ("rope", "tail"):
                        dve.wait_ge(unit_used, ph["n0"] + j + 1)
                        rope_unit(ph, j, rope[:, :, 0:128] if role[1] == 64 else rope[:, :, 128:192])
                    if 5 <= j < 9:
                        add_index(V, 2 * j - 10)
                        add_index(V, 2 * j - 9)
                    if j == 8:
                        dve.wait_ge(idx_added, 16)
                    if j >= 9:
                        for _ in range(2 if j < 12 else 1):
                            take_eight(V)
                sel = V["sel"]
                link(nc.vector.tensor_scalar(sel, sel, TAKEN / 2, -NEG, ALU.is_le, ALU.mult))
                link(nc.vector.tensor_scalar(sel, sel, NEG, None, ALU.add))

                def halves():
                    rs = inverse_sums(L, 0, 8).rearrange("p (h c t) -> p h c t", c=2, t=T)
                    for t in range(T):
                        ins = nc.vector.tensor_scalar(rs[:, :, 1, t], rs[:, :, 1, t], st[:, 24:25], None, ALU.mult)
                    link(ins)
                    for t in range(T):
                        for c in range(2):
                            ins = nc.vector.tensor_tensor(
                                (V["oa"], V["oa1"])[c][:, t, :].rearrange("p (h d) -> p h d", d=128),
                                bank[2 * t + c][:, :].rearrange("p (h d) -> p h d", d=128),
                                rs[:, :, c, t].unsqueeze(2).broadcast_to([P, 4, 128]), ALU.mult)
                    ins.then_inc(halves_out, 1)

                def difference():
                    dve.wait_ge(halves_out, 1)
                    nc.vector.tensor_tensor(V["oa"], V["oa"], V["oa1"], ALU.subtract).then_inc(diff_ok, 1)

                def head_norm():
                    dve.wait_ge(qsq_ok, nx(qsq_ok))
                    link(nc.vector.tensor_reduce(st[:, 32:40], V["osq"].rearrange("p t (h d) -> p (t h) d", d=128), AX.X, ALU.add))
                    nc.vector.tensor_scalar(st[:, 32:40], st[:, 32:40], 1.0 / 128, EPS, ALU.mult, ALU.add).then_inc(ms_ready, 1)

                oa = V["oa"].rearrange("p t (h d) -> p (t h) d", d=128)

                def head_scale():
                    dve.wait_ge(rstd_ready, nx(rstd_ready))
                    link(nc.vector.scalar_tensor_tensor(out=oa, in0=oa, scalar=1.0 - LAMBDA_INIT,
                                                        in1=st[:, 32:40].unsqueeze(2).broadcast_to([P, 8, 128]),
                                                        op0=ALU.mult, op1=ALU.mult))

                def head_gain():
                    nc.vector.tensor_tensor(oa, oa, subln[:, :].unsqueeze(1).broadcast_to([P, 8, 128]), ALU.mult).then_inc(o_ready, 1)

                attention(L, {9: halves, 10: difference, 12: head_norm, 13: head_scale, 14: head_gain})
                heads_out(L, V["ob"], 8, 0)
                out_lo((4, 5, 6, 7))
                split_to(ph["after"] + 2)

            def mix_odd(ph):
                V = ph["views"]
                for j in range(len(ph["units"])):
                    split_to(ph["n0"] + j + LEAD)
                dve.wait_ge(bias_set, 1)
                attention(V["L"], {10: lambda: heads_out(V["L"], V["o0"], 0, 0, 2)})
                heads_out(V["L"], V["o1"], 8, 1, 2)
                out_lo((4, 5, 6, 7))
                split_to(ph["after"] + 2)

            nc.vector.memset(zero_r[:, :].bitcast(F32), 0.0).then_inc(dve_step, 1)
            steps[0] = 1
            nc.vector.memset(st[:, 102:103], 0.0).then_inc(prod_done, 1)

            def setup():
                dve.wait_ge(setup_in[1], 16 * 6)
                for i in range(2):
                    ins = nc.vector.tensor_tensor_reduce(out=f_s[:, i, 0:64], in0=lam_in[:, 128 * i:128 * i + 64],
                                                         in1=lam_in[:, 128 * i + 64:128 * i + 128], scale=1.0, scalar=0.0,
                                                         op0=ALU.mult, op1=ALU.add, accum_out=st[:, 20 + i:21 + i])
                ins.then_inc(lam_sum, 1)
                for i in range(2):
                    g = qk_g[:, i, :].unsqueeze(1).broadcast_to([P, T, 64])
                    nc.vector.tensor_tensor(qk_rope[:, i, :, 0:64], rope[:, :, 0:64], g, ALU.mult)
                    nc.vector.tensor_tensor(qk_rope[:, i, :, 64:96], rope[:, :, 64:96], g[:, :, 32:64], ALU.mult)
                    ins = nc.vector.tensor_tensor(qk_rope[:, i, :, 96:128], rope[:, :, 96:128], g[:, :, 0:32], ALU.mult)
                link(ins)
                dve.wait_ge(lam_exp, 1)
                link(nc.vector.tensor_tensor(st[:, 24:25], st[:, 22:23], st[:, 23:24], ALU.subtract))
                link(nc.vector.tensor_scalar(st[:, 24:25], st[:, 24:25], LAMBDA_INIT, None, ALU.add))

            for ph in phases:
                if ph["kind"] == "edge":
                    edge(ph)
                    if ph["take"] == "input":
                        split_to(LEAD)
                        setup()
                elif ph["kind"] == "ffn":
                    ffn(ph)
                elif ph["kind"] == "mix":
                    {"first": mix_first, "even": mix_even, "odd": mix_odd}[ph["which"]](ph)


_INS = ["x", "w_in", "q_norm_g", "k_norm_g", "dw_w", "w_out",
        "w_gate", "w_up", "w_down", "norm_g_2", "ffn_wg_2", "ffn_wu_2", "ffn_wd_2", "even_w_in_2", "even_w_out_2",
        "even_lambda_2", "even_subln_2", "odd_w_in_2", "odd_w_out_2", "odd_rel_bias_2"]


def plan(a):
    def mlp(l, i):
        return dict(kind="ffn", wg=a["ffn_wg_2"][l, i], wu=a["ffn_wu_2"][l, i], wd=a["ffn_wd_2"][l, i])

    def edge(take, g, row=None, scale=None):
        return dict(kind="edge", take=take, g=g, row=row, scale=scale)

    def post(l, i, scale, g):
        return edge("post", g, a["norm_g_2"][l, i, :], scale)

    return [edge("input", 0), dict(kind="mix", which="first"),
            edge("add", 1), dict(kind="ffn", wg=a["w_gate"][0], wu=a["w_up"][0], wd=a["w_down"][0]),
            edge("add", 2), mlp(0, 0), post(0, 1, 0.5, 3), dict(kind="mix", which="even"),
            post(0, 3, 1.0, 4), mlp(0, 1), post(0, 5, 0.5, 5), mlp(1, 0),
            post(1, 1, 0.5, 6), dict(kind="mix", which="odd"), post(1, 3, 1.0, 7), mlp(1, 1), post(1, 5, 0.5, None)]


def kernel(**inputs):
    import concourse.bacc as _bacc
    from concourse.bass_utils import run_bass_kernel_spmd as _run

    nc = _bacc.Bacc("TRN2", target_bir_lowering=False, num_devices=1)
    arrays, a = {}, {}
    given = {name: np.ascontiguousarray(inputs[name]) for name in _INS}
    given.update(host_tables())
    vectors = [inputs["norm1_g"][0], inputs["norm2_g"][0]] + [inputs["norm_g_2"][l, i] for l in range(2) for i in (0, 2, 4)]
    vectors += [inputs[name][0] for name in ("glu_b", "dw_b", "conv_ln_g", "conv_ln_b")]
    given["param_rows"] = np.concatenate([np.asarray(v).reshape(-1, P) for v in vectors])
    for name, v in given.items():
        arrays[f"in_{name}"] = v
        a[name] = nc.dram_tensor(f"in_{name}", v.shape, mybir.dt.from_np(v.dtype), kind="ExternalInput").ap()
    out = nc.dram_tensor("out_x", (1, S, D), F32, kind="ExternalOutput").ap()

    build(nc, a, out, plan(a))
    r = _run(nc, [arrays], core_ids=[0])
    return r.results[0]["out_x"]
```
